# Optimizing a Trainium2 kernel written in Bass

```python
import jax, jax.numpy as jnp
from jax import lax
import numpy as np

D_MODEL = 1024
BATCH = 1
SEQ = 512
DEPTH = 1

N_META = 16
D_MIX = D_MODEL
GLA_WIDTH = D_MIX // 2
GLA_HEADS = 4
GLA_DV = GLA_WIDTH // GLA_HEADS
GLA_DK = GLA_DV // 2
GLA_KEY_WIDTH = GLA_HEADS * GLA_DK
GLA_GATE_RANK = 16
GLA_TAU = 16.0
GLA_CHUNK = 64
SWA_WIDTH = D_MIX - GLA_WIDTH
SWA_HEAD_DIM = 64
SWA_Q_HEADS = SWA_WIDTH // SWA_HEAD_DIM
SWA_KV_HEADS = 2
SWA_GROUP = SWA_Q_HEADS // SWA_KV_HEADS
SWA_KV_WIDTH = SWA_KV_HEADS * SWA_HEAD_DIM
WINDOW = 128
SWA_BLOCK = 128
ROPE_THETA = 10000.0
D_FF = 256 * ((8 * D_MODEL // 3 + 255) // 256)
NORM_EPS = 1e-6
NEG_INF = -1e30

IN_SPLITS = (GLA_KEY_WIDTH, GLA_KEY_WIDTH, GLA_WIDTH, GLA_WIDTH, GLA_GATE_RANK,
             SWA_WIDTH, SWA_KV_WIDTH, SWA_KV_WIDTH)
D_IN = sum(IN_SPLITS)

kernel_name = "hybrid_gla_swa_macaron_layer"

def rms_norm(x, w):
    xf = x.astype(jnp.float32)
    y = xf * lax.rsqrt(jnp.mean(xf * xf, axis=-1, keepdims=True) + NORM_EPS)
    return (y * w.astype(jnp.float32)).astype(x.dtype)

def swiglu(x, w_gate, w_up, w_down):
    return (jax.nn.silu(x @ w_gate) * (x @ w_up)) @ w_down

def rope(x, pos):
    hd = x.shape[-1]
    inv_freq = 1.0 / (ROPE_THETA ** (jnp.arange(0, hd, 2, dtype=jnp.float32) / hd))
    ang = pos.astype(jnp.float32)[:, None] * inv_freq[None, :]
    ang = jnp.concatenate([ang, ang], axis=-1)[:, None, :]
    xf = x.astype(jnp.float32)
    x1, x2 = jnp.split(xf, 2, axis=-1)
    rot = jnp.concatenate([-x2, x1], axis=-1)
    return (xf * jnp.cos(ang) + rot * jnp.sin(ang)).astype(x.dtype)

def gla_chunked(q, k, v, log_a):
    B, L, H, dk = q.shape
    dv = v.shape[-1]
    C = GLA_CHUNK
    pad = (-L) % C
    n = (L + pad) // C

    def to_chunks(t):
        t = jnp.pad(t, ((0, 0), (pad, 0), (0, 0), (0, 0)))
        return t.reshape(B, n, C, H, t.shape[-1]).transpose(1, 0, 3, 2, 4).astype(jnp.float32)

    qc = to_chunks(q) * (dk ** -0.5)
    kc = to_chunks(k)
    vc = to_chunks(v)
    bc = jnp.cumsum(to_chunks(log_a), axis=3)
    causal = jnp.tril(jnp.ones((C, C), dtype=bool))[None, None, :, :, None]

    def step(S, inp):
        qi, ki, vi, bi = inp
        diff = bi[:, :, :, None, :] - bi[:, :, None, :, :]
        decay = jnp.exp(jnp.where(causal, diff, -jnp.inf))
        attn = jnp.einsum('bhid,bhjd,bhijd->bhij', qi, ki, decay)
        o = jnp.einsum('bhij,bhjv->bhiv', attn, vi) + \
            jnp.einsum('bhid,bhdv->bhiv', qi * jnp.exp(bi), S)
        b_last = bi[:, :, -1:, :]
        S = jnp.exp(b_last[:, :, 0, :])[..., None] * S + \
            jnp.einsum('bhjd,bhjv->bhdv', ki * jnp.exp(b_last - bi), vi)
        return S, o

    S0 = jnp.zeros((B, H, dk, dv), jnp.float32)
    _, o = lax.scan(step, S0, (qc, kc, vc, bc))
    o = o.transpose(1, 0, 3, 2, 4).reshape(B, n * C, H, dv)[:, pad:]
    return o.astype(v.dtype)

def swa_with_sinks(q, k, v, sinks):
    B, L, HQ, hd = q.shape
    T = SWA_BLOCK
    KV, G = SWA_KV_HEADS, SWA_GROUP
    pad = (-L) % T
    Lp = L + pad
    nb = Lp // T
    qb = jnp.pad(q, ((0, 0), (pad, 0), (0, 0), (0, 0))).reshape(B, nb, T, KV, G, hd)
    kp = jnp.pad(k, ((0, 0), (pad + T, 0), (0, 0), (0, 0))).reshape(B, nb + 1, T, KV, hd)
    vp = jnp.pad(v, ((0, 0), (pad + T, 0), (0, 0), (0, 0))).reshape(B, nb + 1, T, KV, hd)
    k_band = jnp.concatenate([kp[:, :-1], kp[:, 1:]], axis=2)
    v_band = jnp.concatenate([vp[:, :-1], vp[:, 1:]], axis=2)
    k_meta = k[:, :N_META]
    v_meta = v[:, :N_META]

    qpos = (jnp.arange(Lp) - pad).reshape(nb, T)
    kpos_all = (jnp.arange(Lp + T) - pad - T).reshape(nb + 1, T)
    kpos = jnp.concatenate([kpos_all[:-1], kpos_all[1:]], axis=1)
    dq = qpos[:, :, None]
    dk_ = kpos[:, None, :]
    band_mask = (dk_ >= N_META) & (dk_ <= dq) & (dq - dk_ < WINDOW)
    meta_mask = jnp.arange(N_META)[None, None, :] <= dq
    mask = jnp.concatenate([band_mask, meta_mask], axis=-1)

    scale = hd ** -0.5
    s_band = jnp.einsum('bntkgd,bnskd->bnkgts', qb, k_band).astype(jnp.float32)
    s_meta = jnp.einsum('bntkgd,bmkd->bnkgtm', qb, k_meta).astype(jnp.float32)
    s = jnp.concatenate([s_band, s_meta], axis=-1) * scale
    s = jnp.where(mask[None, :, None, None], s, NEG_INF)
    sink = sinks.astype(jnp.float32).reshape(KV, G)[None, None, :, :, None, None]
    m = jnp.maximum(jnp.max(s, axis=-1, keepdims=True), sink)
    p = jnp.exp(s - m)
    p = p / (jnp.sum(p, axis=-1, keepdims=True) + jnp.exp(sink - m))
    p = p.astype(v.dtype)
    o = jnp.einsum('bnkgts,bnskd->bntkgd', p[..., :2 * T], v_band) + \
        jnp.einsum('bnkgtm,bmkd->bntkgd', p[..., 2 * T:], v_meta)
    return o.reshape(B, Lp, HQ, hd)[:, pad:]

def hybrid_mixer(h, w_in, gla_w_a2, gla_b_a, gla_out_norm, swa_sinks, swa_out_norm, w_out):
    B, L, _ = h.shape
    pos = jnp.arange(L, dtype=jnp.int32)
    proj = h @ w_in
    offsets = [int(o) for o in np.cumsum(IN_SPLITS)[:-1]]
    gq, gk, gv, gg, ga, sq, sk, sv = jnp.split(proj, offsets, axis=-1)

    log_a = jax.nn.log_sigmoid((ga @ gla_w_a2 + gla_b_a).astype(jnp.float32)) / GLA_TAU
    o_gla = gla_chunked(gq.reshape(B, L, GLA_HEADS, GLA_DK),
                        gk.reshape(B, L, GLA_HEADS, GLA_DK),
                        gv.reshape(B, L, GLA_HEADS, GLA_DV),
                        log_a.reshape(B, L, GLA_HEADS, GLA_DK))
    o_gla = rms_norm(o_gla, gla_out_norm) * jax.nn.silu(gg.reshape(B, L, GLA_HEADS, GLA_DV))
    o_gla = o_gla.reshape(B, L, GLA_WIDTH)

    q = rope(sq.reshape(B, L, SWA_Q_HEADS, SWA_HEAD_DIM), pos)
    k = rope(sk.reshape(B, L, SWA_KV_HEADS, SWA_HEAD_DIM), pos)
    v = sv.reshape(B, L, SWA_KV_HEADS, SWA_HEAD_DIM)
    o_swa = swa_with_sinks(q, k, v, swa_sinks).reshape(B, L, SWA_WIDTH)
    o_swa = rms_norm(o_swa, swa_out_norm)

    return jnp.concatenate([o_gla, o_swa], axis=-1) @ w_out

def setup_inputs(seed: int = 0) -> dict:
    key = jax.random.key(seed)
    ks = jax.random.split(key, 24)
    f32 = jnp.float32
    nrm = lambda k, shape, s: jax.random.normal(k, shape, f32) * s
    gain = lambda k, shape: 1.0 + 0.05 * jax.random.normal(k, shape, f32)
    Dp = DEPTH
    return {
        "x": jax.random.normal(ks[0], (BATCH, SEQ, D_MODEL), f32),
        "meta_tokens": nrm(ks[1], (N_META, D_MODEL), 1.0),
        "ffn1_pre_norm": gain(ks[2], (Dp, D_MODEL)),
        "ffn1_w_gate": nrm(ks[3], (Dp, D_MODEL, D_FF), D_MODEL ** -0.5),
        "ffn1_w_up": nrm(ks[4], (Dp, D_MODEL, D_FF), D_MODEL ** -0.5),
        "ffn1_w_down": nrm(ks[5], (Dp, D_FF, D_MODEL), D_FF ** -0.5),
        "ffn1_post_norm": gain(ks[6], (Dp, D_MODEL)),
        "mix_pre_norm": gain(ks[7], (Dp, D_MODEL)),
        "w_in": nrm(ks[8], (Dp, D_MODEL, D_IN), D_MODEL ** -0.5),
        "gla_w_a2": nrm(ks[9], (Dp, GLA_GATE_RANK, GLA_KEY_WIDTH), GLA_GATE_RANK ** -0.5),
        "gla_b_a": nrm(ks[10], (Dp, GLA_KEY_WIDTH), 0.1),
        "gla_out_norm": gain(ks[11], (Dp, GLA_DV)),
        "swa_sinks": nrm(ks[12], (Dp, SWA_Q_HEADS), 0.5),
        "swa_out_norm": gain(ks[13], (Dp, SWA_WIDTH)),
        "w_out": nrm(ks[14], (Dp, D_MIX, D_MODEL), D_MIX ** -0.5),
        "mix_post_norm": gain(ks[15], (Dp, D_MODEL)),
        "ffn2_pre_norm": gain(ks[16], (Dp, D_MODEL)),
        "ffn2_w_gate": nrm(ks[17], (Dp, D_MODEL, D_FF), D_MODEL ** -0.5),
        "ffn2_w_up": nrm(ks[18], (Dp, D_MODEL, D_FF), D_MODEL ** -0.5),
        "ffn2_w_down": nrm(ks[19], (Dp, D_FF, D_MODEL), D_FF ** -0.5),
        "ffn2_post_norm": gain(ks[20], (Dp, D_MODEL)),
    }

def reference(x, meta_tokens, ffn1_pre_norm, ffn1_w_gate, ffn1_w_up, ffn1_w_down, ffn1_post_norm,
              mix_pre_norm, w_in, gla_w_a2, gla_b_a, gla_out_norm, swa_sinks, swa_out_norm, w_out,
              mix_post_norm, ffn2_pre_norm, ffn2_w_gate, ffn2_w_up, ffn2_w_down, ffn2_post_norm):
    B = x.shape[0]
    meta = jnp.broadcast_to(meta_tokens.astype(x.dtype)[None], (B, N_META, x.shape[-1]))
    h = jnp.concatenate([meta, x], axis=1)
    for l in range(DEPTH):
        f = swiglu(rms_norm(h, ffn1_pre_norm[l]), ffn1_w_gate[l], ffn1_w_up[l], ffn1_w_down[l])
        h = h + 0.5 * rms_norm(f, ffn1_post_norm[l])
        m = hybrid_mixer(rms_norm(h, mix_pre_norm[l]), w_in[l], gla_w_a2[l], gla_b_a[l],
                         gla_out_norm[l], swa_sinks[l], swa_out_norm[l], w_out[l])
        h = h + rms_norm(m, mix_post_norm[l])
        f = swiglu(rms_norm(h, ffn2_pre_norm[l]), ffn2_w_gate[l], ffn2_w_up[l], ffn2_w_down[l])
        h = h + 0.5 * rms_norm(f, ffn2_post_norm[l])
    return h[:, N_META:]


_drawn_inputs = setup_inputs


def setup_inputs(seed=0):
    import zlib

    import numpy as np

    out = dict(_drawn_inputs(seed))
    spreads = {}
    factors = {'gla_b_a': 3.452,
     'gla_out_norm': 2.949,
     'swa_sinks': 8.0,
     'ffn2_post_norm': 3.731,
     'swa_out_norm': 2.675}
    for name, (base, spread) in spreads.items():
        noise = np.random.default_rng([zlib.crc32(name.encode()), seed]).standard_normal(out[name].shape)
        drawn = base * np.exp(spread * noise) if base else spread * noise
        out[name] = __import__('jax').numpy.asarray(drawn.astype(out[name].dtype))
    for name, factor in factors.items():
        out[name] = (out[name] * factor).astype(out[name].dtype)
    return out
```

```python
from contextlib import ExitStack

import numpy as np
import concourse.bass as bass
from concourse import mybir

F32 = mybir.dt.float32
F32R = mybir.dt.float32r
U32 = mybir.dt.uint32
ALU = mybir.AluOpType
ACT = mybir.ActivationFunctionType
AX_X = mybir.AxisListType.X

P = 128
D_MODEL = 1024
SEQ = 512
N_META = 16
L = SEQ + N_META
D_FF = 2816
EPS = 1e-6
KD = D_MODEL // P
KF = D_FF // P
KH = KF // 2

GLA_HEADS, GLA_DK, GLA_DV, GATE_RANK = 4, 64, 128, 16
GLA_TAU = 16.0
SWA_HEADS, KV_HEADS, HEAD_DIM = 8, 2, 64
GROUP = SWA_HEADS // KV_HEADS
ROPE_THETA = 10000.0
NEG = -1e30
C = 128
NC = SEQ // C
SPAN = N_META + 2 * C
LEVELS = [64, 32, 16, 8, 4, 2, 1]

T_GA, T_GK, T_GQ, T_SK, T_SV, T_GV, T_SQ, T_GG = 0, 1, 3, 5, 6, 7, 11, 15
N_IN = 19

UP_UNITS, DOWN_UNITS = 2 * KF, 2 * KD
U_UP1 = 0
U_DOWN1 = U_UP1 + UP_UNITS
U_IN = U_DOWN1 + DOWN_UNITS
U_OUT = U_IN + N_IN
U_UP2 = U_OUT + KD
U_DOWN2 = U_UP2 + UP_UNITS
N_UNITS = U_DOWN2 + DOWN_UNITS
RAW, OPS = 4, 2
W_UP, W_DOWN = KD * P, KH * P

V_PRE1, V_POST1, V_PREM, V_POSTM, V_PRE2, V_POST2 = (KD * n for n in range(6))
V_SWA = 6 * KD
V_GLA = V_SWA + 4
V_BA = V_GLA + 1
V_SINK = V_BA + 2
V_EPS = V_SINK + SWA_HEADS
N_VEC = V_EPS + 2

N_PRE1, N_POST1, N_PREM, N_GLA, N_SWA, N_POSTM, N_PRE2, N_POST2 = range(8)
WIDE = {N_PRE1: 0, N_POST1: 1, N_PREM: 2, N_POSTM: 3, N_PRE2: 4, N_POST2: 5}


def hybrid_layer(nc, x_t, vecs, up1, down1, w_in, w_a2, w_out, up2, down2, cos_t, sin_t, perm, ident, band,
                 level_mask, out):
    ctx = ExitStack()
    with ctx:
        def sb(name, shape, dt, stack=ctx):
            return stack.enter_context(nc.sbuf_tensor(name, shape, dt))

        def sem(name):
            return ctx.enter_context(nc.semaphore(name))

        h = sb("h", [P, KD, L], F32)
        raw = sb("raw", [P, RAW, W_DOWN], F32)
        w_hi = sb("w_hi", [P, OPS, W_DOWN], F32R)
        w_lo = sb("w_lo", [P, OPS, W_DOWN], F32R)
        vec = sb("vec", [P, N_VEC], F32)
        ones = sb("ones", [P, P], F32)
        sumsq = sb("sumsq", [P, L], F32)
        rnorm = sb("rnorm", [P, L], F32)
        gate = sb("gate", [P, L], F32)
        up = sb("up", [P, L], F32)
        sq = sb("sq", [P, 2, L], F32)
        rms = sb("rms", [P, L], F32)
        with ExitStack() as s:
            xa_hi, xa_lo = sb("xa_hi", [P, KD, L], F32R, s), sb("xa_lo", [P, KD, L], F32R, s)
            hid1_hi, hid1_lo = sb("hid1_hi", [P, KF, L], F32R, s), sb("hid1_lo", [P, KF, L], F32R, s)
        with ExitStack() as s:
            y1 = sb("y1", [P, KD, L], F32, s)
            sb("y1_rest", [P, KD, L], F32, s)
            xb_hi, xb_lo = sb("xb_hi", [P, KD, L], F32R, s), sb("xb_lo", [P, KD, L], F32R, s)
        with ExitStack() as s:
            proj = sb("proj", [P, 16, L], F32, s)
            with ExitStack() as x:
                decay = sb("decay", [P, 2, SEQ], F32, x)
                lv_k = sb("lv_k", [P, 2, 2, SEQ], F32, x)
                lv_q = sb("lv_q", [P, 2, 2, SEQ], F32, x)
                zs = sb("zs", [P, 2 * GROUP * SPAN], F32, x)
            with ExitStack() as x:
                cat_hi, cat_lo = sb("cat_hi", [P, KD, SEQ], F32R, x), sb("cat_lo", [P, KD, SEQ], F32R, x)
            sb("mix_operand", [P, 2 * KD, L], F32, s)
            kv3 = sb("kv3", [P, 3, L], F32, s)
            vtok = sb("vtok", [P, NC + 1, 5 * P], F32, s)
            b_real = sb("b_real", [P, 2, SEQ], F32, s)
            b_meta = sb("b_meta", [P, 2, N_META], F32, s)
            q_in = sb("q_in", [P, 2, SEQ], F32, s)
            k_out = sb("k_out", [P, 2, L], F32, s)
            ktok = sb("ktok", [P, NC, 2 * P], F32, s)
            state = sb("state", [P, 2, NC, GLA_DV], F32, s)
            dec = sb("dec", [P, 2, NC], F32, s)
            cos_s, sin_s = sb("cos_s", [P, L], F32, s), sb("sin_s", [P, L], F32, s)
            perm_s, ident_s = sb("perm_s", [P, P], F32, s), sb("ident_s", [P, P], F32, s)
            wa2_s = sb("wa2_s", [GATE_RANK, 2 * P], F32, s)
            band_s = sb("band_s", [P, 2, SPAN], F32, s)
            lmask = sb("lmask", [P, len(LEVELS) + 1, C], U32, s)
            kx = sb("kx", [P, NC, SPAN], F32, s)
            p_t = sb("p_t", [P, 2, GROUP * C], F32, s)
            p_tm = sb("p_tm", [N_META, GROUP * C], F32, s)
            small = sb("small", [P, 8, GROUP], F32, s)
        with ExitStack() as s:
            hid2_hi, hid2_lo = sb("hid2_hi", [P, KF, SEQ], F32R, s), sb("hid2_lo", [P, KF, SEQ], F32R, s)
            xc_hi, xc_lo = sb("xc_hi", [P, KD, SEQ], F32R, s), sb("xc_lo", [P, KD, SEQ], F32R, s)
        with ExitStack() as s:
            y2 = sb("y2", [P, KD, SEQ], F32, s)
        with ExitStack() as s:
            sb("hid2_space", [P, 2 * KF, SEQ], F32, s)
            y3 = sb("y3", [P, KD, SEQ], F32, s)

        ps = ctx.enter_context(nc.psum_tensor("ps", [P, 8, 512], F32))

        raw_landed = [sem(f"raw_landed{i}") for i in range(RAW)]
        hi_split, lo_split = sem("hi_split"), sem("lo_split")
        unit_used = sem("unit_used")
        x_landed = [sem(f"x_landed{k}") for k in range(KD)]
        vec_landed, ones_set = sem("vec_landed"), sem("ones_set")
        table_landed = sem("table_landed")
        squared, summed = sem("squared"), sem("summed")
        norm_summed, rms_ready, norm_ready = sem("norm_summed"), sem("rms_ready"), sem("norm_ready")
        h_updated, x_hi, x_ready = sem("h_updated"), sem("x_hi"), sem("x_ready")
        gate_scaled, gu_evicted = sem("gate_scaled"), sem("gu_evicted")
        silu_done, hid_written, hid_hi, hid_ready = sem("silu_done"), sem("hid_written"), sem("hid_hi"), sem("hid_ready")
        y_evicted = sem("y_evicted")
        proj_evicted = sem("proj_evicted")
        z_done, z_log, z_read = sem("z_done"), sem("z_log"), sem("z_read")
        b_ready, k_diff, k_exp, q_exp = sem("b_ready"), sem("k_diff"), sem("k_exp"), sem("q_exp")
        k_out_ready, q_in_ready = sem("k_out_ready"), sem("q_in_ready")
        rot_done, rot_read, rope_done = sem("rot_done"), sem("rot_read"), sem("rope_done")
        kx_ready = sem("kx_ready")
        v_turned, v_evicted, k_turned, k_evicted = sem("v_turned"), sem("v_evicted"), sem("k_turned"), sem("k_evicted")
        sums_done, states_ready = sem("sums_done"), sem("states_ready")
        at_zeroed, lv_zeroed = sem("at_zeroed"), sem("lv_zeroed")
        lv_diff, lv_exp, lv_ready = sem("lv_diff"), sem("lv_exp"), sem("lv_ready")
        lv_scored, lv_taken = sem("lv_scored"), sem("lv_taken")
        og_done, og_evicted, og_squared = sem("og_done"), sem("og_evicted"), sem("og_squared")
        gg_silu = sem("gg_silu")
        s_done, s_masked, s_max, s_exp, s_normed = sem("s_done"), sem("s_masked"), sem("s_max"), sem("s_exp"), sem("s_normed")
        p_turned, p_act, p_dve = sem("p_turned"), sem("p_act"), sem("p_dve")
        pv_done, pv_evicted, os_squared = sem("pv_done"), sem("pv_evicted"), sem("os_squared")
        mixed, cat_hi_done, cat_ready = sem("mixed"), sem("cat_hi_done"), sem("cat_ready")
        dve_step, act_step = sem("dve_step"), sem("act_step")
        out_ready, stored = sem("out_ready"), sem("stored")

        def f32(ap):
            return ap.bitcast(F32)

        def unit(base, j, i=0):
            return base + j + RAW * i, (base + j) % RAW, (base + j) // RAW + i, (base + j) % OPS

        def in_psum(bank, n_tok):
            return ps[:, bank:bank + 2, 0:L // 2] if n_tok == L else ps[:, bank, 0:SEQ]

        def row(ap, n_tok):
            return ap.rearrange("p (b n) -> p b n", b=2) if n_tok == L else ap[:, 0:SEQ]

        def tokens(n_tok):
            return slice(L - n_tok, L)

        def in_bank(j):
            return 2 * (j % 4) if j < 4 else 2 * (j % 2)

        in_dst = [kv3[:, 0, :], proj[:, 0, :], proj[:, 1, :], proj[:, 2, :], proj[:, 3, :], kv3[:, 1, :], kv3[:, 2, :]]
        in_dst += [proj[:, 4 + n, :] for n in range(12)]
        gk = proj[:, 0:2, :]
        gq = proj[:, 2:4, N_META:L]
        gv = proj[:, 4:8, :]
        sq_heads = proj[:, 8:12, N_META:L]
        gg = proj[:, 12:16, N_META:L]
        ga, sk, sv = kv3[0:GATE_RANK, 0, :], kv3[:, 1, :], kv3[:, 2, :]
        attn = proj[:, 4:8, 0:SEQ]
        o_gla = proj[:, 0:4, 0:SEQ]
        o_swa = sq_heads
        z_log_t = zs[:, 0:2 * L].rearrange("p (t n) -> p t n", t=2)
        z_min = zs[:, 2 * L:4 * L].rearrange("p (t n) -> p t n", t=2)
        scores = zs[:, :].rearrange("p (b h n) -> p b h n", b=2, h=GROUP)
        gla_sq = lv_q[:, :, :, :].rearrange("p a t n -> p (a t) n")
        gla_rms = lv_k[:, :, :, :].rearrange("p a t n -> p (a t) n")
        swa_sq = gla_sq

        block = ctx.enter_context(nc.Block())

        @block.sync
        def _(sp):
            def load(src, base, j, width, i=0):
                u, slot, turn, _ = unit(base, j, i)
                if base + j >= RAW:
                    sp.wait_ge(lo_split, u - RAW + 1)
                sp.dma_start(raw[:, slot, 0:width], src[j + RAW * i]).then_inc(raw_landed[slot], 16)

            def stream(src, base, count, width, first=0):
                rounds = (count - first) // RAW
                with sp.Fori(0, rounds) as i:
                    for j in range(RAW):
                        load(src, base, first + j, width, i)
                for j in range(first + RAW * rounds, count):
                    load(src, base, j, width)

            sp.dma_start(vec[:, :], vecs).then_inc(vec_landed, 16)
            for k in range(KD):
                sp.dma_start(h[:, k, :], x_t[:, k, :]).then_inc(x_landed[k], 16)
                if k % 2 == 1:
                    load(up1, U_UP1, k // 2, W_UP)
            stream(up1, U_UP1, UP_UNITS, W_UP, first=RAW)
            stream(down1, U_DOWN1, DOWN_UNITS, W_DOWN)
            stream(w_in, U_IN, 4, W_UP)
            sp.wait_ge(unit_used, U_IN)
            for dst, src in ((cos_s[:, :], cos_t), (sin_s[:, :], sin_t), (perm_s[:, :], perm), (ident_s[:, :], ident),
                             (wa2_s[:, :], w_a2), (band_s[:, :, :], band), (lmask[:, :, :], level_mask)):
                sp.dma_start(dst, src).then_inc(table_landed, 16)
            stream(w_in, U_IN, N_IN, W_UP, first=4)
            stream(w_out, U_OUT, KD, W_UP)
            stream(up2, U_UP2, UP_UNITS, W_UP)
            stream(down2, U_DOWN2, DOWN_UNITS, W_DOWN)
            for k in range(KD):
                sp.wait_ge(out_ready, k + 1)
                sp.dma_start(out[:, k, :], h[:, k, N_META:L]).then_inc(stored, 16)
            sp.wait_ge(stored, 16 * KD)

        @block.tensor
        def _(pe):
            def products(base, j, i, xh, xl, k0, nk, bank, n_tok, first=True, last=True):
                u, _, _, slot = unit(base, j, i)
                pe.wait_ge(lo_split, u + 1)
                width = L // 2 if n_tok == L else SEQ
                for k in range(nk):
                    wh, wl = w_hi[:, slot, k * P:(k + 1) * P], w_lo[:, slot, k * P:(k + 1) * P]
                    for n in range(n_tok // width):
                        dst, cols = ps[:, bank + n, 0:width], slice(n * width, (n + 1) * width)
                        pe.matmul(dst, wh, xh[:, k0 + k, cols], start=first and k == 0, stop=False)
                        pe.matmul(dst, wh, xl[:, k0 + k, cols], start=False, stop=False)
                        mm = pe.matmul(dst, wl, xh[:, k0 + k, cols], start=False, stop=last and k == nk - 1)
                return mm

            def column_sums(src, n_tok, bank, norm=None, start=True, stop=True):
                width = L // 2 if n_tok == L else SEQ
                for n in range(n_tok // width):
                    mm = pe.matmul(ps[:, bank + n, 0:width], ones[:, :], src[:, n * width:(n + 1) * width],
                                   start=start, stop=stop)
                if norm is not None:
                    mm.then_inc(norm_summed, 1)

            def ffn_up(base, tile0, xh, xl, n_tok, norm, x_count):
                def tile(t, j, q, i=0, before_up=None):
                    if not (isinstance(t, int) and tile0 + t < 2):
                        pe.wait_ge(gu_evicted, tile0 + t - 1)
                    products(base, j, i, xh, xl, 0, KD, 4 * q, n_tok).then_inc(unit_used, 1)
                    if before_up:
                        pe.wait_ge(rms_ready, norm + 1)
                    products(base, j + 1, i, xh, xl, 0, KD, 4 * q + 2, n_tok).then_inc(unit_used, 1)

                pe.wait_ge(x_ready, x_count)
                tile(0, 0, 0)
                pe.wait_ge(summed, (KD - 1) * (WIDE[norm] + 1))
                column_sums(sumsq, n_tok, 6, norm)
                tile(1, 2, 1, before_up=True)
                with pe.Fori(1, KF // 2) as i:
                    tile(2 * i, 0, 0, i)
                    tile(2 * i + 1, 2, 1, i)

            def ffn_down(base, tile0, hid0, hi, lo, n_tok):
                def tile(d, j, q, i=0):
                    if not (isinstance(d, int) and tile0 + d < 2):
                        pe.wait_ge(y_evicted, tile0 + d - 1)
                    products(base, j, i, hi, lo, 0, KH, 2 * q, n_tok, last=False).then_inc(unit_used, 1)
                    products(base, j + 1, i, hi, lo, KH, KH, 2 * q, n_tok, first=False).then_inc(unit_used, 1)

                pe.wait_ge(hid_ready, hid0 + KF)
                tile(0, 0, 0)
                tile(1, 2, 1)
                with pe.Fori(1, KD // 2) as i:
                    tile(2 * i, 0, 0, i)
                    tile(2 * i + 1, 2, 1, i)

            def wide_sum(norm, n_tok, bank):
                pe.wait_ge(summed, (KD - 1) * (WIDE[norm] + 1))
                column_sums(sumsq, n_tok, bank, norm)

            pe.wait_ge(ones_set, 1)
            ffn_up(U_UP1, 0, xa_hi, xa_lo, L, N_PRE1, KD)
            ffn_down(U_DOWN1, 0, 0, hid1_hi, hid1_lo, L)
            wide_sum(N_POST1, L, 4)

            def in_tile(t, j, q, i=0):
                products(U_IN, j, i, xb_hi, xb_lo, 0, KD, q, L).then_inc(unit_used, 1)

            pe.wait_ge(x_ready, 2 * KD)
            for t in range(4):
                if t == 3:
                    pe.wait_ge(rms_ready, N_PREM + 1)
                in_tile(t, t, in_bank(t))
                if t == 1:
                    wide_sum(N_PREM, L, 6)
            with pe.Fori(2, N_IN // 2) as i:
                for n in range(2):
                    t = 2 * i + n
                    pe.wait_ge(proj_evicted, t - 1)
                    pe.wait_ge(lo_split, U_IN + t + 1)
                    slot = (U_IN + n) % OPS
                    for k in range(KD):
                        wh, wl = w_hi[:, slot, k * P:(k + 1) * P], w_lo[:, slot, k * P:(k + 1) * P]
                        for b in range(2):
                            dst, cols = ps[:, 2 * n + b, 0:L // 2], slice(b * L // 2, (b + 1) * L // 2)
                            pe.matmul(dst, wh, xb_hi[:, k, cols], start=k == 0, stop=False)
                            pe.matmul(dst, wh, xb_lo[:, k, cols], start=False, stop=False)
                            mm = pe.matmul(dst, wl, xb_hi[:, k, cols], start=False, stop=k == KD - 1)
                    mm.then_inc(unit_used, 1)
            pe.wait_ge(proj_evicted, N_IN - 2)
            in_tile(N_IN - 1, N_IN - 1, in_bank(N_IN - 1))

            pe.wait_ge(table_landed, 16 * 7)
            for t in range(2):
                for n in range(2):
                    mm = pe.matmul(ps[:, 4 + 2 * t + n, 0:L // 2], wa2_s[:, t * P:(t + 1) * P],
                                   ga[:, n * L // 2:(n + 1) * L // 2], start=True, stop=True)
            mm.then_inc(z_done, 1)

            pe.wait_ge(proj_evicted, N_IN)
            for n in range(2):
                mm = pe.matmul(ps[:, n, 0:L // 2], perm_s[:, :], sk[:, n * L // 2:(n + 1) * L // 2], start=True, stop=True)
            mm.then_inc(rot_done, 1)
            for n in range(4):
                if n >= 2:
                    pe.wait_ge(rot_read, n - 1)
                pe.matmul(ps[:, (2, 3, 0, 2)[n], :], perm_s[:, :], sq_heads[:, n, :], start=True, stop=True)\
                  .then_inc(rot_done, 1)

            pe.wait_ge(z_log, 2)
            pe.wait_ge(z_read, 2)
            for b in range(NC):
                for n in range(4):
                    pe.transpose(ps[:, 4 + b, n * P:(n + 1) * P], gv[:, n, N_META + b * C:N_META + (b + 1) * C], ident_s[:, :])
            for b in range(NC):
                mm = pe.transpose(ps[:, 1, b * P:(b + 1) * P], sv[:, N_META + b * C:N_META + (b + 1) * C], ident_s[:, :])
            mm.then_inc(v_turned, 1)
            pe.wait_ge(rot_read, 5)
            for n in range(4):
                pe.transpose(ps[0:N_META, 0, n * P:(n + 1) * P], gv[:, n, 0:N_META], ident_s[:, :])
            pe.transpose(ps[0:N_META, 3, 0:P], sv[:, 0:N_META], ident_s[:, :]).then_inc(v_turned, 1)

            pe.wait_ge(v_evicted, 2)
            pe.wait_ge(k_out_ready, 1)
            for c in range(NC - 1):
                for t in range(2):
                    pe.transpose(ps[:, 4 + c // 2, (c % 2) * 2 * P + t * P:(c % 2) * 2 * P + (t + 1) * P],
                                 k_out[:, t, N_META + c * C:N_META + (c + 1) * C], ident_s[:, :])
            for t in range(2):
                mm = pe.transpose(ps[0:N_META, 5, 2 * P + t * P:2 * P + (t + 1) * P], k_out[:, t, 0:N_META], ident_s[:, :])
            mm.then_inc(k_turned, 1)

            pe.wait_ge(k_evicted, 1)
            for t in range(2):
                for c in range(NC):
                    rows = N_META if c == 0 else C
                    for n in range(2):
                        head = 2 * t + n
                        mm = pe.matmul(ps[64 * n:64 * n + 64, 6 + t, c * P:(c + 1) * P],
                                       ktok[0:rows, c, head * 64:head * 64 + 64],
                                       vtok[0:rows, c, head * P:(head + 1) * P], start=True, stop=True)
            mm.then_inc(sums_done, 1)

            for lv in range(len(LEVELS) + 1):
                if lv < len(LEVELS):
                    pe.wait_ge(lv_ready, lv + 1)
                if lv:
                    pe.wait_ge(lv_taken, lv)
                for head in range(GLA_HEADS):
                    rows = slice(64 * (head % 2), 64 * (head % 2) + 64)
                    for c in range(NC):
                        cols = slice(c * C, (c + 1) * C)
                        if lv < len(LEVELS):
                            kl, ql = lv_k[rows, lv % 2, head // 2, cols], lv_q[rows, lv % 2, head // 2, cols]
                        else:
                            kl, ql = gk[rows, head // 2, N_META + c * C:N_META + (c + 1) * C], gq[rows, head // 2, cols]
                        mm = pe.matmul(ps[:, head, cols], kl, ql, start=True, stop=True)
                mm.then_inc(lv_scored, 1)

            pe.wait_ge(lv_taken, len(LEVELS) + 1)
            pe.wait_ge(states_ready, 1)
            pe.wait_ge(q_in_ready, 1)
            for head in range(GLA_HEADS):
                rows = slice(64 * (head % 2), 64 * (head % 2) + 64)
                for c in range(NC):
                    cols = slice(c * C, (c + 1) * C)
                    pe.matmul(ps[:, head, cols], vtok[:, c + 1, head * P:(head + 1) * P], attn[:, head, cols],
                              start=True, stop=False)
                    mm = pe.matmul(ps[:, head, cols], state[rows, head // 2, c, :], q_in[rows, head // 2, cols],
                                   start=False, stop=True)
            mm.then_inc(og_done, 1)
            pe.wait_ge(og_squared, 1)
            for head in range(GLA_HEADS):
                column_sums(gla_sq[:, head, :], SEQ, 4 + head, N_GLA if head == GLA_HEADS - 1 else None)

            def swa_scores(p):
                c, g = divmod(p, KV_HEADS)
                rows = slice(64 * g, 64 * g + 64)
                if p:
                    pe.wait_ge(s_masked, p)
                for n in range(GROUP):
                    mm = pe.matmul(ps[:, n, 0:SPAN], sq_heads[rows, n, c * C:(c + 1) * C], kx[rows, c, :],
                                   start=True, stop=True)
                mm.then_inc(s_done, 1)

            def swa_turn(p):
                c, g = divmod(p, KV_HEADS)
                pe.wait_ge(s_normed, p + 1)
                if p:
                    pe.wait_ge(p_act, p)
                    pe.wait_ge(p_dve, p)
                for n in range(GROUP):
                    src, cols = scores[:, p % 2, n, :], slice(n * C, (n + 1) * C)
                    if c:
                        pe.transpose(ps[:, 4, cols], src[:, N_META:N_META + C], ident_s[:, :])
                    pe.transpose(ps[0:N_META, 6, cols], src[:, 0:N_META], ident_s[:, :])
                    mm = pe.transpose(ps[:, 5, cols], src[:, N_META + C:SPAN], ident_s[:, :])
                mm.then_inc(p_turned, 1)

            def swa_values(p):
                c, g = divmod(p, KV_HEADS)
                pe.wait_ge(p_act, p + 1)
                pe.wait_ge(p_dve, p + 1)
                if p:
                    pe.wait_ge(pv_evicted, p)
                rows, v_cols = slice(64 * g, 64 * g + 64), slice(4 * P + 64 * g, 4 * P + 64 * g + 64)
                pe.matmul(ps[rows, 7, :], vtok[0:N_META, 0, v_cols], p_tm[:, :], start=True, stop=False)
                if c:
                    pe.matmul(ps[rows, 7, :], vtok[:, c, v_cols], p_t[:, 0, :], start=False, stop=False)
                pe.matmul(ps[rows, 7, :], vtok[:, c + 1, v_cols], p_t[:, 1, :], start=False, stop=True).then_inc(pv_done, 1)

            pe.wait_ge(kx_ready, 1 + 2 * NC)
            pe.wait_ge(rope_done, 5)
            pe.wait_ge(og_evicted, 1)
            swa_scores(0)
            pe.wait_ge(rms_ready, N_GLA + 1)
            for p in range(NC * KV_HEADS):
                if p + 1 < NC * KV_HEADS:
                    swa_scores(p + 1)
                swa_turn(p)
                swa_values(p)
            pe.wait_ge(os_squared, 1)
            for n in range(4):
                column_sums(swa_sq[:, n, :], SEQ, 0, N_SWA if n == 3 else None, start=n == 0, stop=n == 3)

            def out_tile(t, n):
                pe.wait_ge(y_evicted, KD + t - 1)
                pe.wait_ge(lo_split, U_OUT + t + 1)
                slot = (U_OUT + n) % OPS
                for k in range(KD):
                    wh, wl = w_hi[:, slot, k * P:(k + 1) * P], w_lo[:, slot, k * P:(k + 1) * P]
                    pe.matmul(ps[:, 2 * n, :], wh, cat_hi[:, k, :], start=k == 0, stop=False)
                    pe.matmul(ps[:, 2 * n, :], wh, cat_lo[:, k, :], start=False, stop=False)
                    mm = pe.matmul(ps[:, 2 * n, :], wl, cat_hi[:, k, :], start=False, stop=k == KD - 1)
                mm.then_inc(unit_used, 1)

            pe.wait_ge(cat_ready, KD)
            with pe.Fori(0, KD // 2) as i:
                out_tile(2 * i, 0)
                out_tile(2 * i + 1, 1)
            wide_sum(N_POSTM, SEQ, 4)
            ffn_up(U_UP2, KF, xc_hi, xc_lo, SEQ, N_PRE2, 3 * KD)
            ffn_down(U_DOWN2, 2 * KD, KF, hid2_hi, hid2_lo, SEQ)
            wide_sum(N_POST2, SEQ, 4)

        @block.scalar
        def _(act):
            def split_hi(base, j, width, i=0):
                u, raw_slot, turn, slot = unit(base, j, i)
                if base + j >= OPS:
                    act.wait_ge(unit_used, u - OPS + 1)
                act.wait_ge(raw_landed[raw_slot], 16 * (turn + 1))
                act.activation(w_hi[:, slot, 0:width], raw[:, raw_slot, 0:width], ACT.Copy).then_inc(hi_split, 1)

            def root(norm, n_tok, bank, n_feat, half=False):
                act.wait_ge(norm_summed, norm + 1)
                act.wait_ge(norm_ready, norm)
                f = 4.0 if half else 1.0
                act.activation(row(rms, n_tok), in_psum(bank, n_tok), ACT.Sqrt, bias=vec[:, V_EPS + half:V_EPS + half + 1],
                               scale=f / n_feat).then_inc(rms_ready, 1)

            def square(src, norm, k, n_tok, psum=False):
                if k == 0 and norm:
                    act.wait_ge(norm_summed, norm)
                if k >= 3:
                    act.wait_ge(summed, (KD - 1) * WIDE[norm] + k - 2)
                dst = sumsq if k == 0 else sq[:, k % 2, :]
                return act.activation(row(dst, n_tok) if psum else dst[:, 0:n_tok], src, ACT.Square)

            def operand(norm, n_tok, xh, v0, updates):
                for k in range(KD):
                    if updates is None:
                        act.wait_ge(x_landed[k], 16)
                    else:
                        act.wait_ge(h_updated, updates + k + 1)
                    src = h[:, k, tokens(n_tok)]
                    act.activation(xh[:, k, :], src, ACT.Copy, scale=vec[:, v0 + k:v0 + k + 1]).then_inc(x_hi, 1)
                    square(src, norm, k, n_tok).then_inc(squared, 1)

            def hidden_tile(tile0, t, hi, n_tok, i=0):
                act.wait_ge(gate_scaled, tile0 + t + 1)
                act.activation(gate[:, 0:n_tok], gate[:, 0:n_tok], ACT.Silu).then_inc(silu_done, 1)
                act.wait_ge(hid_written, tile0 + t + 1)
                act.activation(hi[:, t, :], up[:, 0:n_tok], ACT.Copy).then_inc(hid_hi, 1)

            def ffn_up(base, tile0, hi, n_tok, norm):
                split_hi(base, 2, W_UP)
                split_hi(base, 3, W_UP)
                root(norm, n_tok, 6, D_MODEL)
                hidden_tile(tile0, 0, hi, n_tok)
                split_hi(base, 4, W_UP)
                split_hi(base, 5, W_UP)
                hidden_tile(tile0, 1, hi, n_tok)
                with act.Fori(1, KF // 2 - 1) as i:
                    for n in range(2):
                        split_hi(base, 2 * n + 2, W_UP, i)
                        split_hi(base, 2 * n + 3, W_UP, i)
                        hidden_tile(tile0, 2 * i + n, hi, n_tok)
                split_hi(base, UP_UNITS - 2, W_UP)
                split_hi(base, UP_UNITS - 1, W_UP)
                hidden_tile(tile0, KF - 2, hi, n_tok)
                split_hi(base, UP_UNITS, W_DOWN)
                split_hi(base, UP_UNITS + 1, W_DOWN)
                hidden_tile(tile0, KF - 1, hi, n_tok)

            def result_tile(d, q, y, v0, norm, used, n_tok):
                act.wait_ge(unit_used, used)
                act.activation(row(y[:, d, :], n_tok), in_psum(2 * q, n_tok), ACT.Copy,
                               scale=vec[:, v0 + d:v0 + d + 1]).then_inc(act_step, 1)
                square(in_psum(2 * q, n_tok), norm, d, n_tok, psum=True).then_inc(y_evicted, 1)

            def ffn_down(base, y, v0, norm, n_tok, next_width):
                for d in range(KD):
                    for n in range(2):
                        if d < KD - 1:
                            split_hi(base, 2 * d + 2 + n, W_DOWN)
                        elif next_width:
                            split_hi(base, 2 * d + 2 + n, next_width)
                    result_tile(d, d % 2, y, v0, norm, base + 2 * d + 2, n_tok)

            act.wait_ge(vec_landed, 16)
            operand(N_PRE1, L, xa_hi, V_PRE1, None)
            split_hi(U_UP1, 0, W_UP)
            split_hi(U_UP1, 1, W_UP)
            ffn_up(U_UP1, 0, hid1_hi, L, N_PRE1)
            ffn_down(U_DOWN1, y1, V_POST1, N_POST1, L, W_UP)
            root(N_POST1, L, 4, D_MODEL, half=True)
            operand(N_PREM, L, xb_hi, V_PREM, 0)
            for j in range(N_IN):
                split_hi(U_IN, j + 2, W_UP)
                if j == 1:
                    root(N_PREM, L, 6, D_MODEL)

            act.wait_ge(z_done, 1)
            for t in range(2):
                act.activation(row(z_log_t[:, t, :], L), in_psum(4 + 2 * t, L), ACT.Abs,
                               bias=vec[:, V_BA + t:V_BA + t + 1]).then_inc(z_log, 1)
            act.wait_ge(z_log, 2)
            act.activation(z_log_t[:, :, :], z_log_t[:, :, :], ACT.Exp, scale=-1.0).then_inc(z_log, 1)
            act.wait_ge(z_log, 3)
            act.activation(z_log_t[:, :, :], z_log_t[:, :, :], ACT.Ln, bias=1.0).then_inc(z_log, 1)
            act.wait_ge(v_turned, 1)
            act.activation(vtok[:, 1:NC + 1, 0:4 * P], ps[:, 4:4 + NC, :], ACT.Copy).then_inc(act_step, 1)
            act.activation(vtok[:, 1:NC + 1, 4 * P:5 * P], ps[:, 1, :].rearrange("p (b n) -> p b n", b=NC),
                           ACT.Copy).then_inc(v_evicted, 1)
            act.wait_ge(v_turned, 2)
            act.activation(vtok[0:N_META, 0, 0:4 * P], ps[0:N_META, 0, :], ACT.Copy).then_inc(act_step, 1)
            act.activation(vtok[0:N_META, 0, 4 * P:5 * P], ps[0:N_META, 3, 0:P], ACT.Copy).then_inc(v_evicted, 1)
            act.wait_ge(b_ready, 1)
            act.activation(q_in[:, :, :], b_real[:, :, :], ACT.Exp, scale=1 / GLA_TAU).then_inc(q_exp, 1)
            act.activation(dec[:, :, :], b_real[:, :, C - 1:SEQ:C], ACT.Exp, scale=1 / GLA_TAU).then_inc(q_exp, 1)
            act.wait_ge(k_diff, 1)
            act.activation(k_out[:, :, :], k_out[:, :, :], ACT.Exp, scale=1 / GLA_TAU).then_inc(k_exp, 1)
            act.wait_ge(k_turned, 1)
            act.activation(ktok[:, 1:NC, :], ps[:, 4:6, :].rearrange("p b (c n) -> p (b c) n", c=2)[:, 0:NC - 1, :],
                           ACT.Copy).then_inc(act_step, 1)
            act.activation(ktok[0:N_META, 0, :], ps[0:N_META, 5, 2 * P:4 * P], ACT.Copy).then_inc(k_evicted, 1)
            for lv, m in enumerate(LEVELS):
                act.wait_ge(lv_diff, lv + 1)
                d = decay[:, :, :].rearrange("p t (n x) -> p (t n) x", x=2 * m)
                act.activation(d[:, :, 0:m], d[:, :, 0:m], ACT.Exp, scale=-1 / GLA_TAU).then_inc(act_step, 1)
                act.activation(d[:, :, m:2 * m], d[:, :, m:2 * m], ACT.Exp, scale=1 / GLA_TAU).then_inc(lv_exp, 1)
            act.wait_ge(og_done, 1)
            act.activation(gla_sq, ps[:, 0:4, :], ACT.Square).then_inc(og_squared, 1)
            act.activation(o_gla, ps[:, 0:4, :], ACT.Copy).then_inc(og_evicted, 1)
            act.wait_ge(norm_summed, N_GLA + 1)
            act.activation(gla_rms, ps[:, 4:8, :], ACT.Sqrt, bias=vec[:, V_EPS:V_EPS + 1],
                           scale=1 / GLA_DV).then_inc(rms_ready, 1)
            act.activation(gg, gg, ACT.Silu).then_inc(gg_silu, 1)

            def swa_exp(p):
                act.wait_ge(s_max, p + 1)
                for n in range(GROUP):
                    act.activation(scores[:, p % 2, n, :], scores[:, p % 2, n, :], ACT.Exp,
                                   bias=small[:, p % 2, n:n + 1], accum_out=small[:, 2 + p % 2, n:n + 1])\
                       .then_inc(act_step, 1)
                act.activation(small[:, 4 + p % 2, :], small[:, 4 + p % 2, :], ACT.Exp).then_inc(s_exp, 1)

            def swa_evict(p):
                c, g = divmod(p, KV_HEADS)
                act.wait_ge(p_turned, p + 1)
                if p:
                    act.wait_ge(pv_done, p)
                if c:
                    act.activation(p_t[:, 0, :], ps[:, 4, :], ACT.Copy).then_inc(act_step, 1)
                act.activation(p_tm[:, :], ps[0:N_META, 6, :], ACT.Copy).then_inc(p_act, 1)

            def swa_out(p):
                c, g = divmod(p, KV_HEADS)
                act.wait_ge(pv_done, p + 1)
                rows = slice(64 * g, 64 * g + 64)
                act.activation(o_swa[rows, :, c * C:(c + 1) * C], ps[rows, 7, :].rearrange("p (n t) -> p n t", n=GROUP),
                               ACT.Copy).then_inc(pv_evicted, 1)

            swa_exp(0)
            for p in range(NC * KV_HEADS):
                if p + 1 < NC * KV_HEADS:
                    swa_exp(p + 1)
                swa_evict(p)
                swa_out(p)
            act.wait_ge(pv_evicted, NC * KV_HEADS)
            act.activation(swa_sq, o_swa, ACT.Square).then_inc(os_squared, 1)
            act.wait_ge(norm_summed, N_SWA + 1)
            act.activation(decay[:, 0, :], ps[:, 0, :], ACT.Sqrt, bias=vec[:, V_EPS:V_EPS + 1],
                           scale=1 / (SWA_HEADS * HEAD_DIM)).then_inc(rms_ready, 1)
            act.wait_ge(mixed, 1)
            for k in range(KD):
                src = o_gla[:, k, :] if k < 4 else o_swa[:, k - 4, :]
                act.activation(cat_hi[:, k, :], src, ACT.Copy).then_inc(cat_hi_done, 1)
            for d in range(KD):
                split_hi(U_OUT, d + 2, W_UP)
                result_tile(d, d % 2, y2, V_POSTM, N_POSTM, U_OUT + d + 1, SEQ)
            root(N_POSTM, SEQ, 4, D_MODEL)
            operand(N_PRE2, SEQ, xc_hi, V_PRE2, KD)
            ffn_up(U_UP2, KF, hid2_hi, SEQ, N_PRE2)
            ffn_down(U_DOWN2, y3, V_POST2, N_POST2, SEQ, 0)
            root(N_POST2, SEQ, 4, D_MODEL, half=True)

        @block.vector
        def _(dve):
            steps = [0]

            def link(ins):
                steps[0] += 1
                ins.then_inc(dve_step, 1)
                dve.wait_ge(dve_step, steps[0])

            def split_lo(base, j, width, i=0):
                u, raw_slot, _, slot = unit(base, j, i)
                dve.wait_ge(hi_split, u + 1)
                dve.tensor_tensor(w_lo[:, slot, 0:width], raw[:, raw_slot, 0:width], f32(w_hi[:, slot, 0:width]),
                                  ALU.subtract).then_inc(lo_split, 1)

            def reciprocal(norm, n_tok):
                dve.wait_ge(rms_ready, norm + 1)
                dve.reciprocal(rnorm[:, 0:n_tok], rms[:, 0:n_tok]).then_inc(norm_ready, 1)
                dve.wait_ge(norm_ready, norm + 1)

            def low_part(n_tok, xh, xl, v0, k, count):
                dve.wait_ge(x_hi, count + k + 1)
                dve.scalar_tensor_tensor(out=xl[:, k, :], in0=h[:, k, tokens(n_tok)], scalar=vec[:, v0 + k:v0 + k + 1],
                                         in1=f32(xh[:, k, :]), op0=ALU.mult, op1=ALU.subtract).then_inc(x_ready, 1)

            def add_residual(y, k, n_tok):
                link(dve.tensor_tensor(y[:, k, :], y[:, k, :], rnorm[:, 0:n_tok], ALU.mult))
                return dve.tensor_tensor(h[:, k, tokens(n_tok)], h[:, k, tokens(n_tok)], y[:, k, :], ALU.add)

            def residual(post, n_tok, y, xh, xl, v0, count):
                reciprocal(post, n_tok)
                for k in range(KD):
                    add_residual(y, k, n_tok).then_inc(h_updated, 1)
                    if k:
                        low_part(n_tok, xh, xl, v0, k - 1, count)
                low_part(n_tok, xh, xl, v0, KD - 1, count)

            def hidden_tile(base, tile0, t, q, hi, lo, n_tok):
                dve.wait_ge(unit_used, base + 2 * t + 2)
                dve.tensor_tensor(row(gate, n_tok), in_psum(4 * q, n_tok), row(rnorm, n_tok), ALU.mult).then_inc(gate_scaled, 1)
                dve.tensor_tensor(row(up, n_tok), in_psum(4 * q + 2, n_tok), row(rnorm, n_tok), ALU.mult).then_inc(gu_evicted, 1)
                dve.wait_ge(gu_evicted, tile0 + t + 1)
                dve.wait_ge(silu_done, tile0 + t + 1)
                dve.tensor_tensor(up[:, 0:n_tok], up[:, 0:n_tok], gate[:, 0:n_tok], ALU.mult).then_inc(hid_written, 1)
                dve.wait_ge(hid_hi, tile0 + t + 1)
                dve.tensor_tensor(lo[:, t, :], up[:, 0:n_tok], f32(hi[:, t, :]), ALU.subtract).then_inc(hid_ready, 1)
                dve.wait_ge(hid_ready, tile0 + t + 1)

            def ffn_up(base, tile0, hi, lo, n_tok, norm):
                split_lo(base, 2, W_UP)
                split_lo(base, 3, W_UP)
                reciprocal(norm, n_tok)
                hidden_tile(base, tile0, 0, 0, hi, lo, n_tok)
                split_lo(base, 4, W_UP)
                split_lo(base, 5, W_UP)
                hidden_tile(base, tile0, 1, 1, hi, lo, n_tok)
                with dve.Fori(1, KF // 2 - 1) as i:
                    for n in range(2):
                        split_lo(base, 2 * n + 2, W_UP, i)
                        split_lo(base, 2 * n + 3, W_UP, i)
                        hidden_tile(base, tile0, 2 * i + n, n, hi, lo, n_tok)
                split_lo(base, UP_UNITS - 2, W_UP)
                split_lo(base, UP_UNITS - 1, W_UP)
                hidden_tile(base, tile0, KF - 2, 0, hi, lo, n_tok)
                split_lo(base, UP_UNITS, W_DOWN)
                split_lo(base, UP_UNITS + 1, W_DOWN)
                hidden_tile(base, tile0, KF - 1, 1, hi, lo, n_tok)

            dve.memset(ones[:, :], 1.0).then_inc(ones_set, 1)
            dve.wait_ge(vec_landed, 16)
            for k in range(KD):
                low_part(L, xa_hi, xa_lo, V_PRE1, k, 0)
            split_lo(U_UP1, 0, W_UP)
            split_lo(U_UP1, 1, W_UP)
            ffn_up(U_UP1, 0, hid1_hi, hid1_lo, L, N_PRE1)
            for j in range(DOWN_UNITS):
                split_lo(U_DOWN1, j + 2, W_DOWN if j + 2 < DOWN_UNITS else W_UP)
            residual(N_POST1, L, y1, xb_hi, xb_lo, V_PREM, KD)

            def in_evict(j):
                dve.wait_ge(unit_used, U_IN + j + 1)
                dve.tensor_tensor(row(in_dst[j], L), in_psum(in_bank(j), L), row(rnorm, L), ALU.mult).then_inc(proj_evicted, 1)

            for j in range(N_IN):
                split_lo(U_IN, j + 2, W_UP)
                if j == 1:
                    reciprocal(N_PREM, L)
                    in_evict(0)
                if j:
                    in_evict(j)

            dve.wait_ge(z_log, 2)
            for t in range(2):
                dve.tensor_scalar(row(z_min[:, t, :], L), in_psum(4 + 2 * t, L), vec[:, V_BA + t:V_BA + t + 1], 0.0,
                                  ALU.add, ALU.min).then_inc(z_read, 1)
            dve.wait_ge(z_read, 2)
            dve.wait_ge(z_log, 4)
            link(dve.tensor_tensor(z_min[:, :, :], z_min[:, :, :], z_log_t[:, :, :], ALU.subtract))
            for t in range(2):
                dve.tensor_tensor_scan(b_meta[:, t, :], ones[:, 0:N_META], z_min[:, t, 0:N_META], 0.0,
                                       ALU.mult, ALU.add).then_inc(dve_step, 1)
                steps[0] += 1
                for c in range(NC):
                    last = dve.tensor_tensor_scan(b_real[:, t, c * C:(c + 1) * C], ones[:, :],
                                                  z_min[:, t, N_META + c * C:N_META + (c + 1) * C], 0.0, ALU.mult, ALU.add)
                    if t == 0 or c < NC - 1:
                        last.then_inc(dve_step, 1)
                        steps[0] += 1
            last.then_inc(b_ready, 1)
            dve.wait_ge(b_ready, 1)
            dve.wait_ge(dve_step, steps[0])
            b8 = b_real[:, :, :].rearrange("p t (c n) -> p (t c) n", n=C)
            for t in range(2):
                bt = b_real[:, t, :].rearrange("p (c n) -> p c n", n=C)
                link(dve.tensor_tensor(k_out[:, t, N_META:L].rearrange("p (c n) -> p c n", n=C),
                                       bt[:, :, C - 1:C].broadcast_to([P, NC, C]), bt, ALU.subtract))
            dve.tensor_tensor(k_out[:, :, 0:N_META], b_meta[:, :, N_META - 1:N_META].broadcast_to([P, 2, N_META]),
                              b_meta[:, :, :], ALU.subtract).then_inc(k_diff, 1)
            link(dve.tensor_scalar(gq, gq, GLA_DK ** -0.5, None, ALU.mult))

            for n in range(5):
                x = row(sk, L) if n == 0 else sq_heads[:, n - 1, :]
                cs, sn = (row(cos_s, L), row(sin_s, L)) if n == 0 else (cos_s[:, N_META:L], sin_s[:, N_META:L])
                tmp = row(gate, L) if n == 0 else gate[:, 0:SEQ]
                src = in_psum(0, L) if n == 0 else ps[:, (2, 3, 0, 2)[n - 1], :]
                if n == 0:
                    dve.wait_ge(table_landed, 16 * 7)
                dve.wait_ge(rot_done, n + 1)
                dve.tensor_tensor(tmp, src, sn, ALU.mult).then_inc(rot_read, 1)
                link(dve.tensor_tensor(x, x, cs, ALU.mult))
                dve.wait_ge(rot_read, n + 1)
                dve.tensor_tensor(x, x, tmp, ALU.add).then_inc(rope_done, 1)
                dve.wait_ge(rope_done, n + 1)
            dve.wait_ge(k_exp, 1)
            dve.tensor_tensor(k_out[:, :, :], k_out[:, :, :], gk, ALU.mult).then_inc(k_out_ready, 1)
            dve.wait_ge(q_exp, 2)
            dve.tensor_tensor(q_in[:, :, :], q_in[:, :, :], gq, ALU.mult).then_inc(q_in_ready, 1)

            dve.wait_ge(sums_done, 1)
            link(dve.tensor_copy(state[:, :, 0, :], ps[:, 6:8, 0:P]))
            for c in range(1, NC):
                for t in range(2):
                    ins = dve.scalar_tensor_tensor(out=state[:, t, c, :], in0=state[:, t, c - 1, :],
                                                   scalar=dec[:, t, c - 1:c], in1=ps[:, 6 + t, c * P:(c + 1) * P],
                                                   op0=ALU.mult, op1=ALU.add)
                    if (c, t) == (NC - 1, 1):
                        ins.then_inc(states_ready, 1)
                    else:
                        link(ins)

            def lv_operands(lv):
                m = LEVELS[lv]
                d = decay[:, :, :].rearrange("p t (n x) -> p (t n) x", x=2 * m)
                b = b_real[:, :, :].rearrange("p t (n x) -> p (t n) x", x=2 * m)
                dve.tensor_tensor(d, b, b[:, :, m - 1:m].broadcast_to([P, 2 * SEQ // (2 * m), 2 * m]),
                                  ALU.subtract).then_inc(lv_diff, 1)
                dve.wait_ge(lv_exp, lv + 1)
                if lv == 0:
                    dve.wait_ge(lv_zeroed, 2)
                if lv >= 2:
                    dve.wait_ge(lv_scored, lv - 1)
                for t in range(2):
                    dt = decay[:, t, :].rearrange("p (n x) -> p n x", x=2 * m)
                    kt = gk[:, t, N_META:L].rearrange("p (n x) -> p n x", x=2 * m)
                    qt = gq[:, t, :].rearrange("p (n x) -> p n x", x=2 * m)
                    ko = lv_k[:, lv % 2, t, :].rearrange("p (n x) -> p n x", x=2 * m)
                    qo = lv_q[:, lv % 2, t, :].rearrange("p (n x) -> p n x", x=2 * m)
                    link(dve.tensor_tensor(ko[:, :, 0:m], kt[:, :, 0:m], dt[:, :, 0:m], ALU.mult))
                    ins = dve.tensor_tensor(qo[:, :, m:2 * m], qt[:, :, m:2 * m], dt[:, :, m:2 * m], ALU.mult)
                    if t == 0:
                        link(ins)
                ins.then_inc(lv_ready, 1)
                dve.wait_ge(lv_ready, lv + 1)

            def lv_take(lv):
                dve.wait_ge(lv_scored, lv + 1)
                for head in range(GLA_HEADS):
                    ins = dve.copy_predicated(attn[:, head, :].rearrange("p (c n) -> p c n", n=C),
                                              lmask[:, lv:lv + 1, :].broadcast_to([P, NC, C]),
                                              ps[:, head, :].rearrange("p (c n) -> p c n", n=C))
                    if head < GLA_HEADS - 1:
                        link(ins)
                ins.then_inc(lv_taken, 1)
                dve.wait_ge(lv_taken, lv + 1)

            dve.wait_ge(at_zeroed, 1)
            lv_operands(0)
            for lv in range(len(LEVELS) + 1):
                if lv + 1 < len(LEVELS):
                    lv_operands(lv + 1)
                lv_take(lv)

            def gla_norm():
                dve.wait_ge(rms_ready, N_GLA + 1)
                dve.reciprocal(gla_rms, gla_rms).then_inc(norm_ready, 1)
                dve.wait_ge(norm_ready, N_GLA + 1)
                dve.wait_ge(og_evicted, 1)
                link(dve.scalar_tensor_tensor(out=o_gla, in0=o_gla, scalar=vec[:, V_GLA:V_GLA + 1], in1=gla_rms,
                                              op0=ALU.mult, op1=ALU.mult))
                dve.wait_ge(gg_silu, 1)
                link(dve.tensor_tensor(o_gla, o_gla, gg, ALU.mult))

            def swa_mask(p):
                c, g = divmod(p, KV_HEADS)
                sc = scores[:, p % 2, :, :]
                neg_max, sink = small[:, p % 2, :], vec[:, V_SINK + GROUP * g:V_SINK + GROUP * (g + 1)]
                dve.wait_ge(s_done, p + 1)
                if p >= 2:
                    dve.wait_ge(p_turned, p - 1)
                dve.scalar_tensor_tensor(out=sc, in0=ps[:, 0:GROUP, 0:SPAN], scalar=HEAD_DIM ** -0.5,
                                         in1=band_s[:, min(c, 1):min(c, 1) + 1, :].broadcast_to([P, GROUP, SPAN]),
                                         op0=ALU.mult, op1=ALU.add).then_inc(s_masked, 1)
                dve.wait_ge(s_masked, p + 1)
                link(dve.tensor_reduce(neg_max, sc, AX_X, ALU.max))
                link(dve.tensor_tensor(neg_max, neg_max, sink, ALU.max))
                link(dve.tensor_scalar(neg_max, neg_max, -1.0, None, ALU.mult))
                dve.tensor_tensor(small[:, 4 + p % 2, :], sink, neg_max, ALU.add).then_inc(s_max, 1)

            def swa_norm(p):
                rowsum, sink_exp = small[:, 2 + p % 2, :], small[:, 4 + p % 2, :]
                dve.wait_ge(s_exp, p + 1)
                link(dve.tensor_tensor(rowsum, rowsum, sink_exp, ALU.add))
                link(dve.reciprocal(rowsum, rowsum))
                for n in range(GROUP):
                    ins = dve.tensor_scalar(scores[:, p % 2, n, :], scores[:, p % 2, n, :], rowsum[:, n:n + 1], None, ALU.mult)
                    if n < GROUP - 1:
                        link(ins)
                ins.then_inc(s_normed, 1)

            def swa_evict(p):
                dve.wait_ge(p_turned, p + 1)
                if p:
                    dve.wait_ge(pv_done, p)
                dve.tensor_copy(p_t[:, 1, :], ps[:, 5, :]).then_inc(p_dve, 1)

            swa_mask(0)
            for p in range(NC * KV_HEADS):
                if p + 1 < NC * KV_HEADS:
                    swa_mask(p + 1)
                swa_norm(p)
                if p == 0:
                    gla_norm()
                swa_evict(p)
            dve.wait_ge(rms_ready, N_SWA + 1)
            dve.reciprocal(decay[:, 1, :], decay[:, 0, :]).then_inc(norm_ready, 1)
            dve.wait_ge(norm_ready, N_SWA + 1)
            for n in range(4):
                ins = dve.scalar_tensor_tensor(out=o_swa[:, n, :], in0=o_swa[:, n, :], scalar=vec[:, V_SWA + n:V_SWA + n + 1],
                                               in1=decay[:, 1, :], op0=ALU.mult, op1=ALU.mult)
                if n < 3:
                    link(ins)
            ins.then_inc(mixed, 1)
            dve.wait_ge(mixed, 1)
            for k in range(KD):
                src = o_gla[:, k, :] if k < 4 else o_swa[:, k - 4, :]
                dve.wait_ge(cat_hi_done, k + 1)
                dve.tensor_tensor(cat_lo[:, k, :], src, f32(cat_hi[:, k, :]), ALU.subtract).then_inc(cat_ready, 1)
            for d in range(KD):
                split_lo(U_OUT, d + 2, W_UP)
            residual(N_POSTM, SEQ, y2, xc_hi, xc_lo, V_PRE2, 2 * KD)
            ffn_up(U_UP2, KF, hid2_hi, hid2_lo, SEQ, N_PRE2)
            for j in range(DOWN_UNITS - 2):
                split_lo(U_DOWN2, j + 2, W_DOWN)
            reciprocal(N_POST2, SEQ)
            for k in range(KD):
                add_residual(y3, k, SEQ).then_inc(out_ready, 1)

        @block.gpsimd
        def _(pool):
            def add_squares(norm, n_tok, done, ready):
                for k in range(1, KD):
                    pool.wait_ge(done, ready + k + 1)
                    n = (KD - 1) * WIDE[norm] + k
                    if k > 1:
                        pool.wait_ge(summed, n - 1)
                    pool.tensor_tensor(sumsq[:, 0:n_tok], sumsq[:, 0:n_tok], sq[:, k % 2, 0:n_tok], ALU.add)\
                        .then_inc(summed, 1)

            add_squares(N_PRE1, L, squared, 0)
            add_squares(N_POST1, L, y_evicted, 0)
            add_squares(N_PREM, L, squared, KD)

            pool.wait_ge(unit_used, U_IN)
            pool.memset(kx[:, 0, N_META:N_META + C], 0.0).then_inc(kx_ready, 1)
            pool.wait_ge(unit_used, U_OUT)
            pool.memset(lv_k[:, :, :, :], 0.0).then_inc(lv_zeroed, 1)
            pool.memset(lv_q[:, :, :, :], 0.0).then_inc(lv_zeroed, 1)
            pool.wait_ge(v_turned, 2)
            pool.memset(attn, 0.0).then_inc(at_zeroed, 1)
            pool.wait_ge(rope_done, 1)
            pool.wait_ge(kx_ready, 1)
            for c in range(NC):
                pool.tensor_copy(kx[:, c, 0:N_META], sk[:, 0:N_META]).then_inc(kx_ready, 1)
                lo, col = (c - 1, N_META) if c else (0, N_META + C)
                ins = pool.tensor_copy(kx[:, c, col:SPAN], sk[:, N_META + lo * C:N_META + (c + 1) * C])
                ins.then_inc(kx_ready, 1)
            add_squares(N_POSTM, SEQ, y_evicted, KD)
            add_squares(N_PRE2, SEQ, squared, 2 * KD)
            add_squares(N_POST2, SEQ, y_evicted, 2 * KD)


def rope_tables():
    half = HEAD_DIM // 2
    inv_freq = (1.0 / (np.float32(ROPE_THETA) ** (np.arange(0, HEAD_DIM, 2, dtype=np.float32) / np.float32(HEAD_DIM))))
    ang = inv_freq.astype(np.float32)[:, None] * np.arange(L, dtype=np.float32)[None, :]
    cos, sin = np.cos(ang), np.sin(ang)
    return (np.concatenate([cos] * 4).astype(np.float32), np.concatenate([-sin, sin] * 2).astype(np.float32))


def masks():
    t, s = np.arange(C)[:, None], np.arange(C)[None, :]
    meta = np.zeros((C, N_META), np.float32)
    own = np.where(s <= t, 0.0, NEG).astype(np.float32)
    before = np.where(s > t, 0.0, NEG).astype(np.float32)
    none = np.full((C, C), NEG, np.float32)
    band = np.stack([np.concatenate([meta, none, own], 1), np.concatenate([meta, before, own], 1)], 1)
    j, i = t, s
    levels = [(j // (2 * m) == i // (2 * m)) & (j % (2 * m) < m) & (i % (2 * m) >= m) for m in LEVELS]
    levels.append(j == i)
    return band, np.stack(levels, 1).astype(np.uint32)


def kernel(**inputs):
    import concourse.bacc as bacc
    from concourse.bass_utils import run_bass_kernel_spmd

    a = {name: np.asarray(value) for name, value in inputs.items()}

    def tiles(w, k_tiles):
        return w.reshape(k_tiles, P, w.shape[1] // P, P).transpose(2, 1, 0, 3)

    def up_units(gate, up):
        both = np.stack([tiles(gate, KD), tiles(up, KD)], 1)
        return np.ascontiguousarray(both.reshape(UP_UNITS, P, W_UP))

    def down_units(w):
        t = tiles(w, KF).reshape(KD, P, 2, KH, P).transpose(0, 2, 1, 3, 4)
        return np.ascontiguousarray(t.reshape(DOWN_UNITS, P, W_DOWN))

    def columns(v):
        return v.reshape(-1, P).T

    def heads_side_by_side(w, axis):
        shape = w.shape
        w = np.moveaxis(w, axis, 0).reshape(KV_HEADS, GROUP, HEAD_DIM, -1).transpose(1, 0, 2, 3)
        return np.moveaxis(w.reshape((SWA_HEADS * HEAD_DIM,) + tuple(np.delete(shape, axis))), 0, axis)

    w_in = a["w_in"][0]
    at = np.cumsum([0, 256, 256, 512, 512, GATE_RANK, 512, 128, 128])
    q, k, v, g, ga, sq, sk, sv = (w_in[:, at[n]:at[n + 1]] for n in range(8))
    ga = np.concatenate([ga, np.zeros((D_MODEL, P - GATE_RANK), w_in.dtype)], 1)
    w_in = np.concatenate([ga, k, q, sk, sv, v, heads_side_by_side(sq, 1), g], 1)
    w_out = a["w_out"][0]
    w_out = np.concatenate([w_out[:512], heads_side_by_side(w_out[512:], 0)], 0)
    vecs = np.concatenate(
        [columns(a[n][0]) for n in ("ffn1_pre_norm", "ffn1_post_norm", "mix_pre_norm", "mix_post_norm",
                                    "ffn2_pre_norm", "ffn2_post_norm")]
        + [columns(heads_side_by_side(a["swa_out_norm"][0], 0)), columns(a["gla_out_norm"][0]),
           columns(a["gla_b_a"][0]), np.broadcast_to(a["swa_sinks"][0], (P, SWA_HEADS)),
           np.broadcast_to(np.array([EPS, 4 * EPS], np.float32), (P, 2))], 1)
    x_t = np.concatenate([a["meta_tokens"], a["x"][0]], 0).T.reshape(KD, P, L).transpose(1, 0, 2)
    cos_t, sin_t = rope_tables()
    band, level_mask = masks()
    arrays = {
        "x_t": x_t, "vecs": vecs,
        "up1": up_units(a["ffn1_w_gate"][0], a["ffn1_w_up"][0]), "down1": down_units(a["ffn1_w_down"][0]),
        "w_in": tiles(w_in, KD).reshape(N_IN, P, W_UP), "w_a2": a["gla_w_a2"][0],
        "w_out": tiles(w_out, KD).reshape(KD, P, W_UP),
        "up2": up_units(a["ffn2_w_gate"][0], a["ffn2_w_up"][0]), "down2": down_units(a["ffn2_w_down"][0]),
        "cos_t": cos_t, "sin_t": sin_t,
        "perm": np.eye(P, dtype=np.float32)[np.arange(P) ^ (HEAD_DIM // 2)], "ident": np.eye(P, dtype=np.float32),
        "band": band, "level_mask": level_mask,
    }
    arrays = {f"in_{name}": np.ascontiguousarray(value) for name, value in arrays.items()}
    nc = bacc.Bacc("TRN2", target_bir_lowering=False, num_devices=1)
    aps = [nc.dram_tensor(name, v.shape, mybir.dt.from_np(v.dtype), kind="ExternalInput").ap()
           for name, v in arrays.items()]
    out = nc.dram_tensor("out", (P, KD, SEQ), F32, kind="ExternalOutput").ap()
    hybrid_layer(nc, *aps, out)
    r = run_bass_kernel_spmd(nc, [arrays], core_ids=[0])
    y = np.asarray(r.results[0]["out"])
    return np.ascontiguousarray(y.transpose(1, 0, 2).reshape(D_MODEL, SEQ).T)[None]
```

```python
from contextlib import ExitStack

import numpy as np
import concourse.bass as bass
from concourse import mybir

F32 = mybir.dt.float32
F32R = mybir.dt.float32r
U32 = mybir.dt.uint32
ALU = mybir.AluOpType
ACT = mybir.ActivationFunctionType
AX_X = mybir.AxisListType.X

P = 128
D_MODEL = 1024
SEQ = 512
N_META = 16
L = SEQ + N_META
D_FF = 2816
EPS = 1e-6
KD = D_MODEL // P
KF = D_FF // P
KH = KF // 2

GLA_HEADS, GLA_DK, GLA_DV, GATE_RANK = 4, 64, 128, 16
GLA_TAU = 16.0
SWA_HEADS, KV_HEADS, HEAD_DIM = 8, 2, 64
GROUP = SWA_HEADS // KV_HEADS
ROPE_THETA = 10000.0
NEG = -1e30
C = 128
NC = SEQ // C
SPAN = N_META + 2 * C
LEVELS = [64, 32, 16, 8, 4, 2, 1]

T_GA, T_GK, T_GQ, T_SV, T_SK, T_SQ, T_GV, T_GG = 0, 1, 3, 5, 6, 7, 11, 15
N_IN = 19

UP_UNITS, DOWN_UNITS = 2 * KF, 2 * KD
U_UP1 = 0
U_DOWN1 = U_UP1 + UP_UNITS
U_IN = U_DOWN1 + DOWN_UNITS
U_OUT = U_IN + N_IN
U_UP2 = U_OUT + KD
U_DOWN2 = U_UP2 + UP_UNITS
N_UNITS = U_DOWN2 + DOWN_UNITS
RAW, OPS = 4, 2
W_UP, W_DOWN = KD * P, KH * P

V_PRE1, V_POST1, V_PREM, V_POSTM, V_PRE2, V_POST2 = (KD * n for n in range(6))
V_SWA = 6 * KD
V_GLA = V_SWA + 4
V_BA = V_GLA + 1
V_SINK = V_BA + 2
V_EPS = V_SINK + SWA_HEADS
N_VEC = V_EPS + 2

N_PRE1, N_POST1, N_PREM, N_SWA, N_GLA, N_POSTM, N_PRE2, N_POST2 = range(8)
PRE = {N_PRE1: 0, N_PREM: 1, N_PRE2: 2}
POST = {N_POST1: 0, N_POSTM: 1, N_POST2: 2}
BLOCKS = 4
POOL_TILES = (3, 6)
PAIR, PASSES = 2, NC * KV_HEADS * 2


def norm_copies(norm):
    return norm + 1 - 2 * (norm > N_GLA)


def hybrid_layer(nc, x_t, vecs, up1, down1, w_in, w_a2, w_out, up2, down2, cos_t, sin_t, ident, select, band,
                 level_mask, out):
    ctx = ExitStack()
    with ctx:
        def sb(name, shape, dt, stack=ctx):
            return stack.enter_context(nc.sbuf_tensor(name, shape, dt))

        def sem(name):
            return ctx.enter_context(nc.semaphore(name))

        h = sb("h", [P, KD, L], F32)
        raw = sb("raw", [P, RAW, W_DOWN], F32)
        w_hi = sb("w_hi", [P, OPS, W_DOWN], F32R)
        w_lo = sb("w_lo", [P, OPS, W_DOWN], F32R)
        vec = sb("vec", [P, N_VEC], F32)
        carry = sb("carry", [P, SEQ], F32)
        ident_s = sb("ident_s", [P, P], F32)
        select_s = sb("select_s", [P, 31], F32)
        stat = sb("stat", [GLA_HEADS * NC, 2, L // BLOCKS], F32)
        sumsq = sb("sumsq", [P, L], F32)
        rnorm = sb("rnorm", [P, L], F32)
        gate = sb("gate", [P, L], F32)
        up = sb("up", [P, L], F32)
        sq = sb("sq", [P, 2, L], F32)
        small_root = sb("small_root", [P, 1], F32)
        with ExitStack() as s:
            xa_hi, xa_lo = sb("xa_hi", [P, KD, L], F32R, s), sb("xa_lo", [P, KD, L], F32R, s)
            hid1_hi, hid1_lo = sb("hid1_hi", [P, KF, L], F32R, s), sb("hid1_lo", [P, KF, L], F32R, s)
        with ExitStack() as s:
            y1 = sb("y1", [P, KD, L], F32, s)
            sb("y1_rest", [P, KD, L], F32, s)
            xb_hi, xb_lo = sb("xb_hi", [P, KD, L], F32R, s), sb("xb_lo", [P, KD, L], F32R, s)
        with ExitStack() as s:
            proj = sb("proj", [P, 16, L], F32, s)
            with ExitStack() as x:
                vtok = sb("vtok", [P, NC + 1, 4 * P], F32, x)
                state = sb("state", [P, 2, NC, GLA_DV], F32, x)
                sb("gap", [P, 2816], F32, x)
                gla_sq = sb("gla_sq", [P, GLA_HEADS, SEQ], F32, x)
            with ExitStack() as x:
                cat_hi, cat_lo = sb("cat_hi", [P, KD, SEQ], F32R, x), sb("cat_lo", [P, KD, SEQ], F32R, x)
            sb("mix_operand", [P, 2 * KD, L], F32, s)
            kv2 = sb("kv2", [P, 2, L], F32, s)
            with ExitStack() as x:
                b_real = sb("b_real", [P, 2, SEQ], F32, x)
                lmask = sb("lmask", [P, len(LEVELS) + 1, C], U32, x)
            swa_sq = sb("swa_sq", [P, 4, SEQ], F32, s)
            b_meta = sb("b_meta", [P, 2, N_META], F32, s)
            dec = sb("dec", [P, 2, NC], F32, s)
            q_in = sb("q_in", [P, 2, SEQ], F32, s)
            k_out = sb("k_out", [P, 2, L], F32, s)
            ktok = sb("ktok", [P, NC, 2 * P], F32, s)
            attn = sb("attn", [P, GLA_HEADS * SEQ], F32, s)
            cos_s, sin_s = sb("cos_s", [P, L], F32, s), sb("sin_s", [P, L], F32, s)
            wa2_s = sb("wa2_s", [GATE_RANK, 2 * P], F32, s)
            band_s = sb("band_s", [P, 2, SPAN], F32, s)
            kx = sb("kx", [P, NC, SPAN], F32, s)
            small = sb("small", [P, 3, 3, PAIR], F32, s)
            with ExitStack() as x:
                decay = sb("decay", [P, 2, SEQ], F32, x)
                lv_k = sb("lv_k", [P, 2, 2, SEQ], F32, x)
                lv_q = sb("lv_q", [P, 2, 2, SEQ], F32, x)
            with ExitStack() as x:
                scores = sb("scores", [P, 3, PAIR, SPAN], F32, x)
                p_t = sb("p_t", [P, PAIR, 2, C], F32, x)
                p_tm = sb("p_tm", [N_META, PAIR, C], F32, x)
                vs_tok = sb("vs_tok", [P, NC + 1, P], F32, x)
        with ExitStack() as s:
            hid2_hi, hid2_lo = sb("hid2_hi", [P, KF, SEQ], F32R, s), sb("hid2_lo", [P, KF, SEQ], F32R, s)
            xc_hi, xc_lo = sb("xc_hi", [P, KD, SEQ], F32R, s), sb("xc_lo", [P, KD, SEQ], F32R, s)
        with ExitStack() as s:
            y2 = sb("y2", [P, KD, SEQ], F32, s)
        with ExitStack() as s:
            sb("hid2_space", [P, 2 * KF, SEQ], F32, s)
            y3 = sb("y3", [P, KD, SEQ], F32, s)

        ps = ctx.enter_context(nc.psum_tensor("ps", [P, 8, 512], F32))

        raw_landed = [sem(f"raw_landed{i}") for i in range(RAW)]
        hi_split, lo_split = sem("hi_split"), sem("lo_split")
        unit_used = sem("unit_used")
        x_landed = [sem(f"x_landed{k}") for k in range(KD)]
        vec_landed, select_landed, table_landed = sem("vec_landed"), sem("select_landed"), sem("table_landed")
        squared, summed = sem("squared"), sem("summed")
        y_squared, y_summed, y_evicted = sem("y_squared"), sem("y_summed"), sem("y_evicted")
        norm_summed, rms_ready, norm_ready = sem("norm_summed"), sem("rms_ready"), sem("norm_ready")
        norm_spread, r_ready = sem("norm_spread"), sem("r_ready")
        h_updated, h_pool, y_scaled = sem("h_updated"), sem("h_pool"), sem("y_scaled")
        x_hi, x_ready = sem("x_hi"), sem("x_ready")
        gate_scaled, gu_evicted = sem("gate_scaled"), sem("gu_evicted")
        silu_done, hid_written, hid_hi, hid_ready = sem("silu_done"), sem("hid_written"), sem("hid_hi"), sem("hid_ready")
        proj_evicted = sem("proj_evicted")
        z_done, z_log, z_read = sem("z_done"), sem("z_log"), sem("z_read")
        b_ready, k_diff, k_exp, q_exp = sem("b_ready"), sem("k_diff"), sem("k_exp"), sem("q_exp")
        k_out_ready, q_in_ready, q_scaled = sem("k_out_ready"), sem("q_in_ready"), sem("q_scaled")
        tables_scaled, kx_ready = sem("tables_scaled"), sem("kx_ready")
        attn_zeroed, lv_zeroed = sem("attn_zeroed"), sem("lv_zeroed")
        lv_diff, lv_exp, lv_k_ready, lv_q_ready = sem("lv_diff"), sem("lv_exp"), sem("lv_k_ready"), sem("lv_q_ready")
        lv_scored, lv_taken = sem("lv_scored"), sem("lv_taken")
        turned, turned_out = sem("turned"), sem("turned_out")
        v_turned, v_act, v_dve, vm_turned, vm_act = (sem("v_turned"), sem("v_act"), sem("v_dve"), sem("vm_turned"),
                                                     sem("vm_act"))
        sums_done, states_ready = sem("sums_done"), sem("states_ready")
        og_done, og_squared, og_taken, gg_silu = sem("og_done"), sem("og_squared"), sem("og_taken"), sem("gg_silu")
        s_done, s_masked, s_max, s_exp, s_normed = sem("s_done"), sem("s_masked"), sem("s_max"), sem("s_exp"), sem("s_normed")
        p_turned, p_taken = sem("p_turned"), sem("p_taken")
        pv_done, pv_evicted = sem("pv_done"), sem("pv_evicted")
        cat_raw, cat_hi_done, cat_ready = sem("cat_raw"), sem("cat_hi_done"), sem("cat_ready")
        dve_step, act_step = sem("dve_step"), sem("act_step")
        out_dve, out_pool, stored = sem("out_dve"), sem("out_pool"), sem("stored")

        def f32(ap):
            return ap.bitcast(F32)

        def unit(base, j, i=0):
            return base + j + RAW * i, (base + j) % RAW, (base + j) // RAW + i, (base + j) % OPS

        def in_psum(bank, n_tok):
            return ps[:, bank:bank + 2, 0:L // 2] if n_tok == L else ps[:, bank, 0:SEQ]

        def row(ap, n_tok):
            return ap.rearrange("p (b n) -> p b n", b=2) if n_tok == L else ap[:, 0:SEQ]

        def tokens(n_tok):
            return slice(L - n_tok, L)

        def pool_tiles_before(k):
            return sum(n < k for n in POOL_TILES)

        def in_bank(j):
            return 2 * j if j < 3 else 2 * ((j - 3) % 2)

        in_dst = [None] * N_IN
        in_dst[T_GA] = proj[:, 15, :]
        in_dst[T_SK], in_dst[T_SV] = kv2[:, 0, :], kv2[:, 1, :]
        for t, at, count in ((T_GK, 0, 2), (T_GQ, 2, 2), (T_GV, 4, 4), (T_SQ, 8, 4), (T_GG, 12, 4)):
            for n in range(count):
                in_dst[t + n] = proj[:, at + n, :]
        ga = proj[0:GATE_RANK, 15, :]
        gk, gq = proj[:, 0:2, :], proj[:, 2:4, N_META:L]
        gv, gg = proj[:, 4:8, :], proj[:, 12:16, N_META:L]
        sk, sv = kv2[:, 0, :], kv2[:, 1, :]
        sq_heads = proj[:, 8:12, N_META:L]
        o_gla = proj[:, 0:4, 0:SEQ]
        o_swa = sq_heads
        z_log_t = attn[:, 0:2 * L].rearrange("p (t n) -> p t n", t=2)
        z_min = k_out[:, :, :]
        attn_heads = attn[:, :].rearrange("p (h n) -> p h n", h=GLA_HEADS)

        GAP_Z = 2 * 3 + 1
        GAP_B, GAP_DECAY, GAP_LV = GAP_Z + 2, GAP_Z + 3, 2 * 6 + 1
        GAP_TURN = GAP_LV + len(LEVELS) + 1
        GAP_SWA = GAP_TURN + 1
        assert GAP_SWA + PASSES == 2 * N_IN

        def swa_pass(p):
            return p // (NC * KV_HEADS), (p // KV_HEADS) % NC, p % KV_HEADS

        block = ctx.enter_context(nc.Block())

        @block.sync
        def _(sp):
            def load(src, base, j, width, i=0):
                u, slot, turn, _ = unit(base, j, i)
                if base + j >= RAW:
                    sp.wait_ge(lo_split, u - RAW + 1)
                sp.dma_start(raw[:, slot, 0:width], src[j + RAW * i]).then_inc(raw_landed[slot], 16)

            def stream(src, base, count, width, first=0):
                rounds = (count - first) // RAW
                with sp.Fori(0, rounds) as i:
                    for j in range(RAW):
                        load(src, base, first + j, width, i)
                for j in range(first + RAW * rounds, count):
                    load(src, base, j, width)

            sp.dma_start(vec[:, :], vecs).then_inc(vec_landed, 16)
            load(up1, U_UP1, 0, W_UP)
            for k in range(KD):
                sp.dma_start(h[:, k, :], x_t[:, k, :]).then_inc(x_landed[k], 16)
                if k == 0:
                    load(up1, U_UP1, 1, W_UP)
            sp.dma_start(ident_s[:, :], ident).then_inc(select_landed, 16)
            sp.dma_start(select_s[:, :], select).then_inc(select_landed, 16)
            load(up1, U_UP1, 2, W_UP)
            load(up1, U_UP1, 3, W_UP)
            stream(up1, U_UP1, UP_UNITS, W_UP, first=RAW)
            stream(down1, U_DOWN1, DOWN_UNITS, W_DOWN)
            stream(w_in, U_IN, 4, W_UP)
            sp.wait_ge(unit_used, U_IN)
            for dst, src in ((cos_s[:, :], cos_t), (sin_s[:, :], sin_t), (wa2_s[:, :], w_a2),
                             (band_s[:, :, :], band), (lmask[:, :, :], level_mask)):
                sp.dma_start(dst, src).then_inc(table_landed, 16)
            stream(w_in, U_IN, N_IN, W_UP, first=4)
            stream(w_out, U_OUT, KD, W_UP)
            stream(up2, U_UP2, UP_UNITS, W_UP)
            stream(down2, U_DOWN2, DOWN_UNITS, W_DOWN)
            for k in range(KD):
                if k in POOL_TILES:
                    sp.wait_ge(out_pool, pool_tiles_before(k) + 1)
                else:
                    sp.wait_ge(out_dve, k - pool_tiles_before(k) + 1)
                sp.dma_start(out[:, k, :], h[:, k, N_META:L]).then_inc(stored, 16)
            sp.wait_ge(stored, 16 * KD)

        @block.tensor
        def _(pe):
            def k_tile(slot, k, xh, xl, kx_, bank, n_tok, first, last):
                width = L // 2 if n_tok == L else SEQ
                wh, wl = w_hi[:, slot, k * P:(k + 1) * P], w_lo[:, slot, k * P:(k + 1) * P]
                for n in range(n_tok // width):
                    dst, cols = ps[:, bank + n, 0:width], slice(n * width, (n + 1) * width)
                    pe.matmul(dst, wh, xh[:, kx_, cols], start=first, stop=False)
                    pe.matmul(dst, wh, xl[:, kx_, cols], start=False, stop=False)
                    mm = pe.matmul(dst, wl, xh[:, kx_, cols], start=False, stop=last)
                return mm

            def products(base, j, i, xh, xl, k0, nk, bank, n_tok, first=True, last=True, after=None):
                u, _, _, slot = unit(base, j, i)
                pe.wait_ge(lo_split, u + 1)
                for k in range(nk):
                    mm = k_tile(slot, k, xh, xl, k0 + k, bank, n_tok, first and k == 0, last and k == nk - 1)
                    if k == nk - 1:
                        mm.then_inc(unit_used, 1)
                    if after and k in after:
                        after[k]()

            def lead_pair(base, xh, xl, banks, n_tok, ready):
                for step in range(KD + 2):
                    if step < KD:
                        ready(step)
                        if step == 0:
                            pe.wait_ge(lo_split, base + 1)
                        mm = k_tile(base % OPS, step, xh, xl, step, banks[0], n_tok, step == 0, step == KD - 1)
                        if step == KD - 1:
                            mm.then_inc(unit_used, 1)
                    if step >= 2:
                        k = step - 2
                        if k == 0:
                            pe.wait_ge(lo_split, base + 2)
                        mm = k_tile((base + 1) % OPS, k, xh, xl, k, banks[1], n_tok, k == 0, k == KD - 1)
                mm.then_inc(unit_used, 1)

            def block_sums(norm, srcs, n_tok, bank, rows=BLOCKS, row0=0, start=True, stop=True):
                w = n_tok // BLOCKS
                for n, src in enumerate(srcs):
                    for b in range(BLOCKS):
                        at = row0 + b
                        mm = pe.matmul(ps[0:rows, bank, 0:w], select_s[:, 15 - at:15 - at + rows],
                                       src[:, b * w:(b + 1) * w], start=start and n == 0 and b == 0,
                                       stop=stop and n == len(srcs) - 1 and b == BLOCKS - 1)
                if stop:
                    mm.then_inc(norm_summed, 1)

            def spread(norm, n_tok, bank, rows=BLOCKS):
                pe.wait_ge(norm_ready, norm + 1)
                w = n_tok // BLOCKS
                for b in range(rows):
                    if rows > BLOCKS:
                        dst = ps[:, bank + 2 * (b // BLOCKS), (b % BLOCKS) * w:(b % BLOCKS + 1) * w]
                    elif n_tok == L:
                        dst = ps[:, bank + b // 2, (b % 2) * w:(b % 2 + 1) * w]
                    else:
                        dst = ps[:, bank, b * w:(b + 1) * w]
                    mm = pe.matmul(dst, ident_s[0:rows, b:b + 1].broadcast_to([rows, P]), stat[0:rows, norm % 2, 0:w],
                                   start=True, stop=True)
                mm.then_inc(norm_spread, 1)

            def pre_sum(norm, n_tok, bank):
                if norm == N_PRE1:
                    pe.wait_ge(select_landed, 32)
                pe.wait_ge(summed, (KD - 1) * (PRE[norm] + 1))
                block_sums(norm, [sumsq], n_tok, bank)

            def post_norm(norm, n_tok):
                pe.wait_ge(y_summed, (KD - 1) * (POST[norm] + 1))
                block_sums(norm, [sumsq], n_tok, 4)
                spread(norm, n_tok, 4)

            def ffn_up(base, tile0, xh, xl, n_tok, norm, x0):
                def ready(k):
                    pe.wait_ge(x_ready, x0 + k + 1)

                def tile(t, j, q, i=0):
                    pe.wait_ge(gu_evicted, tile0 + t - 1)
                    products(base, j, i, xh, xl, 0, KD, 4 * q, n_tok)
                    products(base, j + 1, i, xh, xl, 0, KD, 4 * q + 2, n_tok)

                lead_pair(base, xh, xl, (0, 2), n_tok, ready)
                if n_tok == L:
                    pre_sum(norm, n_tok, 6)
                    products(base, 2, 0, xh, xl, 0, KD, 4, n_tok, after={4: lambda: spread(norm, n_tok, 6)})
                    pe.wait_ge(r_ready, norm_copies(norm))
                    products(base, 3, 0, xh, xl, 0, KD, 6, n_tok)
                else:
                    products(base, 2, 0, xh, xl, 0, KD, 4, n_tok)
                    pre_sum(norm, n_tok, 1)
                    products(base, 3, 0, xh, xl, 0, KD, 6, n_tok, after={3: lambda: spread(norm, n_tok, 3)})
                with pe.Fori(1, KF // 2) as i:
                    tile(2 * i, 0, 0, i)
                    tile(2 * i + 1, 2, 1, i)

            def ffn_down(base, tile0, hid0, hi, lo, n_tok):
                def tile(d, j, q, i=0):
                    if isinstance(d, int) and d == 0:
                        pe.wait_ge(hid_ready, hid0 + KF - 2)
                        pe.wait_ge(gu_evicted, hid0 + KF - 1)
                    else:
                        if not (isinstance(d, int) and tile0 + d < 2):
                            pe.wait_ge(y_evicted, tile0 + d - 1)
                    products(base, j, i, hi, lo, 0, KH, 2 * q, n_tok, last=False)
                    if isinstance(d, int) and d == 0:
                        pe.wait_ge(hid_ready, hid0 + KF)
                    products(base, j + 1, i, hi, lo, KH, KH, 2 * q, n_tok, first=False)

                tile(0, 0, 0)
                tile(1, 2, 1)
                with pe.Fori(1, KD // 2) as i:
                    tile(2 * i, 0, 0, i)
                    tile(2 * i + 1, 2, 1, i)

            def gate_logits():
                pe.wait_ge(table_landed, 16 * 5)
                pe.wait_ge(proj_evicted, 3)
                for t in range(2):
                    for n in range(2):
                        mm = pe.matmul(ps[:, 4 + 2 * t + n, 0:L // 2], wa2_s[:, t * P:(t + 1) * P],
                                       ga[:, n * L // 2:(n + 1) * L // 2], start=True, stop=True)
                mm.then_inc(z_done, 1)

            def level_scores(lv):
                diagonal = lv == len(LEVELS)
                if not diagonal:
                    pe.wait_ge(lv_k_ready, lv + 1)
                    pe.wait_ge(lv_q_ready, lv + 1)
                if lv:
                    pe.wait_ge(lv_taken, lv)
                for head in range(GLA_HEADS):
                    rows = slice(64 * (head % 2), 64 * (head % 2) + 64)
                    for c in range(NC):
                        cols = slice(c * C, (c + 1) * C)
                        if diagonal:
                            kl, ql = gk[rows, head // 2, N_META + c * C:N_META + (c + 1) * C], gq[rows, head // 2, cols]
                        else:
                            kl, ql = lv_k[rows, lv % 2, head // 2, cols], lv_q[rows, lv % 2, head // 2, cols]
                        mm = pe.matmul(ps[:, 4 + head, cols], kl, ql, start=True, stop=True)
                mm.then_inc(lv_scored, 1)

            def turn_early():
                pe.wait_ge(lv_taken, len(LEVELS) + 1)
                pe.wait_ge(k_out_ready, 1)
                for b in range(NC):
                    pe.transpose(ps[:, 4, b * P:(b + 1) * P], sv[:, N_META + b * C:N_META + (b + 1) * C], ident_s[:, :])
                pe.transpose(ps[0:N_META, 5, 0:P], sv[:, 0:N_META], ident_s[:, :])
                for c in range(NC - 1):
                    for t in range(2):
                        col = (c % 2) * 2 * P + t * P
                        pe.transpose(ps[:, 6 + c // 2, col:col + P], k_out[:, t, N_META + c * C:N_META + (c + 1) * C],
                                     ident_s[:, :])
                for t in range(2):
                    mm = pe.transpose(ps[0:N_META, 7, (2 + t) * P:(3 + t) * P], k_out[:, t, 0:N_META], ident_s[:, :])
                mm.then_inc(turned, 1)

            def swa_scores(p):
                pair, c, g = swa_pass(p)
                rows = slice(64 * g, 64 * g + 64)
                if p:
                    pe.wait_ge(s_masked, p)
                else:
                    pe.wait_ge(turned_out, 1)
                    pe.wait_ge(kx_ready, 1 + 2 * NC)
                for n in range(PAIR):
                    mm = pe.matmul(ps[:, 4 + n, 0:SPAN], sq_heads[rows, PAIR * pair + n, c * C:(c + 1) * C],
                                   kx[rows, c, :], start=True, stop=True)
                mm.then_inc(s_done, 1)

            def swa_turn(p):
                pair, c, g = swa_pass(p)
                pe.wait_ge(s_normed, p + 1)
                if p:
                    pe.wait_ge(pv_evicted, p)
                for n in range(PAIR):
                    src = scores[:, p % 3, n, :]
                    if c:
                        pe.transpose(ps[:, 6, 2 * n * C:(2 * n + 1) * C], src[:, N_META:N_META + C], ident_s[:, :])
                    pe.transpose(ps[:, 6, (2 * n + 1) * C:(2 * n + 2) * C], src[:, N_META + C:SPAN], ident_s[:, :])
                    mm = pe.transpose(ps[0:N_META, 7, n * C:(n + 1) * C], src[:, 0:N_META], ident_s[:, :])
                mm.then_inc(p_turned, 1)

            def swa_values(p):
                pair, c, g = swa_pass(p)
                pe.wait_ge(p_taken, p + 1)
                cols = slice(64 * g, 64 * g + 64)
                dst = ps[64 * g:64 * g + 64, 7, PAIR * C:2 * PAIR * C]
                pe.matmul(dst, vs_tok[0:N_META, 0, cols], p_tm[:, :, :], start=True, stop=False)
                if c:
                    pe.matmul(dst, vs_tok[:, c, cols], p_t[:, :, 0, :], start=False, stop=False)
                pe.matmul(dst, vs_tok[:, c + 1, cols], p_t[:, :, 1, :], start=False, stop=True).then_inc(pv_done, 1)

            def gap_first(g):
                if g == 2 * 2:
                    pre_sum(N_PREM, L, 6)
                if g == 2 * 2 + 1:
                    spread(N_PREM, L, 6)
                p = g - GAP_SWA
                if 0 <= p - 3:
                    swa_values(p - 3)

            def gap(g):
                if g == GAP_Z:
                    gate_logits()
                if 0 <= g - GAP_LV <= len(LEVELS):
                    level_scores(g - GAP_LV)
                if g == GAP_TURN:
                    turn_early()
                p = g - GAP_SWA
                if 0 <= p - 2:
                    swa_turn(p - 2)
                if 0 <= p < PASSES:
                    swa_scores(p)

            ffn_up(U_UP1, 0, xa_hi, xa_lo, L, N_PRE1, 0)
            ffn_down(U_DOWN1, 0, 0, hid1_hi, hid1_lo, L)
            post_norm(N_POST1, L)

            lead_pair(U_IN, xb_hi, xb_lo, (in_bank(0), in_bank(1)), L, lambda k: pe.wait_ge(x_ready, KD + k + 1))
            for j in range(2, N_IN):
                if j == 2:
                    pe.wait_ge(r_ready, norm_copies(N_POST1))
                elif j < 5:
                    pe.wait_ge(proj_evicted, j - 2)
                else:
                    pe.wait_ge(proj_evicted, j - 1)
                products(U_IN, j, 0, xb_hi, xb_lo, 0, KD, in_bank(j), L, after={
                    1: lambda: gap_first(2 * j), 3: lambda: gap(2 * j),
                    5: lambda: gap_first(2 * j + 1), 7: lambda: gap(2 * j + 1)})

            pe.wait_ge(proj_evicted, N_IN)
            for b in range(NC):
                for n in range(4):
                    mm = pe.transpose(ps[:, b, n * P:(n + 1) * P], gv[:, n, N_META + b * C:N_META + (b + 1) * C],
                                      ident_s[:, :])
            mm.then_inc(v_turned, 1)
            gap_first(2 * N_IN)
            gap(2 * N_IN)
            pe.wait_ge(s_masked, PASSES)
            for n in range(4):
                mm = pe.transpose(ps[0:N_META, 4, n * P:(n + 1) * P], gv[:, n, 0:N_META], ident_s[:, :])
            mm.then_inc(vm_turned, 1)

            pe.wait_ge(v_act, 1)
            pe.wait_ge(v_dve, 1)
            pe.wait_ge(vm_act, 1)
            gap_first(2 * N_IN + 1)
            gap(2 * N_IN + 1)
            for t in range(2):
                for c in range(NC):
                    rows = N_META if c == 0 else C
                    for n in range(2):
                        head = 2 * t + n
                        mm = pe.matmul(ps[64 * n:64 * n + 64, t, c * P:(c + 1) * P],
                                       ktok[0:rows, c, head * 64:head * 64 + 64],
                                       vtok[0:rows, c, head * P:(head + 1) * P], start=True, stop=True)
            mm.then_inc(sums_done, 1)
            gap_first(2 * N_IN + 2)

            pe.wait_ge(q_in_ready, 1)
            for head in range(GLA_HEADS):
                rows = slice(64 * (head % 2), 64 * (head % 2) + 64)
                for c in range(NC):
                    cols = slice(c * C, (c + 1) * C)
                    pe.matmul(ps[:, 2 + head, cols], vtok[:, c + 1, head * P:(head + 1) * P], attn_heads[:, head, cols],
                              start=True, stop=False)
                    if head == 0 and c == 0:
                        pe.wait_ge(states_ready, 1)
                    mm = pe.matmul(ps[:, 2 + head, cols], state[rows, head // 2, c, :], q_in[rows, head // 2, cols],
                                   start=False, stop=True)
                mm.then_inc(og_done, 1)

            pe.wait_ge(pv_evicted, PASSES)
            block_sums(N_SWA, [swa_sq[:, n, :] for n in range(4)], SEQ, 6)
            for head in range(GLA_HEADS):
                pe.wait_ge(og_squared, head + 1)
                block_sums(N_GLA, [gla_sq[:, head, :]], SEQ, 7, rows=GLA_HEADS * NC, row0=head * NC, start=head == 0,
                           stop=head == GLA_HEADS - 1)
            spread(N_SWA, SEQ, 6)

            def cat_arrived(k):
                if k == 0:
                    pe.wait_ge(og_taken, GLA_HEADS)
                if k == 4:
                    spread(N_GLA, SEQ, 1, rows=GLA_HEADS * NC)
                pe.wait_ge(cat_ready, k + 1)

            def out_tile(t, n):
                pe.wait_ge(y_evicted, KD + t - 1)
                pe.wait_ge(lo_split, U_OUT + t + 1)
                for k in range(KD):
                    mm = k_tile((U_OUT + n) % OPS, k, cat_hi, cat_lo, k, 2 * n, SEQ, k == 0, k == KD - 1)
                mm.then_inc(unit_used, 1)

            lead_pair(U_OUT, cat_hi, cat_lo, (0, 2), SEQ, cat_arrived)
            with pe.Fori(1, KD // 2) as i:
                out_tile(2 * i, 0)
                out_tile(2 * i + 1, 1)
            post_norm(N_POSTM, SEQ)

            ffn_up(U_UP2, KF, xc_hi, xc_lo, SEQ, N_PRE2, 2 * KD)
            ffn_down(U_DOWN2, 2 * KD, KF, hid2_hi, hid2_lo, SEQ)
            post_norm(N_POST2, SEQ)

        @block.scalar
        def _(act):
            def split_hi(base, j, width, i=0):
                u, raw_slot, turn, slot = unit(base, j, i)
                if base + j >= OPS:
                    act.wait_ge(unit_used, u - OPS + 1)
                act.wait_ge(raw_landed[raw_slot], 16 * (turn + 1))
                act.activation(w_hi[:, slot, 0:width], raw[:, raw_slot, 0:width], ACT.Copy).then_inc(hi_split, 1)

            def root(norm, w, bank, n_feat, rows=BLOCKS, half=False):
                act.wait_ge(norm_summed, norm + 1)
                if norm >= 2:
                    act.wait_ge(norm_spread, norm - 1)
                col = V_EPS + half
                act.activation(stat[0:rows, norm % 2, 0:w], ps[0:rows, bank, 0:w], ACT.Sqrt,
                               bias=vec[0:rows, col:col + 1], scale=(4.0 if half else 1.0) / n_feat).then_inc(rms_ready, 1)

            def preload_sqrt():
                act.activation(small_root[:, :], vec[:, V_EPS:V_EPS + 1], ACT.Sqrt).then_inc(act_step, 1)

            def square(src, norm, k, n_tok, psum=False):
                if k == 0 and norm:
                    act.wait_ge(norm_summed, norm)
                if k >= 3:
                    adder, turn = (y_summed, POST[norm]) if psum else (summed, PRE[norm])
                    act.wait_ge(adder, (KD - 1) * turn + k - 2)
                dst = sumsq if k == 0 else sq[:, k % 2, :]
                act.activation(row(dst, n_tok) if psum else dst[:, 0:n_tok], src, ACT.Square)\
                   .then_inc(y_squared if psum else squared, 1)

            def operand_tile(k, norm, n_tok, xh, v0):
                src = h[:, k, tokens(n_tok)]
                act.activation(xh[:, k, :], src, ACT.Copy, scale=vec[:, v0 + k:v0 + k + 1]).then_inc(x_hi, 1)
                square(src, norm, k, n_tok)

            def operand(norm, n_tok, xh, v0, turn):
                for k in range(KD):
                    before = pool_tiles_before(k)
                    if k in POOL_TILES:
                        act.wait_ge(h_pool, len(POOL_TILES) * turn + before + 1)
                    else:
                        act.wait_ge(h_updated, (KD - len(POOL_TILES)) * turn + k - before + 1)
                    operand_tile(k, norm, n_tok, xh, v0)

            def hidden_tile(tile0, t, hi, n_tok):
                act.wait_ge(gate_scaled, tile0 + t + 1)
                act.activation(gate[:, 0:n_tok], gate[:, 0:n_tok], ACT.Silu).then_inc(silu_done, 1)
                act.wait_ge(hid_written, tile0 + t + 1)
                act.activation(hi[:, t, :], up[:, 0:n_tok], ACT.Copy).then_inc(hid_hi, 1)

            def ffn_up(base, tile0, hi, n_tok, norm):
                split_hi(base, 2, W_UP)
                if n_tok == L:
                    root(norm, n_tok // BLOCKS, 6, D_MODEL)
                    split_hi(base, 3, W_UP)
                    hidden_tile(tile0, 0, hi, n_tok)
                    split_hi(base, 4, W_UP)
                else:
                    split_hi(base, 3, W_UP)
                    root(norm, n_tok // BLOCKS, 1, D_MODEL)
                    split_hi(base, 4, W_UP)
                    hidden_tile(tile0, 0, hi, n_tok)
                split_hi(base, 5, W_UP)
                hidden_tile(tile0, 1, hi, n_tok)
                with act.Fori(1, KF // 2 - 1) as i:
                    for n in range(2):
                        split_hi(base, 2 * n + 2, W_UP, i)
                        split_hi(base, 2 * n + 3, W_UP, i)
                        hidden_tile(tile0, 2 * i + n, hi, n_tok)
                split_hi(base, UP_UNITS - 2, W_UP)
                split_hi(base, UP_UNITS - 1, W_UP)
                hidden_tile(tile0, KF - 2, hi, n_tok)
                split_hi(base, UP_UNITS, W_DOWN)
                split_hi(base, UP_UNITS + 1, W_DOWN)
                hidden_tile(tile0, KF - 1, hi, n_tok)

            def result_tile(d, y, v0, norm, used, n_tok):
                act.wait_ge(unit_used, used)
                src = in_psum(2 * (d % 2), n_tok)
                square(src, norm, d, n_tok, psum=True)
                act.activation(row(y[:, d, :], n_tok), src, ACT.Copy, scale=vec[:, v0 + d:v0 + d + 1]).then_inc(y_evicted, 1)

            def ffn_down(base, y, v0, norm, n_tok, next_width):
                preload_sqrt()
                for d in range(KD):
                    for n in range(2):
                        if d < KD - 1:
                            split_hi(base, 2 * d + 2 + n, W_DOWN)
                        elif next_width:
                            split_hi(base, 2 * d + 2 + n, next_width)
                    result_tile(d, y, v0, norm, base + 2 * d + 2, n_tok)
                root(norm, n_tok // BLOCKS, 4, D_MODEL, half=True)

            def gate_logs():
                act.wait_ge(z_done, 1)
                for t in range(2):
                    act.activation(row(z_log_t[:, t, :], L), in_psum(4 + 2 * t, L), ACT.Abs,
                                   bias=vec[:, V_BA + t:V_BA + t + 1]).then_inc(z_log, 1)

            def gate_logs_rest():
                act.wait_ge(z_log, 2)
                act.activation(z_log_t, z_log_t, ACT.Exp, scale=-1.0).then_inc(z_log, 1)
                act.wait_ge(z_log, 3)
                act.activation(z_log_t, z_log_t, ACT.Ln, bias=1.0).then_inc(z_log, 1)

            def chunk_decays():
                act.wait_ge(b_ready, 1)
                act.activation(q_in[:, :, :], b_real[:, :, :], ACT.Exp, scale=1 / GLA_TAU).then_inc(q_exp, 1)
                act.activation(dec[:, :, :], b_real[:, :, C - 1:SEQ:C], ACT.Exp, scale=1 / GLA_TAU).then_inc(q_exp, 1)
                act.wait_ge(k_diff, 1)
                act.activation(k_out[:, :, :], k_out[:, :, :], ACT.Exp, scale=1 / GLA_TAU).then_inc(k_exp, 1)

            def level_decays(lv):
                m = LEVELS[lv]
                act.wait_ge(lv_diff, lv + 1)
                d = decay[:, :, :].rearrange("p t (n x) -> p (t n) x", x=2 * m)
                act.activation(d[:, :, 0:m], d[:, :, 0:m], ACT.Exp, scale=-1 / GLA_TAU).then_inc(act_step, 1)
                act.activation(d[:, :, m:2 * m], d[:, :, m:2 * m], ACT.Exp, scale=1 / GLA_TAU).then_inc(lv_exp, 1)

            def take_turned():
                act.wait_ge(turned, 1)
                act.activation(vs_tok[:, 1:NC + 1, :], ps[:, 4, :].rearrange("p (b n) -> p b n", b=NC), ACT.Copy)\
                   .then_inc(act_step, 1)
                act.activation(vs_tok[0:N_META, 0, :], ps[0:N_META, 5, 0:P], ACT.Copy).then_inc(act_step, 1)
                act.activation(ktok[:, 1:NC, :], ps[:, 6:8, :].rearrange("p b (c n) -> p (b c) n", c=2)[:, 0:NC - 1, :],
                               ACT.Copy).then_inc(act_step, 1)
                act.activation(ktok[0:N_META, 0, :], ps[0:N_META, 7, 2 * P:4 * P], ACT.Copy).then_inc(turned_out, 1)

            def swa_out(p):
                pair, c, g = swa_pass(p)
                act.wait_ge(pv_done, p + 1)
                rows, cols = slice(64 * g, 64 * g + 64), slice(c * C, (c + 1) * C)
                src = ps[rows, 7, PAIR * C:2 * PAIR * C].rearrange("p (n t) -> p n t", n=PAIR)
                heads = slice(PAIR * pair, PAIR * pair + PAIR)
                act.activation(swa_sq[rows, heads, cols], src, ACT.Square).then_inc(act_step, 1)
                act.activation(o_swa[rows, heads, cols], src, ACT.Copy).then_inc(pv_evicted, 1)

            def swa_evict(p):
                act.wait_ge(p_turned, p + 1)
                src = ps[:, 6, :].rearrange("p (n b t) -> p n b t", n=PAIR, b=2)
                if swa_pass(p)[1]:
                    act.activation(p_t[:, :, :, :], src, ACT.Copy).then_inc(act_step, 1)
                else:
                    act.activation(p_t[:, :, 1, :], src[:, :, 1, :], ACT.Copy).then_inc(act_step, 1)
                act.activation(p_tm[:, :, :], ps[0:N_META, 7, 0:PAIR * C].rearrange("p (n t) -> p n t", n=PAIR),
                               ACT.Copy).then_inc(p_taken, 1)

            def swa_exp(p):
                act.wait_ge(s_max, p + 1)
                for n in range(PAIR):
                    act.activation(scores[:, p % 3, n, :], scores[:, p % 3, n, :], ACT.Exp,
                                   bias=small[:, p % 3, 0, n:n + 1], accum_out=small[:, p % 3, 1, n:n + 1])\
                       .then_inc(act_step, 1)
                act.activation(small[:, p % 3, 2, :], small[:, p % 3, 2, :], ACT.Exp).then_inc(s_exp, 1)

            def gap(g):
                j, p = g // 2, g - GAP_SWA
                if 0 <= p - 3:
                    swa_out(p - 3)
                if 0 <= p - 1 < PASSES:
                    swa_exp(p - 1)
                if g % 2 and j < N_IN:
                    split_hi(U_IN, j + 2, W_UP)
                if g == 2 * 2:
                    root(N_PREM, L // BLOCKS, 6, D_MODEL)
                if g == GAP_Z:
                    gate_logs()
                if g == GAP_Z + 1:
                    gate_logs_rest()
                if g == GAP_DECAY:
                    chunk_decays()
                    level_decays(0)
                if g == GAP_DECAY + 2:
                    level_decays(1)
                if 0 <= g - GAP_LV < len(LEVELS) - 2:
                    level_decays(g - GAP_LV + 2)
                if g == GAP_TURN:
                    take_turned()
                if 0 <= p - 2 < PASSES:
                    swa_evict(p - 2)

            act.wait_ge(vec_landed, 16)
            for k in range(KD):
                if k < 2:
                    split_hi(U_UP1, k, W_UP)
                act.wait_ge(x_landed[k], 16)
                operand_tile(k, N_PRE1, L, xa_hi, V_PRE1)
            ffn_up(U_UP1, 0, hid1_hi, L, N_PRE1)
            ffn_down(U_DOWN1, y1, V_POST1, N_POST1, L, W_UP)
            operand(N_PREM, L, xb_hi, V_PREM, 0)

            split_hi(U_IN, 2, W_UP)
            split_hi(U_IN, 3, W_UP)
            for g in range(2 * 2, 2 * N_IN):
                gap(g)
            act.wait_ge(v_turned, 1)
            act.activation(vtok[:, 1:3, :], ps[:, 0:2, :], ACT.Copy).then_inc(v_act, 1)
            gap(2 * N_IN)
            act.wait_ge(vm_turned, 1)
            act.activation(vtok[0:N_META, 0, :], ps[0:N_META, 4, :], ACT.Copy).then_inc(vm_act, 1)
            gap(2 * N_IN + 1)
            act.activation(gg, gg, ACT.Silu).then_inc(gg_silu, 1)
            gap(2 * N_IN + 2)
            for head in range(GLA_HEADS):
                act.wait_ge(og_done, head + 1)
                act.activation(gla_sq[:, head, :], ps[:, 2 + head, :], ACT.Square).then_inc(og_squared, 1)
            root(N_SWA, C, 6, SWA_HEADS * HEAD_DIM)
            root(N_GLA, C, 7, GLA_DV, rows=GLA_HEADS * NC)
            for k in range(KD):
                act.wait_ge(cat_raw, k + 1)
                src = o_swa[:, k, :] if k < 4 else o_gla[:, k - 4, :]
                act.activation(cat_hi[:, k, :], src, ACT.Copy).then_inc(cat_hi_done, 1)
            for d in range(KD):
                split_hi(U_OUT, d + 2, W_UP)
                result_tile(d, y2, V_POSTM, N_POSTM, U_OUT + d + 1, SEQ)
            root(N_POSTM, C, 4, D_MODEL)
            operand(N_PRE2, SEQ, xc_hi, V_PRE2, 1)

            ffn_up(U_UP2, KF, hid2_hi, SEQ, N_PRE2)
            ffn_down(U_DOWN2, y3, V_POST2, N_POST2, SEQ, 0)

        @block.vector
        def _(dve):
            steps = [0]

            def link(ins):
                steps[0] += 1
                ins.then_inc(dve_step, 1)
                dve.wait_ge(dve_step, steps[0])

            def split_lo(base, j, width, i=0):
                u, raw_slot, _, slot = unit(base, j, i)
                dve.wait_ge(hi_split, u + 1)
                dve.tensor_tensor(w_lo[:, slot, 0:width], raw[:, raw_slot, 0:width], f32(w_hi[:, slot, 0:width]),
                                  ALU.subtract).then_inc(lo_split, 1)

            def reciprocal(norm, w, rows=BLOCKS):
                dve.wait_ge(rms_ready, norm + 1)
                dve.reciprocal(stat[0:rows, norm % 2, 0:w], stat[0:rows, norm % 2, 0:w]).then_inc(norm_ready, 1)

            def take_r(norm, n_tok, bank):
                dve.wait_ge(norm_spread, norm + 1)
                dve.tensor_copy(row(rnorm, n_tok), in_psum(bank, n_tok)).then_inc(r_ready, 1)
                dve.wait_ge(r_ready, norm_copies(norm))

            def low_part(n_tok, xh, xl, v0, k, turn):
                dve.wait_ge(x_hi, KD * turn + k + 1)
                dve.scalar_tensor_tensor(out=xl[:, k, :], in0=h[:, k, tokens(n_tok)], scalar=vec[:, v0 + k:v0 + k + 1],
                                         in1=f32(xh[:, k, :]), op0=ALU.mult, op1=ALU.subtract).then_inc(x_ready, 1)

            def add_residual(y, k, n_tok):
                link(dve.tensor_tensor(y[:, k, :], y[:, k, :], rnorm[:, 0:n_tok], ALU.mult))
                return dve.tensor_tensor(h[:, k, tokens(n_tok)], h[:, k, tokens(n_tok)], y[:, k, :], ALU.add)

            def residual(post, n_tok, y, xh, xl, v0, turn):
                reciprocal(post, n_tok // BLOCKS)
                take_r(post, n_tok, 4)
                for k in range(KD):
                    if k not in POOL_TILES:
                        add_residual(y, k, n_tok).then_inc(h_updated, 1)
                    if k:
                        low_part(n_tok, xh, xl, v0, k - 1, turn)
                low_part(n_tok, xh, xl, v0, KD - 1, turn)

            def add_squares(norm, d, n_tok):
                if d:
                    dve.wait_ge(y_squared, KD * POST[norm] + d + 1)
                    n = (KD - 1) * POST[norm] + d
                    if d > 1:
                        dve.wait_ge(y_summed, n - 1)
                    dve.tensor_tensor(sumsq[:, 0:n_tok], sumsq[:, 0:n_tok], sq[:, d % 2, 0:n_tok], ALU.add)\
                       .then_inc(y_summed, 1)

            def hidden_tile(base, tile0, t, q, hi, lo, n_tok):
                dve.wait_ge(unit_used, base + 2 * t + 2)
                dve.tensor_tensor(row(gate, n_tok), in_psum(4 * q, n_tok), row(rnorm, n_tok), ALU.mult).then_inc(gate_scaled, 1)
                dve.tensor_tensor(row(up, n_tok), in_psum(4 * q + 2, n_tok), row(rnorm, n_tok), ALU.mult).then_inc(gu_evicted, 1)
                dve.wait_ge(gu_evicted, tile0 + t + 1)
                dve.wait_ge(silu_done, tile0 + t + 1)
                dve.tensor_tensor(up[:, 0:n_tok], up[:, 0:n_tok], gate[:, 0:n_tok], ALU.mult).then_inc(hid_written, 1)
                dve.wait_ge(hid_hi, tile0 + t + 1)
                dve.tensor_tensor(lo[:, t, :], up[:, 0:n_tok], f32(hi[:, t, :]), ALU.subtract).then_inc(hid_ready, 1)
                dve.wait_ge(hid_ready, tile0 + t + 1)

            def ffn_up(base, tile0, hi, lo, n_tok, norm):
                split_lo(base, 2, W_UP)
                if n_tok == L:
                    reciprocal(norm, n_tok // BLOCKS)
                    split_lo(base, 3, W_UP)
                    take_r(norm, n_tok, 6)
                    hidden_tile(base, tile0, 0, 0, hi, lo, n_tok)
                    split_lo(base, 4, W_UP)
                else:
                    split_lo(base, 3, W_UP)
                    reciprocal(norm, n_tok // BLOCKS)
                    split_lo(base, 4, W_UP)
                    take_r(norm, n_tok, 3)
                    hidden_tile(base, tile0, 0, 0, hi, lo, n_tok)
                split_lo(base, 5, W_UP)
                hidden_tile(base, tile0, 1, 1, hi, lo, n_tok)
                with dve.Fori(1, KF // 2 - 1) as i:
                    for n in range(2):
                        split_lo(base, 2 * n + 2, W_UP, i)
                        split_lo(base, 2 * n + 3, W_UP, i)
                        hidden_tile(base, tile0, 2 * i + n, n, hi, lo, n_tok)
                split_lo(base, UP_UNITS - 2, W_UP)
                split_lo(base, UP_UNITS - 1, W_UP)
                hidden_tile(base, tile0, KF - 2, 0, hi, lo, n_tok)
                split_lo(base, UP_UNITS, W_DOWN)
                split_lo(base, UP_UNITS + 1, W_DOWN)
                hidden_tile(base, tile0, KF - 1, 1, hi, lo, n_tok)

            def ffn_down(base, norm, n_tok, next_width):
                for d in range(KD):
                    for n in range(2):
                        if d < KD - 1:
                            split_lo(base, 2 * d + 2 + n, W_DOWN)
                        elif next_width:
                            split_lo(base, 2 * d + 2 + n, next_width)
                    add_squares(norm, d, n_tok)

            def in_evict(j):
                dve.wait_ge(unit_used, U_IN + j + 1)
                src, dst = in_psum(in_bank(j), L), in_dst[j]
                if j == T_SK or T_SQ <= j < T_GV:
                    if j == T_SK:
                        dve.wait_ge(tables_scaled, 2)
                    link(dve.tensor_tensor(row(gate, L), src, row(sin_s, L), ALU.mult))
                    link(dve.stream_shuffle(up[:, :], gate[:, :], [(n + 16) % 32 for n in range(32)]))
                    link(dve.tensor_tensor(row(dst, L), src, row(cos_s, L), ALU.mult))
                    dve.tensor_tensor(dst, dst, up[:, :], ALU.add).then_inc(proj_evicted, 1)
                    dve.wait_ge(proj_evicted, j + 1)
                else:
                    dve.tensor_tensor(row(dst, L), src, row(rnorm, L), ALU.mult).then_inc(proj_evicted, 1)

            def z_minimum():
                dve.wait_ge(z_log, 2)
                for t in range(2):
                    dve.tensor_scalar(row(z_min[:, t, :], L), in_psum(4 + 2 * t, L), vec[:, V_BA + t:V_BA + t + 1], 0.0,
                                      ALU.add, ALU.min).then_inc(z_read, 1)
                dve.wait_ge(z_read, 2)

            def sum_log_a():
                dve.wait_ge(z_log, 4)
                link(dve.tensor_tensor(z_min, z_min, z_log_t, ALU.subtract))
                for t in range(2):
                    link(dve.tensor_tensor_scan(b_meta[:, t, :], carry[:, 1:1 + N_META], z_min[:, t, 0:N_META], 0.0,
                                                ALU.mult, ALU.add))
                    ins = dve.tensor_tensor_scan(b_real[:, t, :], carry[:, :], z_min[:, t, N_META:L], 0.0,
                                                 ALU.mult, ALU.add)
                    if t == 0:
                        link(ins)
                ins.then_inc(b_ready, 1)
                dve.wait_ge(b_ready, 1)

            def key_differences():
                for t in range(2):
                    bt = b_real[:, t, :].rearrange("p (c n) -> p c n", n=C)
                    link(dve.tensor_tensor(k_out[:, t, N_META:L].rearrange("p (c n) -> p c n", n=C),
                                           bt[:, :, C - 1:C].broadcast_to([P, NC, C]), bt, ALU.subtract))
                dve.tensor_tensor(k_out[:, :, 0:N_META], b_meta[:, :, N_META - 1:N_META].broadcast_to([P, 2, N_META]),
                                  b_meta[:, :, :], ALU.subtract).then_inc(k_diff, 1)

            def level_differences(lv):
                m = LEVELS[lv]
                if lv:
                    dve.wait_ge(lv_k_ready, lv)
                    dve.wait_ge(lv_q_ready, lv)
                d = decay[:, :, :].rearrange("p t (n x) -> p (t n) x", x=2 * m)
                b = b_real[:, :, :].rearrange("p t (n x) -> p (t n) x", x=2 * m)
                dve.tensor_tensor(d, b, b[:, :, m - 1:m].broadcast_to([P, SEQ // m, 2 * m]), ALU.subtract)\
                   .then_inc(lv_diff, 1)

            def level_queries(lv):
                m = LEVELS[lv]
                dve.wait_ge(lv_exp, lv + 1)
                if lv < 2:
                    dve.wait_ge(lv_zeroed, 2)
                else:
                    dve.wait_ge(lv_scored, lv - 1)
                half = [ap.rearrange("p t (n x) -> p t n x", x=2 * m)[:, :, :, m:2 * m]
                        for ap in (lv_q[:, lv % 2, :, :], gq, decay[:, :, :])]
                dve.tensor_tensor(half[0], half[1], half[2], ALU.mult).then_inc(lv_q_ready, 1)

            def level_take(lv):
                dve.wait_ge(lv_scored, lv + 1)
                if lv == 0:
                    dve.wait_ge(attn_zeroed, 1)
                m = LEVELS[lv] if lv < len(LEVELS) else 0
                size = 2 * m or C
                a, n = GLA_HEADS * NC, C // size
                dst, src = [ap.rearrange("p (a n x) -> p a n x", a=a, x=size)[:, :, :, m:size]
                            for ap in (attn[:, :], ps[:, 4:8, :].rearrange("p h n -> p (h n)"))]
                mask = lmask[:, lv:lv + 1, :].rearrange("p a (n x) -> p a n x", x=size)[:, :, :, m:size]
                dve.copy_predicated(dst, mask.broadcast_to([P, a, n, size - m]), src).then_inc(lv_taken, 1)
                dve.wait_ge(lv_taken, lv + 1)

            def swa_mask(p):
                pair, c, g = swa_pass(p)
                sc = scores[:, p % 3, :, :]
                neg_max = small[:, p % 3, 0, :]
                sink = vec[:, V_SINK + GROUP * g + PAIR * pair:V_SINK + GROUP * g + PAIR * pair + PAIR]
                dve.wait_ge(s_done, p + 1)
                if p >= 3:
                    dve.wait_ge(p_turned, p - 2)
                which = min(c, 1)
                dve.scalar_tensor_tensor(out=sc, in0=ps[:, 4:4 + PAIR, 0:SPAN], scalar=HEAD_DIM ** -0.5,
                                         in1=band_s[:, which:which + 1, :].broadcast_to([P, PAIR, SPAN]),
                                         op0=ALU.mult, op1=ALU.add).then_inc(s_masked, 1)
                dve.wait_ge(s_masked, p + 1)
                link(dve.tensor_reduce(neg_max, sc, AX_X, ALU.max))
                link(dve.tensor_tensor(neg_max, neg_max, sink, ALU.max))
                link(dve.tensor_scalar(neg_max, neg_max, -1.0, None, ALU.mult))
                dve.tensor_tensor(small[:, p % 3, 2, :], sink, neg_max, ALU.add).then_inc(s_max, 1)

            def swa_norm(p):
                rowsum, sink_exp = small[:, p % 3, 1, :], small[:, p % 3, 2, :]
                dve.wait_ge(s_exp, p + 1)
                link(dve.tensor_tensor(rowsum, rowsum, sink_exp, ALU.add))
                link(dve.reciprocal(rowsum, rowsum))
                for n in range(PAIR):
                    ins = dve.tensor_scalar(scores[:, p % 3, n, :], scores[:, p % 3, n, :], rowsum[:, n:n + 1], None, ALU.mult)
                    if n < PAIR - 1:
                        link(ins)
                ins.then_inc(s_normed, 1)

            def gap(g):
                j, p = g // 2, g - GAP_SWA
                if g == 2 * 2:
                    reciprocal(N_PREM, L // BLOCKS)
                    take_r(N_PREM, L, 6)
                    in_evict(0)
                    in_evict(1)
                if g % 2 and j < N_IN:
                    in_evict(j)
                if 0 <= p - 1 < PASSES:
                    swa_norm(p - 1)
                if g % 2 and j < N_IN:
                    split_lo(U_IN, j + 2, W_UP)
                if g == GAP_Z:
                    z_minimum()
                if g == GAP_B:
                    sum_log_a()
                if g == GAP_DECAY:
                    key_differences()
                    level_differences(0)
                if g == GAP_DECAY + 1:
                    dve.wait_ge(proj_evicted, T_GQ + 2)
                    dve.tensor_scalar(gq, gq, GLA_DK ** -0.5, None, ALU.mult).then_inc(q_scaled, 1)
                    dve.wait_ge(q_scaled, 1)
                    level_queries(0)
                if g == GAP_DECAY + 2:
                    level_differences(1)
                    level_queries(1)
                if 0 <= g - GAP_LV <= len(LEVELS):
                    lv = g - GAP_LV
                    if lv + 2 < len(LEVELS):
                        level_differences(lv + 2)
                    level_take(lv)
                    if lv + 2 < len(LEVELS):
                        level_queries(lv + 2)
                if 0 <= p < PASSES:
                    swa_mask(p)

            link(dve.memset(carry[:, :], 1.0))
            link(dve.memset(carry[:, 0:SEQ:C], 0.0))
            dve.wait_ge(vec_landed, 16)
            for k in range(KD):
                if k < 2:
                    split_lo(U_UP1, k, W_UP)
                low_part(L, xa_hi, xa_lo, V_PRE1, k, 0)
            ffn_up(U_UP1, 0, hid1_hi, hid1_lo, L, N_PRE1)
            ffn_down(U_DOWN1, N_POST1, L, W_UP)
            residual(N_POST1, L, y1, xb_hi, xb_lo, V_PREM, 1)

            split_lo(U_IN, 2, W_UP)
            split_lo(U_IN, 3, W_UP)
            for g in range(2 * 2, 2 * N_IN):
                gap(g)
            dve.wait_ge(v_turned, 1)
            dve.tensor_copy(vtok[:, 3:5, :], ps[:, 2:4, :]).then_inc(v_dve, 1)
            gap(2 * N_IN)
            gap(2 * N_IN + 1)

            dve.wait_ge(sums_done, 1)
            link(dve.tensor_copy(state[:, :, 0, :], ps[:, 0:2, 0:P]))
            for c in range(1, NC):
                for t in range(2):
                    ins = dve.scalar_tensor_tensor(out=state[:, t, c, :], in0=state[:, t, c - 1, :],
                                                   scalar=dec[:, t, c - 1:c], in1=ps[:, t, c * P:(c + 1) * P],
                                                   op0=ALU.mult, op1=ALU.add)
                    if (c, t) == (NC - 1, 1):
                        ins.then_inc(states_ready, 1)
                    else:
                        link(ins)
            dve.wait_ge(gg_silu, 1)
            link(dve.tensor_scalar(gg, gg, vec[:, V_GLA:V_GLA + 1], None, ALU.mult))
            for head in range(GLA_HEADS):
                dve.wait_ge(og_squared, head + 1)
                dve.tensor_tensor(o_gla[:, head, :], ps[:, 2 + head, :], gg[:, head, :], ALU.mult).then_inc(og_taken, 1)
            reciprocal(N_SWA, C)
            dve.wait_ge(og_taken, GLA_HEADS)
            dve.wait_ge(norm_spread, N_SWA + 1)
            reciprocal(N_GLA, C, rows=GLA_HEADS * NC)
            for n in range(4):
                dve.scalar_tensor_tensor(out=o_swa[:, n, :], in0=o_swa[:, n, :], scalar=vec[:, V_SWA + n:V_SWA + n + 1],
                                         in1=ps[:, 6, :], op0=ALU.mult, op1=ALU.mult).then_inc(cat_raw, 1)

            def cat_low(k):
                src = o_swa[:, k, :] if k < 4 else o_gla[:, k - 4, :]
                dve.wait_ge(cat_hi_done, k + 1)
                dve.tensor_tensor(cat_lo[:, k, :], src, f32(cat_hi[:, k, :]), ALU.subtract).then_inc(cat_ready, 1)

            for k in range(4):
                cat_low(k)
            dve.wait_ge(norm_spread, N_GLA + 1)
            for head in range(GLA_HEADS):
                dve.tensor_tensor(o_gla[:, head, :], o_gla[:, head, :], ps[:, 1 + 2 * head, :], ALU.mult).then_inc(cat_raw, 1)
                if head:
                    cat_low(4 + head - 1)
            cat_low(KD - 1)
            for d in range(KD):
                split_lo(U_OUT, d + 2, W_UP)
                add_squares(N_POSTM, d, SEQ)
            residual(N_POSTM, SEQ, y2, xc_hi, xc_lo, V_PRE2, 2)

            ffn_up(U_UP2, KF, hid2_hi, hid2_lo, SEQ, N_PRE2)
            ffn_down(U_DOWN2, N_POST2, SEQ, 0)
            reciprocal(N_POST2, C)
            take_r(N_POST2, SEQ, 4)
            for k in range(KD):
                if k not in POOL_TILES:
                    add_residual(y3, k, SEQ).then_inc(out_dve, 1)

        @block.gpsimd
        def _(pool):
            def add_squares(norm, n_tok):
                for k in range(1, KD):
                    pool.wait_ge(squared, KD * PRE[norm] + k + 1)
                    n = (KD - 1) * PRE[norm] + k
                    if k > 1:
                        pool.wait_ge(summed, n - 1)
                    pool.tensor_tensor(sumsq[:, 0:n_tok], sumsq[:, 0:n_tok], sq[:, k % 2, 0:n_tok], ALU.add)\
                        .then_inc(summed, 1)

            def residual(norm, y, n_tok, done):
                pool.wait_ge(r_ready, norm_copies(norm))
                for n, k in enumerate(POOL_TILES):
                    pool.tensor_tensor(y[:, k, :], y[:, k, :], rnorm[:, 0:n_tok], ALU.mult).then_inc(y_scaled, 1)
                    pool.wait_ge(y_scaled, len(POOL_TILES) * POST[norm] + n + 1)
                    cols = tokens(n_tok)
                    pool.tensor_tensor(h[:, k, cols], h[:, k, cols], y[:, k, :], ALU.add).then_inc(done, 1)

            def level_keys(lv):
                m = LEVELS[lv]
                pool.wait_ge(lv_exp, lv + 1)
                if lv < 2:
                    pool.wait_ge(lv_zeroed, 2)
                else:
                    pool.wait_ge(lv_scored, lv - 1)
                half = [ap.rearrange("p t (n x) -> p t n x", x=2 * m)[:, :, :, 0:m]
                        for ap in (lv_k[:, lv % 2, :, :], gk[:, :, N_META:L], decay[:, :, :])]
                pool.tensor_tensor(half[0], half[1], half[2], ALU.mult).then_inc(lv_k_ready, 1)

            add_squares(N_PRE1, L)
            residual(N_POST1, y1, L, h_pool)
            add_squares(N_PREM, L)
            pool.memset(lv_k[:, :, :, :], 0.0).then_inc(lv_zeroed, 1)
            pool.memset(lv_q[:, :, :, :], 0.0).then_inc(lv_zeroed, 1)
            pool.memset(kx[:, 0, N_META:N_META + C], 0.0).then_inc(kx_ready, 1)
            pool.wait_ge(table_landed, 16 * 5)
            pool.wait_ge(r_ready, norm_copies(N_PREM))
            for table in (cos_s, sin_s):
                pool.tensor_tensor(table[:, :], table[:, :], rnorm[:, :], ALU.mult).then_inc(tables_scaled, 1)
            pool.wait_ge(b_ready, 1)
            pool.memset(attn[:, :], 0.0).then_inc(attn_zeroed, 1)
            level_keys(0)
            level_keys(1)
            pool.wait_ge(proj_evicted, T_SK + 1)
            pool.wait_ge(kx_ready, 1)
            for c in range(NC):
                pool.tensor_copy(kx[:, c, 0:N_META], sk[:, 0:N_META]).then_inc(kx_ready, 1)
                before, col = (c - 1, N_META) if c else (0, N_META + C)
                pool.tensor_copy(kx[:, c, col:SPAN], sk[:, N_META + before * C:N_META + (c + 1) * C]).then_inc(kx_ready, 1)
                if c == 1:
                    level_keys(2)
            pool.wait_ge(k_exp, 1)
            pool.tensor_tensor(k_out[:, :, :], k_out[:, :, :], gk, ALU.mult).then_inc(k_out_ready, 1)
            level_keys(3)
            pool.wait_ge(q_exp, 2)
            pool.wait_ge(q_scaled, 1)
            pool.tensor_tensor(q_in[:, :, :], q_in[:, :, :], gq, ALU.mult).then_inc(q_in_ready, 1)
            for lv in range(4, len(LEVELS)):
                level_keys(lv)
            residual(N_POSTM, y2, SEQ, h_pool)
            add_squares(N_PRE2, SEQ)
            residual(N_POST2, y3, SEQ, out_pool)


def rope_tables():
    half = HEAD_DIM // 2
    inv_freq = (1.0 / (np.float32(ROPE_THETA) ** (np.arange(0, HEAD_DIM, 2, dtype=np.float32) / np.float32(HEAD_DIM))))
    ang = inv_freq.astype(np.float32)[:, None] * np.arange(L, dtype=np.float32)[None, :]
    cos, sin = np.cos(ang), np.sin(ang)
    quarters = half // 2
    cos = np.concatenate([cos[:quarters]] * 2 + [cos[quarters:]] * 2)
    sin = np.concatenate([sin[:quarters], -sin[:quarters], sin[quarters:], -sin[quarters:]])
    return np.concatenate([cos] * 2).astype(np.float32), np.concatenate([sin] * 2).astype(np.float32)


def masks():
    t, s = np.arange(C)[:, None], np.arange(C)[None, :]
    meta = np.zeros((C, N_META), np.float32)
    own = np.where(s <= t, 0.0, NEG).astype(np.float32)
    before = np.where(s > t, 0.0, NEG).astype(np.float32)
    none = np.full((C, C), NEG, np.float32)
    band = np.stack([np.concatenate([meta, none, own], 1), np.concatenate([meta, before, own], 1)], 1)
    j, i = t, s
    levels = [(j // (2 * m) == i // (2 * m)) & (j % (2 * m) < m) & (i % (2 * m) >= m) for m in LEVELS]
    levels.append(j == i)
    return band, np.stack(levels, 1).astype(np.uint32)


def kernel(**inputs):
    import concourse.bacc as bacc
    from concourse.bass_utils import run_bass_kernel_spmd

    a = {name: np.asarray(value) for name, value in inputs.items()}

    def tiles(w, k_tiles):
        return w.reshape(k_tiles, P, w.shape[1] // P, P).transpose(2, 1, 0, 3)

    def up_units(gate, up):
        both = np.stack([tiles(gate, KD), tiles(up, KD)], 1)
        return np.ascontiguousarray(both.reshape(UP_UNITS, P, W_UP))

    def down_units(w):
        t = tiles(w, KF).reshape(KD, P, 2, KH, P).transpose(0, 2, 1, 3, 4)
        return np.ascontiguousarray(t.reshape(DOWN_UNITS, P, W_DOWN))

    def columns(v):
        return v.reshape(-1, P).T

    def heads_side_by_side(w, axis):
        shape = w.shape
        w = np.moveaxis(w, axis, 0).reshape(KV_HEADS, GROUP, HEAD_DIM, -1).transpose(1, 0, 2, 3)
        return np.moveaxis(w.reshape((SWA_HEADS * HEAD_DIM,) + tuple(np.delete(shape, axis))), 0, axis)

    def halves_exchangeable(w):
        w = w.reshape(D_MODEL, -1, 2, 2, HEAD_DIM // 4).transpose(0, 1, 3, 2, 4)
        return w.reshape(D_MODEL, -1)

    w_in = a["w_in"][0]
    at = np.cumsum([0, 256, 256, 512, 512, GATE_RANK, 512, 128, 128])
    q, k, v, g, ga, sq, sk, sv = (w_in[:, at[n]:at[n + 1]] for n in range(8))
    ga = np.concatenate([ga, np.zeros((D_MODEL, P - GATE_RANK), w_in.dtype)], 1)
    w_in = np.concatenate([ga, k, q, sv, halves_exchangeable(sk), halves_exchangeable(heads_side_by_side(sq, 1)), v, g], 1)
    w_out = a["w_out"][0]
    w_out = np.concatenate([heads_side_by_side(w_out[512:], 0), w_out[:512]], 0)
    vecs = np.concatenate(
        [columns(a[n][0]) for n in ("ffn1_pre_norm", "ffn1_post_norm", "mix_pre_norm", "mix_post_norm",
                                    "ffn2_pre_norm", "ffn2_post_norm")]
        + [columns(heads_side_by_side(a["swa_out_norm"][0], 0)), columns(a["gla_out_norm"][0]),
           columns(a["gla_b_a"][0]), np.broadcast_to(a["swa_sinks"][0], (P, SWA_HEADS)),
           np.broadcast_to(np.array([EPS, 4 * EPS], np.float32), (P, 2))], 1)
    x_t = np.concatenate([a["meta_tokens"], a["x"][0]], 0).T.reshape(KD, P, L).transpose(1, 0, 2)
    cos_t, sin_t = rope_tables()
    band, level_mask = masks()
    arrays = {
        "x_t": x_t, "vecs": vecs,
        "up1": up_units(a["ffn1_w_gate"][0], a["ffn1_w_up"][0]), "down1": down_units(a["ffn1_w_down"][0]),
        "w_in": tiles(w_in, KD).reshape(N_IN, P, W_UP), "w_a2": a["gla_w_a2"][0],
        "w_out": tiles(w_out, KD).reshape(KD, P, W_UP),
        "up2": up_units(a["ffn2_w_gate"][0], a["ffn2_w_up"][0]), "down2": down_units(a["ffn2_w_down"][0]),
        "cos_t": cos_t, "sin_t": sin_t,
        "ident": np.eye(P, dtype=np.float32), "select": np.broadcast_to((np.arange(31) == 15).astype(np.float32), (P, 31)),
        "band": band, "level_mask": level_mask,
    }
    arrays = {f"in_{name}": np.ascontiguousarray(value) for name, value in arrays.items()}
    nc = bacc.Bacc("TRN2", target_bir_lowering=False, num_devices=1)
    aps = [nc.dram_tensor(name, v.shape, mybir.dt.from_np(v.dtype), kind="ExternalInput").ap()
           for name, v in arrays.items()]
    out = nc.dram_tensor("out", (P, KD, SEQ), F32, kind="ExternalOutput").ap()
    hybrid_layer(nc, *aps, out)
    r = run_bass_kernel_spmd(nc, [arrays], core_ids=[0])
    y = np.asarray(r.results[0]["out"])
    return np.ascontiguousarray(y.transpose(1, 0, 2).reshape(D_MODEL, SEQ).T)[None]
```

```python
from contextlib import ExitStack

import numpy as np
import concourse.bass as bass
from concourse import mybir

F32 = mybir.dt.float32
F32R = mybir.dt.float32r
U32 = mybir.dt.uint32
ALU = mybir.AluOpType
ACT = mybir.ActivationFunctionType
AX_X = mybir.AxisListType.X

P = 128
D_MODEL = 1024
SEQ = 512
N_META = 16
L = SEQ + N_META
D_FF = 2816
EPS = 1e-6
KD = D_MODEL // P
KF = D_FF // P
KH = KF // 2

GLA_HEADS, GLA_DK, GLA_DV, GATE_RANK = 4, 64, 128, 16
GLA_TAU = 16.0
SWA_HEADS, KV_HEADS, HEAD_DIM = 8, 2, 64
GROUP = SWA_HEADS // KV_HEADS
ROPE_THETA = 10000.0
NEG = -1e30
C = 128
NC = SEQ // C
SPAN = N_META + 2 * C
LEVELS = [64, 32, 16, 8, 4, 2, 1]

T_GA, T_GK, T_GQ, T_SV, T_SK, T_SQ, T_GV, T_GG = 0, 1, 3, 5, 6, 7, 11, 15
N_IN = 19

UP_UNITS, DOWN_UNITS = 2 * KF, 2 * KD
U_UP1 = 0
U_DOWN1 = U_UP1 + UP_UNITS
U_IN = U_DOWN1 + DOWN_UNITS
U_OUT = U_IN + N_IN
U_UP2 = U_OUT + KD
U_DOWN2 = U_UP2 + UP_UNITS
N_UNITS = U_DOWN2 + DOWN_UNITS
RAW, OPS = 4, 2
W_UP, W_DOWN = KD * P, KH * P

V_PRE1, V_POST1, V_PREM, V_POSTM, V_PRE2, V_POST2 = (KD * n for n in range(6))
V_SWA = 6 * KD
V_GLA = V_SWA + 4
V_BA = V_GLA + 1
V_SINK = V_BA + 2
V_EPS = V_SINK + SWA_HEADS
N_VEC = V_EPS + 2

N_PRE1, N_POST1, N_PREM, N_SWA, N_GLA, N_POSTM, N_PRE2, N_POST2 = 0, 1, 3, 4, 5, 6, 8, 9
BEFORE = {N_PRE1: 0, N_PREM: 1, N_PRE2: 3}
TAIL = KD - 3
POST = {N_POST1: 0, N_POSTM: 1, N_POST2: 2}
HALVED = [1, 2, 1]
BLOCKS = 4
LEAD_LAG, SUM_STEP, SPREAD_STEP = (KD, KD - 2), 3, 5
POOL_TILES = (2, 4, 6)
PAIR, PASSES = 2, NC * KV_HEADS * 2


def whole_tiles_before(post):
    return sum(KD - n for n in HALVED[:post])


def halves_before(post):
    return 2 * sum(HALVED[:post])


def sums_before(norm, half=0):
    turn = (N_PRE1, N_PREM, N_PRE2).index(norm)
    return (KD - 1) * (turn + half) + TAIL * max(turn - 1, 0)


def norm_copies(norm):
    return norm + 1 - 2 * (norm > N_GLA)


def hybrid_layer(nc, x_t, vecs, up1, down1, w_in, w_a2, w_out, up2, down2, cos_t, sin_t, ident, select, band,
                 level_mask, out):
    ctx = ExitStack()
    with ctx:
        def sb(name, shape, dt, stack=ctx):
            return stack.enter_context(nc.sbuf_tensor(name, shape, dt))

        def sem(name):
            return ctx.enter_context(nc.semaphore(name))

        h = sb("h", [P, KD, L], F32)
        raw = sb("raw", [P, RAW, W_DOWN], F32)
        w_hi = sb("w_hi", [P, OPS, W_DOWN], F32R)
        w_lo = sb("w_lo", [P, OPS, W_DOWN], F32R)
        vec = sb("vec", [P, N_VEC], F32)
        carry = sb("carry", [P, SEQ], F32)
        ident_s = sb("ident_s", [P, P], F32)
        select_s = sb("select_s", [P, 31], F32)
        stat = sb("stat", [GLA_HEADS * NC, 2, L // BLOCKS], F32)
        sumsq = sb("sumsq", [P, L], F32)
        rnorm = sb("rnorm", [P, L], F32)
        gate = sb("gate", [P, L], F32)
        up = sb("up", [P, L], F32)
        sq = sb("sq", [P, 2, L], F32)
        table_probe = sb("table_probe", [P, 1], F32)
        with ExitStack() as s:
            xa_hi, xa_lo = sb("xa_hi", [P, KD, L], F32R, s), sb("xa_lo", [P, KD, L], F32R, s)
            hid1_hi, hid1_lo = sb("hid1_hi", [P, KF, L], F32R, s), sb("hid1_lo", [P, KF, L], F32R, s)
        with ExitStack() as s:
            y1 = sb("y1", [P, KD, L], F32, s)
            squares1 = sb("squares1", [P, KD, L], F32, s)
            xb_hi, xb_lo = sb("xb_hi", [P, KD, L], F32R, s), sb("xb_lo", [P, KD, L], F32R, s)
        with ExitStack() as s:
            proj = sb("proj", [P, 16, L], F32, s)
            with ExitStack() as x:
                sb("gla_sq_offset", [P, 6400], F32, x)
                gla_sq = sb("gla_sq", [P, GLA_HEADS, SEQ], F32, x)
            with ExitStack() as x:
                cat_hi, cat_lo = sb("cat_hi", [P, KD, SEQ], F32R, x), sb("cat_lo", [P, KD, SEQ], F32R, x)
            sb("mix_operand", [P, 2 * KD, L], F32, s)
            kv2 = sb("kv2", [P, 2, L], F32, s)
            with ExitStack() as x:
                b_real = sb("b_real", [P, 2, SEQ], F32, x)
                lmask = sb("lmask", [P, len(LEVELS) + 1, C], U32, x)
            swa_sq = sb("swa_sq", [P, 4, SEQ], F32, s)
            b_meta = sb("b_meta", [P, 2, N_META], F32, s)
            dec = sb("dec", [P, 2, NC], F32, s)
            q_in = sb("q_in", [P, 2, SEQ], F32, s)
            k_out = sb("k_out", [P, 2, L], F32, s)
            ktok = sb("ktok", [P, NC, 2 * P], F32, s)
            attn = sb("attn", [P, GLA_HEADS * SEQ], F32, s)
            cos_s, sin_s = sb("cos_s", [P, L], F32, s), sb("sin_s", [P, L], F32, s)
            with ExitStack() as x:
                wa2_s = sb("wa2_s", [GATE_RANK, 2 * P], F32, x)
            p_tm = sb("p_tm", [N_META, PAIR, C], F32, s)
            band_s = sb("band_s", [P, 2, SPAN], F32, s)
            kx = sb("kx", [P, NC, SPAN], F32, s)
            small = sb("small", [P, 3, 3, PAIR], F32, s)
            with ExitStack() as x:
                decay = sb("decay", [P, 2, SEQ], F32, x)
                lv_k = sb("lv_k", [P, 2, 2, SEQ], F32, x)
                lv_q = sb("lv_q", [P, 2, 2, SEQ], F32, x)
            with ExitStack() as x:
                scores = sb("scores", [P, 3, PAIR, SPAN], F32, x)
                p_t = sb("p_t", [P, PAIR, 2, C], F32, x)
                vs_tok = sb("vs_tok", [P, NC + 1, P], F32, x)
                vtok = sb("vtok", [P, NC + 1, 4 * P], F32, x)
        with ExitStack() as s:
            hid2_hi, hid2_lo = sb("hid2_hi", [P, KF, SEQ], F32R, s), sb("hid2_lo", [P, KF, SEQ], F32R, s)
            xc_hi, xc_lo = sb("xc_hi", [P, KD, SEQ], F32R, s), sb("xc_lo", [P, KD, SEQ], F32R, s)
        with ExitStack() as s:
            y2 = sb("y2", [P, KD, SEQ], F32, s)
            squares2 = sb("squares2", [P, KD, SEQ], F32, s)
        with ExitStack() as s:
            sb("hid2_space", [P, 2 * KF, SEQ], F32, s)
            y3 = sb("y3", [P, KD, SEQ], F32, s)

        ps = ctx.enter_context(nc.psum_tensor("ps", [P, 8, 512], F32))

        raw_landed = [sem(f"raw_landed{i}") for i in range(RAW)]
        hi_split, lo_split = sem("hi_split"), sem("lo_split")
        unit_used = sem("unit_used")
        x_landed = [sem(f"x_landed{k}") for k in range(KD)]
        vec_landed, select_landed, table_landed = sem("vec_landed"), sem("select_landed"), sem("table_landed")
        carry_set = sem("carry_set")
        tail_summed = sem("tail_summed")
        squared, summed = sem("squared"), sem("summed")
        y_squared, y_summed, y_evicted = sem("y_squared"), sem("y_summed"), sem("y_evicted")
        half_done, half_squared, half_summed = sem("half_done"), sem("half_squared"), sem("half_summed")
        norm_summed, rms_ready, norm_ready = sem("norm_summed"), sem("rms_ready"), sem("norm_ready")
        norm_spread, r_ready = sem("norm_spread"), sem("r_ready")
        h_updated, h_pool, y_scaled = sem("h_updated"), sem("h_pool"), sem("y_scaled")
        x_hi, x_ready = sem("x_hi"), sem("x_ready")
        gate_scaled, gu_evicted = sem("gate_scaled"), sem("gu_evicted")
        silu_done, hid_written, hid_hi, hid_ready = sem("silu_done"), sem("hid_written"), sem("hid_hi"), sem("hid_ready")
        proj_evicted = sem("proj_evicted")
        z_done, z_log, z_read = sem("z_done"), sem("z_log"), sem("z_read")
        b_ready, k_diff, k_exp, q_exp = sem("b_ready"), sem("k_diff"), sem("k_exp"), sem("q_exp")
        k_out_ready, q_in_ready = sem("k_out_ready"), sem("q_in_ready")
        tables_scaled, kx_ready = sem("tables_scaled"), sem("kx_ready")
        attn_zeroed, lv_zeroed = sem("attn_zeroed"), sem("lv_zeroed")
        lv_diff, lv_exp, lv_k_ready, lv_q_ready = sem("lv_diff"), sem("lv_exp"), sem("lv_k_ready"), sem("lv_q_ready")
        lv_scored, lv_taken = sem("lv_scored"), sem("lv_taken")
        turned, turned_out = sem("turned"), sem("turned_out")
        v_taken, swa_summed = sem("v_taken"), sem("swa_summed")
        og_done, og_squared, og_taken, gg_silu = sem("og_done"), sem("og_squared"), sem("og_taken"), sem("gg_silu")
        s_done, s_masked, s_max, s_exp, s_normed = sem("s_done"), sem("s_masked"), sem("s_max"), sem("s_exp"), sem("s_normed")
        p_turned, p_taken = sem("p_turned"), sem("p_taken")
        pv_done, pv_evicted = sem("pv_done"), sem("pv_evicted")
        cat_raw, cat_hi_done, cat_ready = sem("cat_raw"), sem("cat_hi_done"), sem("cat_ready")
        dve_step, act_step = sem("dve_step"), sem("act_step")
        y3_scaled = sem("y3_scaled")
        out_dve, out_pool, stored = sem("out_dve"), sem("out_pool"), sem("stored")

        def f32(ap):
            return ap.bitcast(F32)

        def unit(base, j, i=0):
            return base + j + RAW * i, (base + j) % RAW, (base + j) // RAW + i, (base + j) % OPS

        def in_psum(bank, n_tok):
            return ps[:, bank:bank + 2, 0:L // 2] if n_tok == L else ps[:, bank, 0:SEQ]

        def row(ap, n_tok):
            return ap.rearrange("p (b n) -> p b n", b=2) if n_tok == L else ap[:, 0:SEQ]

        def tokens(n_tok):
            return slice(L - n_tok, L)

        def half_cols(half, n_tok):
            return slice(half * (n_tok // 2), (half + 1) * (n_tok // 2))

        def h_cols(half, n_tok):
            start = L - n_tok + half * (n_tok // 2)
            return slice(start, start + n_tok // 2)

        def pool_tiles_before(k):
            return sum(n < k for n in POOL_TILES)

        def in_bank(j):
            return 2 * j if j < 3 else 2 * ((j - 3) % 2)

        in_dst = [None] * N_IN
        in_dst[T_GA] = proj[:, 15, :]
        in_dst[T_SK], in_dst[T_SV] = kv2[:, 0, :], kv2[:, 1, :]
        for t, at, count in ((T_GK, 0, 2), (T_GQ, 2, 2), (T_GV, 4, 4), (T_SQ, 8, 4), (T_GG, 12, 4)):
            for n in range(count):
                in_dst[t + n] = proj[:, at + n, :]
        ga = proj[0:GATE_RANK, 15, :]
        gk, gq = proj[:, 0:2, :], proj[:, 2:4, N_META:L]
        gv, gg = proj[:, 4:8, :], proj[:, 12:16, N_META:L]
        sk, sv = kv2[:, 0, :], kv2[:, 1, :]
        sq_heads = proj[:, 8:12, N_META:L]
        o_gla = proj[:, 0:4, 0:SEQ]
        o_swa = sq_heads
        z_log_t = attn[:, 0:2 * L].rearrange("p (t n) -> p t n", t=2)
        z_min = k_out[:, :, :]
        state = k_out[:, :, 0:SEQ].rearrange("p t (c n) -> p t c n", c=NC)

        def place(head):
            return head % 2 * 2 + head // 2

        attn_heads = attn[:, :].rearrange("p (h n) -> p h n", h=GLA_HEADS)

        GAP_Z = 2 * 3 + 1
        GAP_B, GAP_DECAY, GAP_LV = GAP_Z + 2, GAP_Z + 3, 2 * 6 + 1
        GAP_TURN = GAP_LV + len(LEVELS) + 1
        GAP_SWA = GAP_TURN + 1
        assert GAP_SWA + PASSES == 2 * N_IN
        FREE = slice(3 * P, 4 * P)
        GAP_V, V_STEPS = 2 * (T_GV + 1), 2 * 4 + 2 + NC

        def gla_step(g):
            step = g - GAP_V
            if 0 <= step < 8:
                return "blocks", step // 2, 2 * (step % 2)
            if 8 <= step < 10:
                return "meta", 2 * (step - 8), 0
            return ("state", step - 10, 0) if 10 <= step < V_STEPS else None

        def gla_steps_before(g):
            return min(max(g - GAP_V, 0), V_STEPS)

        assert GAP_V >= GAP_SWA and GAP_V + V_STEPS == 2 * N_IN

        def swa_pass(p):
            return p // (NC * KV_HEADS), (p // KV_HEADS) % NC, p % KV_HEADS

        block = ctx.enter_context(nc.Block())

        @block.sync
        def _(sp):
            def load(src, base, j, width, i=0):
                u, slot, turn, _ = unit(base, j, i)
                if base + j >= RAW:
                    sp.wait_ge(lo_split, u - RAW + 1)
                sp.dma_start(raw[:, slot, 0:width], src[j + RAW * i]).then_inc(raw_landed[slot], 16)

            def stream(src, base, count, width, first=0):
                rounds = (count - first) // RAW
                with sp.Fori(0, rounds) as i:
                    for j in range(RAW):
                        load(src, base, first + j, width, i)
                for j in range(first + RAW * rounds, count):
                    load(src, base, j, width)

            sp.dma_start(vec[:, :], vecs).then_inc(vec_landed, 16)
            load(up1, U_UP1, 0, W_UP)
            for k in range(KD):
                sp.dma_start(h[:, k, :], x_t[:, k, :]).then_inc(x_landed[k], 16)
                if k == 0:
                    load(up1, U_UP1, 1, W_UP)
            sp.dma_start(ident_s[:, :], ident).then_inc(select_landed, 16)
            sp.dma_start(select_s[:, :], select).then_inc(select_landed, 16)
            load(up1, U_UP1, 2, W_UP)
            load(up1, U_UP1, 3, W_UP)
            stream(up1, U_UP1, UP_UNITS, W_UP, first=RAW)
            stream(down1, U_DOWN1, DOWN_UNITS, W_DOWN)
            stream(w_in, U_IN, 4, W_UP)
            sp.wait_ge(unit_used, U_IN)
            for dst, src in ((cos_s[:, :], cos_t), (sin_s[:, :], sin_t), (wa2_s[:, :], w_a2),
                             (band_s[:, :, :], band), (lmask[:, :, :], level_mask)):
                sp.dma_start(dst, src).then_inc(table_landed, 16)
            stream(w_in, U_IN, N_IN, W_UP, first=4)
            stream(w_out, U_OUT, KD, W_UP)
            stream(up2, U_UP2, UP_UNITS, W_UP)
            stream(down2, U_DOWN2, DOWN_UNITS, W_DOWN)
            for half in range(2):
                for k in range(KD):
                    before = pool_tiles_before(k)
                    if k in POOL_TILES:
                        sp.wait_ge(out_pool, len(POOL_TILES) * half + before + 1)
                    else:
                        sp.wait_ge(out_dve, (KD - len(POOL_TILES)) * half + k - before + 1)
                    sp.dma_start(out[:, k, half_cols(half, SEQ)], h[:, k, h_cols(half, SEQ)]).then_inc(stored, 16)
            sp.wait_ge(stored, 16 * 2 * KD)

        @block.tensor
        def _(pe):
            def k_tile(slot, k, xh, xl, kx_, bank, n_tok, first, last):
                width = L // 2 if n_tok == L else SEQ
                wh, wl = w_hi[:, slot, k * P:(k + 1) * P], w_lo[:, slot, k * P:(k + 1) * P]
                for n in range(n_tok // width):
                    dst, cols = ps[:, bank + n, 0:width], slice(n * width, (n + 1) * width)
                    pe.matmul(dst, wh, xh[:, kx_, cols], start=first, stop=False)
                    pe.matmul(dst, wh, xl[:, kx_, cols], start=False, stop=False)
                    mm = pe.matmul(dst, wl, xh[:, kx_, cols], start=False, stop=last)
                return mm

            def products(base, j, i, xh, xl, k0, nk, bank, n_tok, first=True, last=True, after=None):
                u, _, _, slot = unit(base, j, i)
                pe.wait_ge(lo_split, u + 1)
                for k in range(nk):
                    mm = k_tile(slot, k, xh, xl, k0 + k, bank, n_tok, first and k == 0, last and k == nk - 1)
                    if k == nk - 1:
                        mm.then_inc(unit_used, 1)
                    if after and k in after:
                        after[k]()

            def half_k_tile(slot, k, xh, xl, kx_, dst, half, n_tok, first, last):
                wh, wl = w_hi[:, slot, k * P:(k + 1) * P], w_lo[:, slot, k * P:(k + 1) * P]
                cols = half_cols(half, n_tok)
                pe.matmul(dst, wh, xh[:, kx_, cols], start=first, stop=False)
                pe.matmul(dst, wh, xl[:, kx_, cols], start=False, stop=False)
                return pe.matmul(dst, wl, xh[:, kx_, cols], start=False, stop=last)

            def half_norm_sum(norm, half, n_tok):
                post, w = POST[norm], n_tok // BLOCKS
                pe.wait_ge(half_summed, halves_before(post) + HALVED[post] * (half + 1))
                for b in range(2):
                    at = (2 * half + b) * w
                    mm = pe.matmul(ps[0:2, 4 + 2 * half, 0:w], select_s[:, 15 - b:17 - b], sumsq[:, at:at + w],
                                   start=b == 0, stop=b == 1)
                mm.then_inc(norm_summed, 1)

            def half_spread(norm, half, n_tok):
                pe.wait_ge(norm_ready, norm + half + 1)
                w = n_tok // BLOCKS
                for b in range(2):
                    mm = pe.matmul(ps[:, 5 + 2 * half, b * w:(b + 1) * w], ident_s[0:2, b:b + 1].broadcast_to([2, P]),
                                   stat[0:2, (norm + half) % 2, 0:w], start=True, stop=True)
                mm.then_inc(norm_spread, 1)

            def last_pair(base, norm, xh, xl, nk, banks, n_tok, evicted, sum_at, spread_at):
                one_tile = banks[0] == banks[1]
                for half in range(2):
                    for n in range(2):
                        if half == 0:
                            pe.wait_ge(y_evicted, evicted[n])
                            pe.wait_ge(lo_split, base + n + 1)
                        for k in range(nk):
                            mm = half_k_tile((base + n) % OPS, k, xh, xl, (n * nk if one_tile else 0) + k,
                                             ps[:, banks[n] + half, 0:n_tok // 2], half, n_tok,
                                             k == 0 and not (one_tile and n), k == nk - 1 and not (one_tile and n == 0))
                            if half == 0 and (n, k) == (1, nk - 1):
                                mm.then_inc(half_done, 1)
                            if half and k == nk - 1:
                                mm.then_inc(unit_used, 1)
                            if half and n * nk + k == sum_at:
                                half_norm_sum(norm, 0, n_tok)
                            if half and n * nk + k == spread_at:
                                half_spread(norm, 0, n_tok)

            def lead_halves(base, norm, xh, xl, banks, n_tok, x0):
                for half in range(2):
                    dst = [ps[:, b + half, 0:n_tok // 2] if n_tok == L else ps[:, b, half_cols(half, n_tok)]
                           for b in banks]
                    lag = LEAD_LAG[half]
                    for step in range(KD + lag):
                        if step < KD:
                            pe.wait_ge(x_ready, x0 + half * KD + step + 1)
                            if (half, step) == (0, 0):
                                pe.wait_ge(lo_split, base + 1)
                            mm = half_k_tile(base % OPS, step, xh, xl, step, dst[0], half, n_tok, step == 0, step == KD - 1)
                            if (half, step) == (1, KD - 1):
                                mm.then_inc(unit_used, 1)
                        if step >= lag:
                            if half == 0 and step == lag:
                                pe.wait_ge(lo_split, base + 2)
                            k = step - lag
                            mm = half_k_tile((base + 1) % OPS, k, xh, xl, k, dst[1], half, n_tok, k == 0, k == KD - 1)
                        if (half, step) == (0, SUM_STEP):
                            half_norm_sum(norm, 1, n_tok)
                        if (half, step) == (0, SPREAD_STEP):
                            half_spread(norm, 1, n_tok)
                mm.then_inc(unit_used, 1)

            def lead_pair(base, xh, xl, banks, n_tok, ready):
                for step in range(KD + 2):
                    if step < KD:
                        ready(step)
                        if step == 0:
                            pe.wait_ge(lo_split, base + 1)
                        mm = k_tile(base % OPS, step, xh, xl, step, banks[0], n_tok, step == 0, step == KD - 1)
                        if step == KD - 1:
                            mm.then_inc(unit_used, 1)
                    if step >= 2:
                        k = step - 2
                        if k == 0:
                            pe.wait_ge(lo_split, base + 2)
                        mm = k_tile((base + 1) % OPS, k, xh, xl, k, banks[1], n_tok, k == 0, k == KD - 1)
                mm.then_inc(unit_used, 1)

            def block_sums(norm, srcs, n_tok, bank, rows=BLOCKS, row0=0, start=True, stop=True):
                w = n_tok // BLOCKS
                for n, src in enumerate(srcs):
                    for b in range(BLOCKS):
                        at = row0 + b
                        mm = pe.matmul(ps[0:rows, bank, 0:w], select_s[:, 15 - at:15 - at + rows],
                                       src[:, b * w:(b + 1) * w], start=start and n == 0 and b == 0,
                                       stop=stop and n == len(srcs) - 1 and b == BLOCKS - 1)
                if stop:
                    mm.then_inc(norm_summed, 1)

            def spread(norm, n_tok, bank, rows=BLOCKS):
                pe.wait_ge(norm_ready, norm + 1)
                w = n_tok // BLOCKS
                for b in range(rows):
                    if rows > BLOCKS:
                        dst = ps[:, bank + 2 * (b // BLOCKS), (b % BLOCKS) * w:(b % BLOCKS + 1) * w]
                    elif n_tok == L:
                        dst = ps[:, bank + b // 2, (b % 2) * w:(b % 2 + 1) * w]
                    else:
                        dst = ps[:, bank, b * w:(b + 1) * w]
                    mm = pe.matmul(dst, ident_s[0:rows, b:b + 1].broadcast_to([rows, P]), stat[0:rows, norm % 2, 0:w],
                                   start=True, stop=True)
                mm.then_inc(norm_spread, 1)

            def pre_sum(norm, n_tok, bank):
                if norm == N_PRE1:
                    pe.wait_ge(select_landed, 32)
                pe.wait_ge(summed, KD - 1 if norm == N_PRE1 else sums_before(norm, 1) + TAIL)
                block_sums(norm, [sumsq], n_tok, bank)

            def ffn_up(base, tile0, xh, xl, n_tok, norm):
                def tile(t, j, q, i=0):
                    pe.wait_ge(gu_evicted, tile0 + t - 1)
                    products(base, j, i, xh, xl, 0, KD, 4 * q, n_tok)
                    products(base, j + 1, i, xh, xl, 0, KD, 4 * q + 2, n_tok)

                if n_tok == L:
                    lead_pair(base, xh, xl, (0, 2), n_tok, lambda k: pe.wait_ge(x_ready, k + 1))
                    pre_sum(norm, n_tok, 6)
                    products(base, 2, 0, xh, xl, 0, KD, 4, n_tok, after={4: lambda: spread(norm, n_tok, 6)})
                    pe.wait_ge(r_ready, norm_copies(norm))
                    products(base, 3, 0, xh, xl, 0, KD, 6, n_tok)
                else:
                    lead_halves(base, N_POSTM, xh, xl, (0, 2), n_tok, BEFORE[norm] * KD)
                    products(base, 2, 0, xh, xl, 0, KD, 4, n_tok)
                    pre_sum(norm, n_tok, 1)
                    products(base, 3, 0, xh, xl, 0, KD, 6, n_tok, after={3: lambda: spread(norm, n_tok, 3)})
                with pe.Fori(1, KF // 2) as i:
                    tile(2 * i, 0, 0, i)
                    tile(2 * i + 1, 2, 1, i)

            def ffn_down(base, tile0, hid0, hi, lo, n_tok, norm):
                def tile(d, j, q, i=0):
                    if isinstance(d, int) and d == 0:
                        pe.wait_ge(hid_ready, hid0 + KF - 2)
                        pe.wait_ge(gu_evicted, hid0 + KF - 1)
                    else:
                        if not (isinstance(d, int) and tile0 + d < 2):
                            pe.wait_ge(y_evicted, tile0 + d - 1)
                    products(base, j, i, hi, lo, 0, KH, 2 * q, n_tok, last=False)
                    if isinstance(d, int) and d == 0:
                        pe.wait_ge(hid_ready, hid0 + KF)
                    products(base, j + 1, i, hi, lo, KH, KH, 2 * q, n_tok, first=False)

                tile(0, 0, 0)
                tile(1, 2, 1)
                with pe.Fori(1, KD // 2 - 1) as i:
                    tile(2 * i, 0, 0, i)
                    tile(2 * i + 1, 2, 1, i)
                tile(KD - 2, 2 * KD - 4, 0)
                last_pair(base + 2 * KD - 2, norm, hi, lo, KH, (2, 2), n_tok, [tile0 + KD - 2] * 2, 3, 8)

            def gate_logits():
                pe.wait_ge(table_landed, 16 * 5)
                pe.wait_ge(proj_evicted, 3)
                for t in range(2):
                    for n in range(2):
                        mm = pe.matmul(ps[:, 4 + 2 * t + n, 0:L // 2], wa2_s[:, t * P:(t + 1) * P],
                                       ga[:, n * L // 2:(n + 1) * L // 2], start=True, stop=True)
                mm.then_inc(z_done, 1)

            def level_scores(lv):
                diagonal = lv == len(LEVELS)
                if not diagonal:
                    pe.wait_ge(lv_k_ready, lv + 1)
                    pe.wait_ge(lv_q_ready, lv + 1)
                if lv >= 2:
                    pe.wait_ge(lv_taken, lv if diagonal else lv - 1)
                for c in range(NC):
                    cols = slice(c * C, (c + 1) * C)
                    for head in range(GLA_HEADS):
                        rows = slice(64 * (head % 2), 64 * (head % 2) + 64)
                        if diagonal:
                            kl, ql = gk[rows, head // 2, N_META + c * C:N_META + (c + 1) * C], gq[rows, head // 2, cols]
                            dst = ps[:, 4 + place(head), cols]
                        else:
                            m, at = LEVELS[lv], (head // 2 * NC + c) * C // 2
                            kl = lv_k[rows, lv % 2, head // 2, cols]
                            ql = lv_q[rows, lv % 2, head // 2, cols].rearrange("p (n x) -> p n x", x=2 * m)[:, :, m:2 * m]
                            dst = ps[:, 4 + 2 * (lv % 2) + head % 2, at:at + C // 2].rearrange("p (n x) -> p n x", x=m)
                        mm = pe.matmul(dst, kl, ql, start=True, stop=True)
                mm.then_inc(lv_scored, 1)

            def turn_early():
                pe.wait_ge(lv_taken, len(LEVELS) + 1)
                pe.wait_ge(k_out_ready, 1)
                for b in range(NC):
                    pe.transpose(ps[:, 4, b * P:(b + 1) * P], sv[:, N_META + b * C:N_META + (b + 1) * C], ident_s[:, :])
                pe.transpose(ps[0:N_META, 5, 0:P], sv[:, 0:N_META], ident_s[:, :])
                for c in range(NC - 1):
                    for t in range(2):
                        col = (c % 2) * 2 * P + t * P
                        pe.transpose(ps[:, 6 + c // 2, col:col + P], k_out[:, t, N_META + c * C:N_META + (c + 1) * C],
                                     ident_s[:, :])
                for t in range(2):
                    mm = pe.transpose(ps[0:N_META, 7, (2 + t) * P:(3 + t) * P], k_out[:, t, 0:N_META], ident_s[:, :])
                mm.then_inc(turned, 1)

            def gla_work(kind, n, b):
                if kind == "blocks":
                    pe.wait_ge(proj_evicted, T_GV + n + 1)
                    for i in range(2):
                        at = N_META + (b + i) * C
                        pe.transpose(ps[:, 4 + i, FREE], gv[:, n, at:at + C], ident_s[:, :])
                elif kind == "meta":
                    for i in range(2):
                        pe.transpose(ps[0:N_META, 4 + i, FREE], gv[:, n + i, 0:N_META], ident_s[:, :])
                else:
                    rows = C if n else N_META
                    for head in range(GLA_HEADS):
                        at = 64 * (head % 2)
                        pe.matmul(ps[at:at + 64, 4 + head // 2, FREE], ktok[0:rows, n, head * 64:head * 64 + 64],
                                  vtok[0:rows, n, head * P:(head + 1) * P], start=True, stop=True)

            def swa_scores(p):
                pair, c, g = swa_pass(p)
                rows = slice(64 * g, 64 * g + 64)
                if p:
                    pe.wait_ge(s_masked, p)
                else:
                    pe.wait_ge(turned_out, 1)
                    pe.wait_ge(kx_ready, 1 + 2 * NC)
                if gla_steps_before(GAP_SWA + p):
                    pe.wait_ge(v_taken, gla_steps_before(GAP_SWA + p))
                if gla_step(GAP_SWA + p):
                    gla_work(*gla_step(GAP_SWA + p))
                for n in range(PAIR):
                    mm = pe.matmul(ps[:, 4 + n, 0:SPAN], sq_heads[rows, PAIR * pair + n, c * C:(c + 1) * C],
                                   kx[rows, c, :], start=True, stop=True)
                mm.then_inc(s_done, 1)

            def swa_turn(p):
                pair, c, g = swa_pass(p)
                pe.wait_ge(s_normed, p + 1)
                if p:
                    pe.wait_ge(pv_evicted, p)
                for n in range(PAIR):
                    src = scores[:, p % 3, n, :]
                    if c:
                        pe.transpose(ps[:, 6, 2 * n * C:(2 * n + 1) * C], src[:, N_META:N_META + C], ident_s[:, :])
                    pe.transpose(ps[:, 6, (2 * n + 1) * C:(2 * n + 2) * C], src[:, N_META + C:SPAN], ident_s[:, :])
                    mm = pe.transpose(ps[0:N_META, 7, n * C:(n + 1) * C], src[:, 0:N_META], ident_s[:, :])
                mm.then_inc(p_turned, 1)

            def swa_values(p):
                pair, c, g = swa_pass(p)
                pe.wait_ge(p_taken, p + 1)
                cols = slice(64 * g, 64 * g + 64)
                dst = ps[64 * g:64 * g + 64, 7, PAIR * C:2 * PAIR * C]
                pe.matmul(dst, vs_tok[0:N_META, 0, cols], p_tm[:, :, :], start=True, stop=False)
                if c:
                    pe.matmul(dst, vs_tok[:, c, cols], p_t[:, :, 0, :], start=False, stop=False)
                pe.matmul(dst, vs_tok[:, c + 1, cols], p_t[:, :, 1, :], start=False, stop=True).then_inc(pv_done, 1)

            def gap_first(g):
                if g == 2 * 2:
                    pre_sum(N_PREM, L, 6)
                if g == 2 * 2 + 1:
                    spread(N_PREM, L, 6)
                p = g - GAP_SWA
                if 0 <= p - 3:
                    swa_values(p - 3)

            def gap(g):
                if g == GAP_Z:
                    gate_logits()
                if 0 <= g - GAP_LV <= len(LEVELS):
                    level_scores(g - GAP_LV)
                if g == GAP_TURN:
                    turn_early()
                p = g - GAP_SWA
                if 0 <= p - 2:
                    swa_turn(p - 2)
                if 0 <= p < PASSES:
                    swa_scores(p)

            ffn_up(U_UP1, 0, xa_hi, xa_lo, L, N_PRE1)
            ffn_down(U_DOWN1, 0, 0, hid1_hi, hid1_lo, L, N_POST1)

            lead_halves(U_IN, N_POST1, xb_hi, xb_lo, (in_bank(0), in_bank(1)), L, BEFORE[N_PREM] * KD)
            for j in range(2, N_IN):
                if j == 2:
                    pe.wait_ge(r_ready, norm_copies(N_POST1 + 1))
                elif j < 5:
                    pe.wait_ge(proj_evicted, j - 2)
                else:
                    pe.wait_ge(proj_evicted, j - 1)
                products(U_IN, j, 0, xb_hi, xb_lo, 0, KD, in_bank(j), L, after={
                    1: lambda: gap_first(2 * j), 3: lambda: gap(2 * j),
                    5: lambda: gap_first(2 * j + 1), 7: lambda: gap(2 * j + 1)})

            def gla_output(head):
                rows = slice(64 * (head % 2), 64 * (head % 2) + 64)
                if head == 0:
                    pe.wait_ge(v_taken, V_STEPS - 1)
                    pe.wait_ge(q_in_ready, 1)
                    pe.wait_ge(proj_evicted, N_IN)
                for c in range(NC):
                    cols = slice(c * C, (c + 1) * C)
                    pe.matmul(ps[:, head, cols], vtok[:, c + 1, head * P:(head + 1) * P], attn_heads[:, place(head), cols],
                              start=True, stop=False)
                    if head == 0 and c == NC - 1:
                        pe.wait_ge(v_taken, V_STEPS)
                    mm = pe.matmul(ps[:, head, cols], state[rows, head // 2, c, :], q_in[rows, head // 2, cols],
                                   start=False, stop=True)
                mm.then_inc(og_done, 1)

            gap_first(2 * N_IN)
            gla_output(0)
            gap(2 * N_IN)
            gla_output(1)
            gap_first(2 * N_IN + 1)
            gap(2 * N_IN + 1)
            gla_output(2)
            gap_first(2 * N_IN + 2)
            gla_output(3)

            pe.wait_ge(swa_summed, 1 + 2 * NC)
            block_sums(N_SWA, [swa_sq[:, 0, :]], SEQ, 6)
            for head in range(GLA_HEADS):
                pe.wait_ge(og_squared, head + 1)
                block_sums(N_GLA, [gla_sq[:, head, :]], SEQ, 7, rows=GLA_HEADS * NC, row0=head * NC, start=head == 0,
                           stop=head == GLA_HEADS - 1)
                if head == 1:
                    spread(N_SWA, SEQ, 6)

            def cat_arrived(k):
                if k == 0:
                    pe.wait_ge(og_taken, GLA_HEADS)
                if k == 1:
                    spread(N_GLA, SEQ, 1, rows=GLA_HEADS * NC)
                pe.wait_ge(cat_ready, k + 1)

            def out_tile(t, n):
                pe.wait_ge(y_evicted, KD + t - 1)
                pe.wait_ge(lo_split, U_OUT + t + 1)
                for k in range(KD):
                    mm = k_tile((U_OUT + n) % OPS, k, cat_hi, cat_lo, k, 2 * n, SEQ, k == 0, k == KD - 1)
                mm.then_inc(unit_used, 1)

            lead_pair(U_OUT, cat_hi, cat_lo, (0, 2), SEQ, cat_arrived)
            with pe.Fori(1, KD // 2 - 1) as i:
                out_tile(2 * i, 0)
                out_tile(2 * i + 1, 1)
            last_pair(U_OUT + KD - 2, N_POSTM, cat_hi, cat_lo, KD, (0, 2), SEQ, [2 * KD - 3, 2 * KD - 2], 4, 9)

            ffn_up(U_UP2, KF, xc_hi, xc_lo, SEQ, N_PRE2)
            ffn_down(U_DOWN2, 2 * KD, KF, hid2_hi, hid2_lo, SEQ, N_POST2)
            half_norm_sum(N_POST2, 1, SEQ)
            half_spread(N_POST2, 1, SEQ)

        @block.scalar
        def _(act):
            def split_hi(base, j, width, i=0):
                u, raw_slot, turn, slot = unit(base, j, i)
                if base + j >= OPS:
                    act.wait_ge(unit_used, u - OPS + 1)
                act.wait_ge(raw_landed[raw_slot], 16 * (turn + 1))
                act.activation(w_hi[:, slot, 0:width], raw[:, raw_slot, 0:width], ACT.Copy).then_inc(hi_split, 1)

            def root(norm, w, bank, n_feat, rows=BLOCKS, half_step=False):
                act.wait_ge(norm_summed, norm + 1)
                if norm >= 2:
                    act.wait_ge(norm_spread, norm - 1)
                col = V_EPS + half_step
                act.activation(stat[0:rows, norm % 2, 0:w], ps[0:rows, bank, 0:w], ACT.Sqrt,
                               bias=vec[0:rows, col:col + 1], scale=(4.0 if half_step else 1.0) / n_feat).then_inc(rms_ready, 1)

            def preload_sqrt():
                act.activation(table_probe[:, :], carry[:, 0:1], ACT.Sqrt).then_inc(act_step, 1)

            def operand_tile(k):
                act.activation(xa_hi[:, k, :], h[:, k, :], ACT.Copy, scale=vec[:, V_PRE1 + k:V_PRE1 + k + 1]).then_inc(x_hi, 1)

            def square_tile(k):
                if k >= 3:
                    act.wait_ge(summed, k - 2)
                act.activation(sq[:, k % 2, :] if k else sumsq[:, :], h[:, k, :], ACT.Square).then_inc(squared, 1)

            def half_operand(norm, half, k, n_tok, xh, v0):
                before, turn = pool_tiles_before(k), BEFORE[norm] - 1 + half
                if k in POOL_TILES:
                    act.wait_ge(h_pool, len(POOL_TILES) * turn + before + 1)
                else:
                    act.wait_ge(h_updated, (KD - len(POOL_TILES)) * turn + k - before + 1)
                act.activation(xh[:, k, half_cols(half, n_tok)], h[:, k, h_cols(half, n_tok)], ACT.Copy,
                               scale=vec[:, v0 + k:v0 + k + 1]).then_inc(x_hi, 1)

            def half_square(half, k, n_tok, squares):
                cols = half_cols(half, n_tok)
                act.activation(squares[:, k, cols], h[:, k, h_cols(half, n_tok)], ACT.Square).then_inc(squared, 1)

            def hidden_tile(tile0, t, hi, n_tok):
                act.wait_ge(gate_scaled, tile0 + t + 1)
                act.activation(gate[:, 0:n_tok], gate[:, 0:n_tok], ACT.Silu).then_inc(silu_done, 1)
                act.wait_ge(hid_written, tile0 + t + 1)
                act.activation(hi[:, t, :], up[:, 0:n_tok], ACT.Copy).then_inc(hid_hi, 1)

            def ffn_up(base, tile0, hi, n_tok, norm):
                split_hi(base, 2, W_UP)
                if n_tok == L:
                    root(norm, n_tok // BLOCKS, 6, D_MODEL)
                    split_hi(base, 3, W_UP)
                    hidden_tile(tile0, 0, hi, n_tok)
                    split_hi(base, 4, W_UP)
                else:
                    split_hi(base, 3, W_UP)
                    root(norm, n_tok // BLOCKS, 1, D_MODEL)
                    split_hi(base, 4, W_UP)
                    hidden_tile(tile0, 0, hi, n_tok)
                split_hi(base, 5, W_UP)
                hidden_tile(tile0, 1, hi, n_tok)
                with act.Fori(1, KF // 2 - 1) as i:
                    for n in range(2):
                        split_hi(base, 2 * n + 2, W_UP, i)
                        split_hi(base, 2 * n + 3, W_UP, i)
                        hidden_tile(tile0, 2 * i + n, hi, n_tok)
                split_hi(base, UP_UNITS - 2, W_UP)
                split_hi(base, UP_UNITS - 1, W_UP)
                hidden_tile(tile0, KF - 2, hi, n_tok)
                split_hi(base, UP_UNITS, W_DOWN)
                split_hi(base, UP_UNITS + 1, W_DOWN)
                hidden_tile(tile0, KF - 1, hi, n_tok)

            def result_tile(d, y, v0, norm, used, n_tok):
                act.wait_ge(unit_used, used)
                if d == 0:
                    act.wait_ge(norm_summed, norm)
                if d >= 3:
                    act.wait_ge(y_summed, whole_tiles_before(POST[norm]) - POST[norm] + d - 2)
                src = in_psum(2 * (d % 2), n_tok)
                act.activation(row(sq[:, d % 2, :] if d else sumsq, n_tok), src, ACT.Square).then_inc(y_squared, 1)
                act.activation(row(y[:, d, :], n_tok), src, ACT.Copy, scale=vec[:, v0 + d:v0 + d + 1]).then_inc(y_evicted, 1)

            def half_result(half, y, v0, norm, used, n_tok):
                post = POST[norm]
                if half:
                    act.wait_ge(unit_used, used)
                else:
                    act.wait_ge(half_done, post + 1)
                    act.wait_ge(y_summed, whole_tiles_before(post + 1) - post - 2 + (HALVED[post] == 2))
                last = range(KD - HALVED[post], KD)
                cols = half_cols(half, n_tok)
                for d in last:
                    act.activation(sq[:, d % 2, cols], ps[:, 2 * (d % 2) + half, 0:n_tok // 2], ACT.Square)\
                       .then_inc(half_squared, 1)
                for d in last:
                    act.activation(y[:, d, cols], ps[:, 2 * (d % 2) + half, 0:n_tok // 2], ACT.Copy,
                                   scale=vec[:, v0 + d:v0 + d + 1]).then_inc(y_evicted if half else act_step, 1)

            def half_root(norm, half, n_tok, half_step):
                root(norm + half, n_tok // BLOCKS, 4 + 2 * half, D_MODEL, rows=2, half_step=half_step)

            def to_next_stage(post, pre, base, n_tok, y, v_post, xh, v_pre, squares, half_step):
                half_result(0, y, v_post, post, base, n_tok)
                half_root(post, 0, n_tok, half_step)
                split_hi(base, 0, W_UP)
                for k in range(KD):
                    half_operand(pre, 0, k, n_tok, xh, v_pre)
                    if k == 2:
                        half_result(1, y, v_post, post, base, n_tok)
                    if k == 3:
                        split_hi(base, 1, W_UP)
                    if k == 4:
                        half_root(post, 1, n_tok, half_step)
                    if k >= 3:
                        half_square(0, k - 3, n_tok, squares)
                for k in range(KD - 3, KD):
                    half_square(0, k, n_tok, squares)
                for k in range(KD):
                    half_operand(pre, 1, k, n_tok, xh, v_pre)
                    half_square(1, k, n_tok, squares)

            def ffn_down(base, y, v0, norm, n_tok):
                preload_sqrt()
                for d in range(KD - 1):
                    split_hi(base, 2 * d + 2, W_DOWN)
                    split_hi(base, 2 * d + 3, W_DOWN)
                    result_tile(d, y, v0, norm, base + 2 * d + 2, n_tok)

            def gate_logs():
                act.wait_ge(z_done, 1)
                for t in range(2):
                    act.activation(row(z_log_t[:, t, :], L), in_psum(4 + 2 * t, L), ACT.Abs,
                                   bias=vec[:, V_BA + t:V_BA + t + 1]).then_inc(z_log, 1)

            def gate_logs_rest():
                act.wait_ge(z_log, 2)
                act.activation(z_log_t, z_log_t, ACT.Exp, scale=-1.0).then_inc(z_log, 1)
                act.wait_ge(z_log, 3)
                act.activation(z_log_t, z_log_t, ACT.Ln, bias=1.0).then_inc(z_log, 1)

            def chunk_decays():
                act.wait_ge(b_ready, 1)
                act.activation(q_in[:, :, :], b_real[:, :, :], ACT.Exp, scale=1 / GLA_TAU).then_inc(q_exp, 1)
                act.activation(dec[:, :, :], b_real[:, :, C - 1:SEQ:C], ACT.Exp, scale=1 / GLA_TAU).then_inc(q_exp, 1)
                act.wait_ge(k_diff, 1)
                act.activation(k_out[:, :, :], k_out[:, :, :], ACT.Exp, scale=1 / GLA_TAU).then_inc(k_exp, 1)

            def level_decays(lv):
                m = LEVELS[lv]
                act.wait_ge(lv_diff, lv + 1)
                d = decay[:, :, :].rearrange("p t (n x) -> p (t n) x", x=2 * m)
                act.activation(d[:, :, 0:m], d[:, :, 0:m], ACT.Exp, scale=-1 / GLA_TAU).then_inc(act_step, 1)
                act.activation(d[:, :, m:2 * m], d[:, :, m:2 * m], ACT.Exp, scale=1 / GLA_TAU).then_inc(lv_exp, 1)

            def take_turned():
                act.wait_ge(turned, 1)
                act.activation(vs_tok[:, 1:NC + 1, :], ps[:, 4, :].rearrange("p (b n) -> p b n", b=NC), ACT.Copy)\
                   .then_inc(act_step, 1)
                act.activation(vs_tok[0:N_META, 0, :], ps[0:N_META, 5, 0:P], ACT.Copy).then_inc(act_step, 1)
                act.activation(ktok[:, 1:NC, :], ps[:, 6:8, :].rearrange("p b (c n) -> p (b c) n", c=2)[:, 0:NC - 1, :],
                               ACT.Copy).then_inc(act_step, 1)
                act.activation(ktok[0:N_META, 0, :], ps[0:N_META, 7, 2 * P:4 * P], ACT.Copy).then_inc(turned_out, 1)

            def swa_out(p):
                pair, c, g = swa_pass(p)
                act.wait_ge(pv_done, p + 1)
                rows, cols = slice(64 * g, 64 * g + 64), slice(c * C, (c + 1) * C)
                src = ps[rows, 7, PAIR * C:2 * PAIR * C].rearrange("p (n t) -> p n t", n=PAIR)
                heads = slice(PAIR * pair, PAIR * pair + PAIR)
                act.activation(swa_sq[rows, heads, cols], src, ACT.Square).then_inc(act_step, 1)
                act.activation(o_swa[rows, heads, cols], src, ACT.Copy).then_inc(pv_evicted, 1)

            def swa_evict(p):
                act.wait_ge(p_turned, p + 1)
                src = ps[:, 6, :].rearrange("p (n b t) -> p n b t", n=PAIR, b=2)
                if swa_pass(p)[1]:
                    act.activation(p_t[:, :, :, :], src, ACT.Copy).then_inc(act_step, 1)
                else:
                    act.activation(p_t[:, :, 1, :], src[:, :, 1, :], ACT.Copy).then_inc(act_step, 1)
                act.activation(p_tm[:, :, :], ps[0:N_META, 7, 0:PAIR * C].rearrange("p (n t) -> p n t", n=PAIR),
                               ACT.Copy).then_inc(p_taken, 1)

            def swa_exp(p):
                act.wait_ge(s_max, p + 1)
                for n in range(PAIR):
                    act.activation(scores[:, p % 3, n, :], scores[:, p % 3, n, :], ACT.Exp,
                                   bias=small[:, p % 3, 0, n:n + 1], accum_out=small[:, p % 3, 1, n:n + 1])\
                       .then_inc(act_step, 1)
                act.activation(small[:, p % 3, 2, :], small[:, p % 3, 2, :], ACT.Exp).then_inc(s_exp, 1)

            def gap(g):
                j, p = g // 2, g - GAP_SWA
                if 0 <= p - 3:
                    swa_out(p - 3)
                if 0 <= p - 1 < PASSES:
                    swa_exp(p - 1)
                if g % 2 and j < N_IN:
                    split_hi(U_IN, j + 2, W_UP)
                if g == 2 * 2:
                    root(N_PREM, L // BLOCKS, 6, D_MODEL)
                if g == GAP_Z:
                    gate_logs()
                if g == GAP_Z + 1:
                    gate_logs_rest()
                if g == GAP_DECAY:
                    chunk_decays()
                    level_decays(0)
                if g == GAP_DECAY + 2:
                    level_decays(1)
                if 0 <= g - GAP_LV < len(LEVELS) - 2:
                    level_decays(g - GAP_LV + 2)
                if g == GAP_TURN:
                    take_turned()
                if 0 <= p - 2 < PASSES:
                    swa_evict(p - 2)

            act.wait_ge(carry_set, 1)
            preload_sqrt()
            act.wait_ge(vec_landed, 16)
            for k in range(KD):
                if k < 2:
                    split_hi(U_UP1, k, W_UP)
                act.wait_ge(x_landed[k], 16)
                operand_tile(k)
                if k >= 3:
                    square_tile(k - 3)
            for k in range(KD - 3, KD):
                square_tile(k)
            ffn_up(U_UP1, 0, hid1_hi, L, N_PRE1)
            ffn_down(U_DOWN1, y1, V_POST1, N_POST1, L)
            to_next_stage(N_POST1, N_PREM, U_IN, L, y1, V_POST1, xb_hi, V_PREM, squares1, True)

            split_hi(U_IN, 2, W_UP)
            split_hi(U_IN, 3, W_UP)
            for g in range(2 * 2, 2 * N_IN):
                gap(g)
            gap(2 * N_IN)
            act.wait_ge(proj_evicted, N_IN)
            act.activation(gg[:, 0:2, :], gg[:, 0:2, :], ACT.Silu).then_inc(gg_silu, 1)
            gap(2 * N_IN + 1)
            act.activation(gg[:, 2:4, :], gg[:, 2:4, :], ACT.Silu).then_inc(gg_silu, 1)
            for head in range(GLA_HEADS):
                if head == GLA_HEADS - 2:
                    gap(2 * N_IN + 2)
                act.wait_ge(og_done, head + 1)
                act.activation(gla_sq[:, head, :], ps[:, head, :], ACT.Square).then_inc(og_squared, 1)
            preload_sqrt()
            root(N_SWA, C, 6, SWA_HEADS * HEAD_DIM)
            for k in range(KD):
                if k == 2:
                    root(N_GLA, C, 7, GLA_DV, rows=GLA_HEADS * NC)
                act.wait_ge(cat_raw, k + 1)
                src = o_swa[:, k, :] if k < 4 else o_gla[:, k - 4, :]
                act.activation(cat_hi[:, k, :], src, ACT.Copy).then_inc(cat_hi_done, 1)
            for d in range(KD - 2):
                split_hi(U_OUT, d + 2, W_UP)
                result_tile(d, y2, V_POSTM, N_POSTM, U_OUT + d + 1, SEQ)
            to_next_stage(N_POSTM, N_PRE2, U_UP2, SEQ, y2, V_POSTM, xc_hi, V_PRE2, squares2, False)

            ffn_up(U_UP2, KF, hid2_hi, SEQ, N_PRE2)
            ffn_down(U_DOWN2, y3, V_POST2, N_POST2, SEQ)
            for half in range(2):
                half_result(half, y3, V_POST2, N_POST2, N_UNITS, SEQ)
                half_root(N_POST2, half, SEQ, True)

        @block.vector
        def _(dve):
            steps = [0]

            def link(ins):
                steps[0] += 1
                ins.then_inc(dve_step, 1)
                dve.wait_ge(dve_step, steps[0])

            def split_lo(base, j, width, i=0):
                u, raw_slot, _, slot = unit(base, j, i)
                dve.wait_ge(hi_split, u + 1)
                dve.tensor_tensor(w_lo[:, slot, 0:width], raw[:, raw_slot, 0:width], f32(w_hi[:, slot, 0:width]),
                                  ALU.subtract).then_inc(lo_split, 1)

            def reciprocal(norm, w, rows=BLOCKS):
                dve.wait_ge(rms_ready, norm + 1)
                dve.reciprocal(stat[0:rows, norm % 2, 0:w], stat[0:rows, norm % 2, 0:w]).then_inc(norm_ready, 1)

            def take_r(norm, n_tok, bank):
                dve.wait_ge(norm_spread, norm + 1)
                dve.tensor_copy(row(rnorm, n_tok), in_psum(bank, n_tok)).then_inc(r_ready, 1)
                dve.wait_ge(r_ready, norm_copies(norm))

            def low_part(k):
                dve.wait_ge(x_hi, k + 1)
                dve.scalar_tensor_tensor(out=xa_lo[:, k, :], in0=h[:, k, :], scalar=vec[:, V_PRE1 + k:V_PRE1 + k + 1],
                                         in1=f32(xa_hi[:, k, :]), op0=ALU.mult, op1=ALU.subtract).then_inc(x_ready, 1)

            def half_low_part(norm, half, k, n_tok, xh, xl, v0):
                dve.wait_ge(x_hi, KD * (BEFORE[norm] + half) + k + 1)
                cols = half_cols(half, n_tok)
                dve.scalar_tensor_tensor(out=xl[:, k, cols], in0=h[:, k, h_cols(half, n_tok)],
                                         scalar=vec[:, v0 + k:v0 + k + 1], in1=f32(xh[:, k, cols]),
                                         op0=ALU.mult, op1=ALU.subtract).then_inc(x_ready, 1)

            def half_take_r(norm, half, n_tok):
                dve.wait_ge(norm_spread, norm + half + 1)
                dve.tensor_copy(rnorm[:, half_cols(half, n_tok)], ps[:, 5 + 2 * half, 0:n_tok // 2]).then_inc(r_ready, 1)
                dve.wait_ge(r_ready, norm_copies(norm + half))

            def residual_tiles(y, half, n_tok, done, between, behind=0):
                cols = half_cols(half, n_tok)
                for k in range(KD + behind):
                    own = k < KD and k not in POOL_TILES
                    if own:
                        dve.tensor_tensor(y[:, k, cols], y[:, k, cols], rnorm[:, cols], ALU.mult).then_inc(dve_step, 1)
                        steps[0] += 1
                        scaled = steps[0]
                    between(k)
                    if own:
                        dve.wait_ge(dve_step, scaled)
                        to = h[:, k, h_cols(half, n_tok)]
                        dve.tensor_tensor(to, to, y[:, k, cols], ALU.add).then_inc(done, 1)

            def add_half_squares(norm, half, n_tok):
                post, cols = POST[norm], half_cols(half, n_tok)
                for n in range(HALVED[post]):
                    at = halves_before(post) + half * HALVED[post] + n
                    dve.wait_ge(half_squared, at + 1)
                    if n:
                        dve.wait_ge(half_summed, at)
                    elif half == 0:
                        dve.wait_ge(y_summed, whole_tiles_before(post + 1) - (post + 1))
                    dve.tensor_tensor(sumsq[:, cols], sumsq[:, cols], sq[:, (KD - HALVED[post] + n) % 2, cols], ALU.add)\
                       .then_inc(half_summed, 1)

            def to_next_stage(post, pre, base, n_tok, y, xh, xl, v_pre, squares):
                add_half_squares(post, 0, n_tok)
                reciprocal(post, n_tok // BLOCKS, rows=2)
                half_take_r(post, 0, n_tok)

                def first(k):
                    if k >= 2:
                        half_low_part(pre, 0, k - 2, n_tok, xh, xl, v_pre)
                    if k == 1:
                        split_lo(base, 0, W_UP)
                    if k == 4:
                        add_half_squares(post, 1, n_tok)
                    if k == 6:
                        reciprocal(post + 1, n_tok // BLOCKS, rows=2)

                def second(k):
                    if k >= 2:
                        half_low_part(pre, 1, k - 2, n_tok, xh, xl, v_pre)

                residual_tiles(y, 0, n_tok, h_updated, first, behind=2)
                half_take_r(post, 1, n_tok)
                residual_tiles(y, 1, n_tok, h_updated, second, behind=2)
                cols = half_cols(1, n_tok)
                for k in range(TAIL + 1, KD):
                    dve.wait_ge(squared, KD * (BEFORE[pre] + 1) + k + 1)
                    ins = dve.tensor_tensor(squares[:, TAIL, cols], squares[:, TAIL, cols], squares[:, k, cols], ALU.add)
                    if k < KD - 1:
                        link(ins)
                ins.then_inc(tail_summed, 1)

            def add_squares(norm, d, n_tok):
                if d:
                    post = POST[norm]
                    dve.wait_ge(y_squared, whole_tiles_before(post) + d + 1)
                    n = whole_tiles_before(post) - post + d
                    if d > 1:
                        dve.wait_ge(y_summed, n - 1)
                    dve.tensor_tensor(sumsq[:, 0:n_tok], sumsq[:, 0:n_tok], sq[:, d % 2, 0:n_tok], ALU.add)\
                       .then_inc(y_summed, 1)

            def hidden_tile(base, tile0, t, q, hi, lo, n_tok):
                dve.wait_ge(unit_used, base + 2 * t + 2)
                dve.tensor_tensor(row(gate, n_tok), in_psum(4 * q, n_tok), row(rnorm, n_tok), ALU.mult).then_inc(gate_scaled, 1)
                dve.tensor_tensor(row(up, n_tok), in_psum(4 * q + 2, n_tok), row(rnorm, n_tok), ALU.mult).then_inc(gu_evicted, 1)
                dve.wait_ge(gu_evicted, tile0 + t + 1)
                dve.wait_ge(silu_done, tile0 + t + 1)
                dve.tensor_tensor(up[:, 0:n_tok], up[:, 0:n_tok], gate[:, 0:n_tok], ALU.mult).then_inc(hid_written, 1)
                dve.wait_ge(hid_hi, tile0 + t + 1)
                dve.tensor_tensor(lo[:, t, :], up[:, 0:n_tok], f32(hi[:, t, :]), ALU.subtract).then_inc(hid_ready, 1)
                dve.wait_ge(hid_ready, tile0 + t + 1)

            def ffn_up(base, tile0, hi, lo, n_tok, norm):
                split_lo(base, 2, W_UP)
                if n_tok == L:
                    reciprocal(norm, n_tok // BLOCKS)
                    split_lo(base, 3, W_UP)
                    take_r(norm, n_tok, 6)
                    hidden_tile(base, tile0, 0, 0, hi, lo, n_tok)
                    split_lo(base, 4, W_UP)
                else:
                    split_lo(base, 3, W_UP)
                    reciprocal(norm, n_tok // BLOCKS)
                    split_lo(base, 4, W_UP)
                    take_r(norm, n_tok, 3)
                    hidden_tile(base, tile0, 0, 0, hi, lo, n_tok)
                split_lo(base, 5, W_UP)
                hidden_tile(base, tile0, 1, 1, hi, lo, n_tok)
                with dve.Fori(1, KF // 2 - 1) as i:
                    for n in range(2):
                        split_lo(base, 2 * n + 2, W_UP, i)
                        split_lo(base, 2 * n + 3, W_UP, i)
                        hidden_tile(base, tile0, 2 * i + n, n, hi, lo, n_tok)
                split_lo(base, UP_UNITS - 2, W_UP)
                split_lo(base, UP_UNITS - 1, W_UP)
                hidden_tile(base, tile0, KF - 2, 0, hi, lo, n_tok)
                split_lo(base, UP_UNITS, W_DOWN)
                split_lo(base, UP_UNITS + 1, W_DOWN)
                hidden_tile(base, tile0, KF - 1, 1, hi, lo, n_tok)

            def ffn_down(base, norm, n_tok):
                for d in range(KD - 1):
                    split_lo(base, 2 * d + 2, W_DOWN)
                    split_lo(base, 2 * d + 3, W_DOWN)
                    add_squares(norm, d, n_tok)

            def in_evict(j):
                dve.wait_ge(unit_used, U_IN + j + 1)
                src, dst = in_psum(in_bank(j), L), in_dst[j]
                if j == T_SK or T_SQ <= j < T_GV:
                    if j == T_SK:
                        dve.wait_ge(tables_scaled, 2)
                    link(dve.tensor_tensor(row(gate, L), src, row(sin_s, L), ALU.mult))
                    link(dve.stream_shuffle(up[:, :], gate[:, :], [(n + 16) % 32 for n in range(32)]))
                    link(dve.tensor_tensor(row(dst, L), src, row(cos_s, L), ALU.mult))
                    dve.tensor_tensor(dst, dst, up[:, :], ALU.add).then_inc(proj_evicted, 1)
                    dve.wait_ge(proj_evicted, j + 1)
                elif T_GQ <= j < T_GQ + 2:
                    dve.scalar_tensor_tensor(out=row(dst, L), in0=src, scalar=GLA_DK ** -0.5, in1=row(rnorm, L),
                                             op0=ALU.mult, op1=ALU.mult).then_inc(proj_evicted, 1)
                else:
                    dve.tensor_tensor(row(dst, L), src, row(rnorm, L), ALU.mult).then_inc(proj_evicted, 1)

            def z_minimum():
                dve.wait_ge(z_log, 2)
                for t in range(2):
                    dve.tensor_scalar(row(z_min[:, t, :], L), in_psum(4 + 2 * t, L), vec[:, V_BA + t:V_BA + t + 1], 0.0,
                                      ALU.add, ALU.min).then_inc(z_read, 1)
                dve.wait_ge(z_read, 2)

            def sum_log_a():
                dve.wait_ge(z_log, 4)
                link(dve.tensor_tensor(z_min, z_min, z_log_t, ALU.subtract))
                for t in range(2):
                    link(dve.tensor_tensor_scan(b_meta[:, t, :], carry[:, 1:1 + N_META], z_min[:, t, 0:N_META], 0.0,
                                                ALU.mult, ALU.add))
                    ins = dve.tensor_tensor_scan(b_real[:, t, :], carry[:, :], z_min[:, t, N_META:L], 0.0,
                                                 ALU.mult, ALU.add)
                    if t == 0:
                        link(ins)
                ins.then_inc(b_ready, 1)
                dve.wait_ge(b_ready, 1)

            def key_differences():
                for t in range(2):
                    bt = b_real[:, t, :].rearrange("p (c n) -> p c n", n=C)
                    link(dve.tensor_tensor(k_out[:, t, N_META:L].rearrange("p (c n) -> p c n", n=C),
                                           bt[:, :, C - 1:C].broadcast_to([P, NC, C]), bt, ALU.subtract))
                dve.tensor_tensor(k_out[:, :, 0:N_META], b_meta[:, :, N_META - 1:N_META].broadcast_to([P, 2, N_META]),
                                  b_meta[:, :, :], ALU.subtract).then_inc(k_diff, 1)

            def level_differences(lv):
                m = LEVELS[lv]
                if lv:
                    dve.wait_ge(lv_k_ready, lv)
                    dve.wait_ge(lv_q_ready, lv)
                d = decay[:, :, :].rearrange("p t (n x) -> p (t n) x", x=2 * m)
                b = b_real[:, :, :].rearrange("p t (n x) -> p (t n) x", x=2 * m)
                dve.tensor_tensor(d, b, b[:, :, m - 1:m].broadcast_to([P, SEQ // m, 2 * m]), ALU.subtract)\
                   .then_inc(lv_diff, 1)

            def level_queries(lv):
                m = LEVELS[lv]
                dve.wait_ge(lv_exp, lv + 1)
                if lv < 2:
                    dve.wait_ge(lv_zeroed, 2)
                else:
                    dve.wait_ge(lv_scored, lv - 1)
                half = [ap.rearrange("p t (n x) -> p t n x", x=2 * m)[:, :, :, m:2 * m]
                        for ap in (lv_q[:, lv % 2, :, :], gq, decay[:, :, :])]
                dve.tensor_tensor(half[0], half[1], half[2], ALU.mult).then_inc(lv_q_ready, 1)

            def level_take(lv):
                dve.wait_ge(lv_scored, lv + 1)
                if lv == 0:
                    dve.wait_ge(attn_zeroed, 1)
                m = LEVELS[lv] if lv < len(LEVELS) else 0
                size = 2 * m or C
                a, n = GLA_HEADS * NC, C // size
                bank = 4 + 2 * (lv % 2) if m else 4
                dst = attn[:, :].rearrange("p (a n x) -> p a n x", a=a, x=size)[:, :, :, m:size]
                src = ps[:, bank:bank + (2 if m else 4), :].rearrange("p h n -> p (h n)")\
                    .rearrange("p (a n x) -> p a n x", a=a, x=size - m)
                mask = lmask[:, lv:lv + 1, :].rearrange("p a (n x) -> p a n x", x=size)[:, :, :, m:size]
                dve.copy_predicated(dst, mask.broadcast_to([P, a, n, size - m]), src).then_inc(lv_taken, 1)
                dve.wait_ge(lv_taken, lv + 1)

            def swa_mask(p):
                pair, c, g = swa_pass(p)
                sc = scores[:, p % 3, :, :]
                neg_max = small[:, p % 3, 0, :]
                sink = vec[:, V_SINK + GROUP * g + PAIR * pair:V_SINK + GROUP * g + PAIR * pair + PAIR]
                dve.wait_ge(s_done, p + 1)
                if p >= 3:
                    dve.wait_ge(p_turned, p - 2)
                which = min(c, 1)
                dve.scalar_tensor_tensor(out=sc, in0=ps[:, 4:4 + PAIR, 0:SPAN], scalar=HEAD_DIM ** -0.5,
                                         in1=band_s[:, which:which + 1, :].broadcast_to([P, PAIR, SPAN]),
                                         op0=ALU.mult, op1=ALU.add).then_inc(s_masked, 1)
                dve.wait_ge(s_masked, p + 1)
                link(dve.tensor_reduce(neg_max, sc, AX_X, ALU.max))
                link(dve.tensor_tensor(neg_max, neg_max, sink, ALU.max))
                link(dve.tensor_scalar(neg_max, neg_max, -1.0, None, ALU.mult))
                dve.tensor_tensor(small[:, p % 3, 2, :], sink, neg_max, ALU.add).then_inc(s_max, 1)

            def take_gla_work(kind, n, b):
                if kind == "blocks":
                    dve.tensor_copy(vtok[:, 1 + b:3 + b, n * P:(n + 1) * P], ps[:, 4:6, FREE]).then_inc(v_taken, 1)
                elif kind == "meta":
                    dst = vtok[0:N_META, 0, n * P:(n + 2) * P].rearrange("p (n x) -> p n x", n=2)
                    dve.tensor_copy(dst, ps[0:N_META, 4:6, FREE]).then_inc(v_taken, 1)
                elif n == 0:
                    dve.wait_ge(turned, 1)
                    dve.tensor_copy(state[:, :, 0, :], ps[:, 4:6, FREE]).then_inc(v_taken, 1)
                else:
                    dve.wait_ge(v_taken, 10 + n)
                    for t in range(2):
                        ins = dve.scalar_tensor_tensor(out=state[:, t, n, :], in0=state[:, t, n - 1, :],
                                                       scalar=dec[:, t, n - 1:n], in1=ps[:, 4 + t, FREE],
                                                       op0=ALU.mult, op1=ALU.add)
                        if t == 0:
                            link(ins)
                    ins.then_inc(v_taken, 1)

            def swa_norm(p):
                rowsum, sink_exp = small[:, p % 3, 1, :], small[:, p % 3, 2, :]
                dve.wait_ge(s_exp, p + 1)
                link(dve.tensor_tensor(rowsum, rowsum, sink_exp, ALU.add))
                link(dve.reciprocal(rowsum, rowsum))
                for n in range(PAIR):
                    ins = dve.tensor_scalar(scores[:, p % 3, n, :], scores[:, p % 3, n, :], rowsum[:, n:n + 1], None, ALU.mult)
                    if n < PAIR - 1:
                        link(ins)
                ins.then_inc(s_normed, 1)

            def gap(g):
                j, p = g // 2, g - GAP_SWA
                if g == 2 * 2:
                    reciprocal(N_PREM, L // BLOCKS)
                    take_r(N_PREM, L, 6)
                    in_evict(0)
                    in_evict(1)
                if g % 2 and j < N_IN and g != GAP_LV:
                    in_evict(j)
                if 0 <= p - 1 < PASSES:
                    swa_norm(p - 1)
                late_split = g in (GAP_DECAY + 1, 2 * N_IN - 1)
                if g % 2 and j < N_IN and not late_split:
                    split_lo(U_IN, j + 2, W_UP)
                if g == GAP_Z:
                    z_minimum()
                if g == GAP_B:
                    sum_log_a()
                if g == GAP_DECAY:
                    key_differences()
                    level_differences(0)
                if g == GAP_DECAY + 1:
                    dve.wait_ge(proj_evicted, T_GQ + 2)
                    level_queries(0)
                    split_lo(U_IN, j + 2, W_UP)
                if g == GAP_DECAY + 2:
                    level_differences(1)
                    level_queries(1)
                if 0 <= g - GAP_LV <= len(LEVELS):
                    lv = g - GAP_LV
                    if lv + 2 < len(LEVELS):
                        level_differences(lv + 2)
                    level_take(lv)
                    if lv + 2 < len(LEVELS):
                        level_queries(lv + 2)
                if g == GAP_LV:
                    in_evict(j)
                if 0 <= p < PASSES:
                    swa_mask(p)
                if gla_step(g):
                    take_gla_work(*gla_step(g))
                if g == 2 * N_IN - 1:
                    split_lo(U_IN, j + 2, W_UP)

            link(dve.memset(carry[:, :], 1.0))
            dve.memset(carry[:, 0:SEQ:C], 0.0).then_inc(carry_set, 1)
            dve.wait_ge(carry_set, 1)
            dve.wait_ge(vec_landed, 16)
            for k in range(KD):
                if k < 2:
                    split_lo(U_UP1, k, W_UP)
                low_part(k)
            ffn_up(U_UP1, 0, hid1_hi, hid1_lo, L, N_PRE1)
            ffn_down(U_DOWN1, N_POST1, L)
            to_next_stage(N_POST1, N_PREM, U_IN, L, y1, xb_hi, xb_lo, V_PREM, squares1)

            split_lo(U_IN, 2, W_UP)
            split_lo(U_IN, 3, W_UP)
            for g in range(2 * 2, 2 * N_IN):
                gap(g)
            gap(2 * N_IN)

            dve.wait_ge(gg_silu, 2)
            link(dve.tensor_scalar(gg, gg, vec[:, V_GLA:V_GLA + 1], None, ALU.mult))
            for head in range(GLA_HEADS):
                dve.wait_ge(og_squared, head + 1)
                dve.tensor_tensor(o_gla[:, head, :], ps[:, head, :], gg[:, head, :], ALU.mult).then_inc(og_taken, 1)

            def cat_low(k):
                src = o_swa[:, k, :] if k < 4 else o_gla[:, k - 4, :]
                dve.wait_ge(cat_hi_done, k + 1)
                dve.tensor_tensor(cat_lo[:, k, :], src, f32(cat_hi[:, k, :]), ALU.subtract).then_inc(cat_ready, 1)

            reciprocal(N_SWA, C)
            dve.wait_ge(norm_spread, N_SWA + 1)
            for n in range(4):
                dve.scalar_tensor_tensor(out=o_swa[:, n, :], in0=o_swa[:, n, :], scalar=vec[:, V_SWA + n:V_SWA + n + 1],
                                         in1=ps[:, 6, :], op0=ALU.mult, op1=ALU.mult).then_inc(cat_raw, 1)
                if n:
                    cat_low(n - 1)
                if n == 1:
                    reciprocal(N_GLA, C, rows=GLA_HEADS * NC)
            cat_low(3)
            dve.wait_ge(norm_spread, N_GLA + 1)
            dve.wait_ge(og_taken, GLA_HEADS)
            for head in range(GLA_HEADS):
                dve.tensor_tensor(o_gla[:, head, :], o_gla[:, head, :], ps[:, 1 + 2 * head, :], ALU.mult).then_inc(cat_raw, 1)
                if head:
                    cat_low(4 + head - 1)
            cat_low(KD - 1)
            for d in range(KD - 2):
                split_lo(U_OUT, d + 2, W_UP)
                add_squares(N_POSTM, d, SEQ)
            to_next_stage(N_POSTM, N_PRE2, U_UP2, SEQ, y2, xc_hi, xc_lo, V_PRE2, squares2)

            ffn_up(U_UP2, KF, hid2_hi, hid2_lo, SEQ, N_PRE2)
            ffn_down(U_DOWN2, N_POST2, SEQ)
            own_tiles = [k for k in range(KD) if k not in POOL_TILES]
            for half in range(2):
                if half == 0:
                    add_half_squares(N_POST2, 0, SEQ)
                    reciprocal(N_POST2, C, rows=2)
                half_take_r(N_POST2, half, SEQ)
                cols = half_cols(half, SEQ)
                for n in range(len(own_tiles) + 1):
                    if n < len(own_tiles):
                        y = y3[:, own_tiles[n], cols]
                        dve.tensor_tensor(y, y, rnorm[:, cols], ALU.mult).then_inc(y3_scaled, 1)
                    if n:
                        dve.wait_ge(y3_scaled, len(own_tiles) * half + n)
                        k = own_tiles[n - 1]
                        to = h[:, k, h_cols(half, SEQ)]
                        dve.tensor_tensor(to, to, y3[:, k, cols], ALU.add).then_inc(out_dve, 1)
                    if (half, n) == (0, 3):
                        add_half_squares(N_POST2, 1, SEQ)
                    if (half, n) == (0, 5):
                        reciprocal(N_POST2 + 1, C, rows=2)

        @block.gpsimd
        def _(pool):
            def add_square(norm, cols, half, k, square):
                pool.wait_ge(squared, KD * (BEFORE[norm] + half) + k + 1)
                if k > 1:
                    pool.wait_ge(summed, sums_before(norm, half) + k - 1)
                so_far = square(0) if k == 1 else sumsq[:, cols]
                pool.tensor_tensor(sumsq[:, cols], so_far, square(k), ALU.add).then_inc(summed, 1)

            def half_residual(norm, half, y, n_tok, done):
                pool.wait_ge(r_ready, norm_copies(norm + half))
                cols, to = half_cols(half, n_tok), h_cols(half, n_tok)
                for n, k in enumerate(POOL_TILES):
                    pool.tensor_tensor(y[:, k, cols], y[:, k, cols], rnorm[:, cols], ALU.mult).then_inc(y_scaled, 1)
                    pool.wait_ge(y_scaled, len(POOL_TILES) * (2 * POST[norm] + half) + n + 1)
                    pool.tensor_tensor(h[:, k, to], h[:, k, to], y[:, k, cols], ALU.add).then_inc(done, 1)

            def to_next_stage(post, pre, base, n_tok, y, squares):
                def add(half, tiles):
                    cols = half_cols(half, n_tok)
                    pool.wait_ge(norm_summed, post + half + 1)
                    for k in tiles:
                        add_square(pre, cols, half, k, lambda n: squares[:, n, cols])

                half_residual(post, 0, y, n_tok, h_pool)
                u, raw_slot, _, slot = unit(base, 1)
                pool.wait_ge(hi_split, u + 1)
                pool.tensor_tensor(w_lo[:, slot, 0:W_UP], raw[:, raw_slot, 0:W_UP], f32(w_hi[:, slot, 0:W_UP]),
                                   ALU.subtract).then_inc(lo_split, 1)
                add(0, range(1, 4))
                half_residual(post, 1, y, n_tok, h_pool)
                add(0, range(4, KD))
                add(1, range(1, TAIL))
                pool.wait_ge(tail_summed, 1 + (pre == N_PRE2))
                add(1, [TAIL])

            def level_keys(lv):
                m = LEVELS[lv]
                pool.wait_ge(lv_exp, lv + 1)
                if lv < 2:
                    pool.wait_ge(lv_zeroed, 2)
                else:
                    pool.wait_ge(lv_scored, lv - 1)
                half = [ap.rearrange("p t (n x) -> p t n x", x=2 * m)[:, :, :, 0:m]
                        for ap in (lv_k[:, lv % 2, :, :], gk[:, :, N_META:L], decay[:, :, :])]
                pool.tensor_tensor(half[0], half[1], half[2], ALU.mult).then_inc(lv_k_ready, 1)

            for k in range(1, KD):
                add_square(N_PRE1, slice(0, L), 0, k, lambda n: sq[:, n % 2, :] if n else sumsq[:, :])
            to_next_stage(N_POST1, N_PREM, U_IN, L, y1, squares1)
            pool.memset(lv_k[:, :, :, :], 0.0).then_inc(lv_zeroed, 1)
            pool.memset(lv_q[:, :, :, :], 0.0).then_inc(lv_zeroed, 1)
            pool.memset(kx[:, 0, N_META:N_META + C], 0.0).then_inc(kx_ready, 1)
            pool.wait_ge(table_landed, 16 * 5)
            pool.wait_ge(r_ready, norm_copies(N_PREM))
            for table in (cos_s, sin_s):
                pool.tensor_tensor(table[:, :], table[:, :], rnorm[:, :], ALU.mult).then_inc(tables_scaled, 1)
            pool.wait_ge(b_ready, 1)
            pool.memset(attn[:, :], 0.0).then_inc(attn_zeroed, 1)
            level_keys(0)
            level_keys(1)
            level_keys(2)
            pool.wait_ge(proj_evicted, T_SK + 1)
            pool.wait_ge(kx_ready, 1)
            for c in range(NC):
                pool.tensor_copy(kx[:, c, 0:N_META], sk[:, 0:N_META]).then_inc(kx_ready, 1)
                before, col = (c - 1, N_META) if c else (0, N_META + C)
                pool.tensor_copy(kx[:, c, col:SPAN], sk[:, N_META + before * C:N_META + (c + 1) * C]).then_inc(kx_ready, 1)
                if c == 1:
                    level_keys(3)
            pool.wait_ge(k_exp, 1)
            pool.tensor_tensor(k_out[:, :, :], k_out[:, :, :], gk, ALU.mult).then_inc(k_out_ready, 1)
            level_keys(4)
            pool.wait_ge(q_exp, 2)
            pool.wait_ge(proj_evicted, T_GQ + 2)
            pool.tensor_tensor(q_in[:, :, :], q_in[:, :, :], gq, ALU.mult).then_inc(q_in_ready, 1)
            for lv in range(5, len(LEVELS)):
                level_keys(lv)
            pool.wait_ge(pv_evicted, PASSES // 2)
            pool.tensor_tensor(swa_sq[:, 0, :], swa_sq[:, 0, :], swa_sq[:, 1, :], ALU.add).then_inc(swa_summed, 1)
            for c in range(NC):
                pool.wait_ge(pv_evicted, PASSES // 2 + KV_HEADS * (c + 1))
                cols = slice(c * C, (c + 1) * C)
                for n in (2, 3):
                    pool.wait_ge(swa_summed, 2 * c + n - 1)
                    pool.tensor_tensor(swa_sq[:, 0, cols], swa_sq[:, 0, cols], swa_sq[:, n, cols], ALU.add)\
                        .then_inc(swa_summed, 1)
            to_next_stage(N_POSTM, N_PRE2, U_UP2, SEQ, y2, squares2)
            for half in range(2):
                half_residual(N_POST2, half, y3, SEQ, out_pool)


def rope_tables():
    half = HEAD_DIM // 2
    inv_freq = (1.0 / (np.float32(ROPE_THETA) ** (np.arange(0, HEAD_DIM, 2, dtype=np.float32) / np.float32(HEAD_DIM))))
    ang = inv_freq.astype(np.float32)[:, None] * np.arange(L, dtype=np.float32)[None, :]
    cos, sin = np.cos(ang), np.sin(ang)
    quarters = half // 2
    cos = np.concatenate([cos[:quarters]] * 2 + [cos[quarters:]] * 2)
    sin = np.concatenate([sin[:quarters], -sin[:quarters], sin[quarters:], -sin[quarters:]])
    return np.concatenate([cos] * 2).astype(np.float32), np.concatenate([sin] * 2).astype(np.float32)


def masks():
    t, s = np.arange(C)[:, None], np.arange(C)[None, :]
    meta = np.zeros((C, N_META), np.float32)
    own = np.where(s <= t, 0.0, NEG).astype(np.float32)
    before = np.where(s > t, 0.0, NEG).astype(np.float32)
    none = np.full((C, C), NEG, np.float32)
    band = np.stack([np.concatenate([meta, none, own], 1), np.concatenate([meta, before, own], 1)], 1)
    j, i = t, s
    levels = [(j // (2 * m) == i // (2 * m)) & (j % (2 * m) < m) & (i % (2 * m) >= m) for m in LEVELS]
    levels.append(j == i)
    return band, np.stack(levels, 1).astype(np.uint32)


def kernel(**inputs):
    import concourse.bacc as bacc
    from concourse.bass_utils import run_bass_kernel_spmd

    a = {name: np.asarray(value) for name, value in inputs.items()}

    def tiles(w, k_tiles):
        return w.reshape(k_tiles, P, w.shape[1] // P, P).transpose(2, 1, 0, 3)

    def up_units(gate, up):
        both = np.stack([tiles(gate, KD), tiles(up, KD)], 1)
        return np.ascontiguousarray(both.reshape(UP_UNITS, P, W_UP))

    def down_units(w):
        t = tiles(w, KF).reshape(KD, P, 2, KH, P).transpose(0, 2, 1, 3, 4)
        return np.ascontiguousarray(t.reshape(DOWN_UNITS, P, W_DOWN))

    def columns(v):
        return v.reshape(-1, P).T

    def heads_side_by_side(w, axis):
        shape = w.shape
        w = np.moveaxis(w, axis, 0).reshape(KV_HEADS, GROUP, HEAD_DIM, -1).transpose(1, 0, 2, 3)
        return np.moveaxis(w.reshape((SWA_HEADS * HEAD_DIM,) + tuple(np.delete(shape, axis))), 0, axis)

    def halves_exchangeable(w):
        w = w.reshape(D_MODEL, -1, 2, 2, HEAD_DIM // 4).transpose(0, 1, 3, 2, 4)
        return w.reshape(D_MODEL, -1)

    w_in = a["w_in"][0]
    at = np.cumsum([0, 256, 256, 512, 512, GATE_RANK, 512, 128, 128])
    q, k, v, g, ga, sq, sk, sv = (w_in[:, at[n]:at[n + 1]] for n in range(8))
    ga = np.concatenate([ga, np.zeros((D_MODEL, P - GATE_RANK), w_in.dtype)], 1)
    w_in = np.concatenate([ga, k, q, sv, halves_exchangeable(sk), halves_exchangeable(heads_side_by_side(sq, 1)), v, g], 1)
    w_out = a["w_out"][0]
    w_out = np.concatenate([heads_side_by_side(w_out[512:], 0), w_out[:512]], 0)
    vecs = np.concatenate(
        [columns(a[n][0]) for n in ("ffn1_pre_norm", "ffn1_post_norm", "mix_pre_norm", "mix_post_norm",
                                    "ffn2_pre_norm", "ffn2_post_norm")]
        + [columns(heads_side_by_side(a["swa_out_norm"][0], 0)), columns(a["gla_out_norm"][0]),
           columns(a["gla_b_a"][0]), np.broadcast_to(a["swa_sinks"][0], (P, SWA_HEADS)),
           np.broadcast_to(np.array([EPS, 4 * EPS], np.float32), (P, 2))], 1)
    x_t = np.concatenate([a["meta_tokens"], a["x"][0]], 0).T.reshape(KD, P, L).transpose(1, 0, 2)
    cos_t, sin_t = rope_tables()
    band, level_mask = masks()
    arrays = {
        "x_t": x_t, "vecs": vecs,
        "up1": up_units(a["ffn1_w_gate"][0], a["ffn1_w_up"][0]), "down1": down_units(a["ffn1_w_down"][0]),
        "w_in": tiles(w_in, KD).reshape(N_IN, P, W_UP), "w_a2": a["gla_w_a2"][0],
        "w_out": tiles(w_out, KD).reshape(KD, P, W_UP),
        "up2": up_units(a["ffn2_w_gate"][0], a["ffn2_w_up"][0]), "down2": down_units(a["ffn2_w_down"][0]),
        "cos_t": cos_t, "sin_t": sin_t,
        "ident": np.eye(P, dtype=np.float32), "select": np.broadcast_to((np.arange(31) == 15).astype(np.float32), (P, 31)),
        "band": band, "level_mask": level_mask,
    }
    arrays = {f"in_{name}": np.ascontiguousarray(value) for name, value in arrays.items()}
    nc = bacc.Bacc("TRN2", target_bir_lowering=False, num_devices=1)
    aps = [nc.dram_tensor(name, v.shape, mybir.dt.from_np(v.dtype), kind="ExternalInput").ap()
           for name, v in arrays.items()]
    out = nc.dram_tensor("out", (P, KD, SEQ), F32, kind="ExternalOutput").ap()
    hybrid_layer(nc, *aps, out)
    r = run_bass_kernel_spmd(nc, [arrays], core_ids=[0])
    y = np.asarray(r.results[0]["out"])
    return np.ascontiguousarray(y.transpose(1, 0, 2).reshape(D_MODEL, SEQ).T)[None]
```
